# Optimizing a Trainium2 kernel written in Bass

```python
import math
import jax
import jax.numpy as jnp
from jax import lax
import numpy as np
import jax, jax.numpy as jnp

D_MODEL = 1024
BATCH = 1
SEQ = 256
DEPTH = 2

HEAD_DIM = 64
BRANCH_WIDTH = 512
N_BRANCH = 4
SSM_HEADS = 8
SSM_HEAD_DIM = 64
SSM_INNER = SSM_HEADS * SSM_HEAD_DIM
SSM_GROUPS = 2
SSM_STATE = 128
SSM_CONV = 4
SSM_CHUNK = 256
SSM_CONV_CH = SSM_INNER + 2 * SSM_GROUPS * SSM_STATE
FOX_HEADS = 8
MOBA_HEADS = 8
MOBA_BLOCK = 256
MOBA_TOPK = 3
MOBA_Q_BLOCK = 64
DSA_HEADS = 8
IDX_HEADS = 4
IDX_DIM = 64
DSA_TOPK = 256
Q_BLOCK = 128
ROPE_THETA = 10000.0
FFN_HIDDEN = -(-8 * D_MODEL // (3 * 256)) * 256
EPS = 1e-6

IN_SPLITS = (
    SSM_INNER, SSM_INNER, SSM_GROUPS * SSM_STATE, SSM_GROUPS * SSM_STATE, SSM_HEADS,
    FOX_HEADS * HEAD_DIM, FOX_HEADS * HEAD_DIM, FOX_HEADS * HEAD_DIM, FOX_HEADS,
    MOBA_HEADS * HEAD_DIM, MOBA_HEADS * HEAD_DIM, MOBA_HEADS * HEAD_DIM,
    DSA_HEADS * HEAD_DIM, DSA_HEADS * HEAD_DIM, DSA_HEADS * HEAD_DIM,
    IDX_HEADS * IDX_DIM, IDX_DIM, IDX_HEADS,
)
D_IN = sum(IN_SPLITS)


def rms_norm(x, g):
    x32 = x.astype(jnp.float32)
    y = x32 * lax.rsqrt(jnp.mean(x32 * x32, axis=-1, keepdims=True) + EPS)
    return (y * g.astype(jnp.float32)).astype(x.dtype)

def rope_tables(seq):
    pos = jnp.arange(seq, dtype=jnp.float32)
    inv = ROPE_THETA ** (-jnp.arange(0, HEAD_DIM, 2, dtype=jnp.float32) / HEAD_DIM)
    ang = pos[:, None] * inv[None, :]
    return jnp.cos(ang), jnp.sin(ang)

def apply_rope(t, cos, sin):
    t1, t2 = jnp.split(t.astype(jnp.float32), 2, axis=-1)
    c = cos[None, :, None, :]
    s = sin[None, :, None, :]
    return jnp.concatenate([t1 * c - t2 * s, t2 * c + t1 * s], axis=-1).astype(t.dtype)

def split_heads(t, n_heads):
    return t.reshape(t.shape[0], t.shape[1], n_heads, -1)

def causal_dwconv(u, w, b):
    width = w.shape[0]
    up = jnp.pad(u, ((0, 0), (width - 1, 0), (0, 0)))
    y = lax.conv_general_dilated(up, w[:, None, :], window_strides=(1,), padding='VALID',
                                 dimension_numbers=('NWC', 'WIO', 'NWC'),
                                 feature_group_count=u.shape[-1])
    return y + b

def ssd_chunked(x, dt, a, bmat, cmat):
    bsz, seq, n_heads, hp = x.shape
    pad = (-seq) % SSM_CHUNK
    padl = lambda t: jnp.pad(t, ((0, 0), (0, pad)) + ((0, 0),) * (t.ndim - 2))
    n_chunk = (seq + pad) // SSM_CHUNK
    chunk = lambda t: padl(t).reshape((bsz, n_chunk, SSM_CHUNK) + t.shape[2:])
    xc, dtc, bc, cc = chunk(x), chunk(dt), chunk(bmat), chunk(cmat)
    a_cs = jnp.cumsum((dtc * a).transpose(0, 3, 1, 2), axis=-1)
    xdt = xc * dtc[..., None]
    causal = jnp.tril(jnp.ones((SSM_CHUNK, SSM_CHUNK), dtype=bool))
    seg = a_cs[..., :, None] - a_cs[..., None, :]
    decay = jnp.exp(jnp.where(causal, seg, -jnp.inf))
    scores = jnp.einsum('bclhn,bcshn->bhcls', cc, bc) * decay
    y_diag = jnp.einsum('bhcls,bcshp->bclhp', scores, xdt)
    decay_states = jnp.exp(a_cs[..., -1:] - a_cs)
    states = jnp.einsum('bclhn,bhcl,bclhp->bchpn', bc, decay_states, xdt)
    chunk_decay = jnp.exp(a_cs[..., -1])

    def step(h, inp):
        s_c, d_c = inp
        return h * d_c[..., None, None] + s_c, h

    h0 = jnp.zeros((bsz, n_heads, hp, bmat.shape[-1]), jnp.float32)
    _, prev = lax.scan(step, h0, (states.transpose(1, 0, 2, 3, 4), chunk_decay.transpose(2, 0, 1)))
    prev = prev.transpose(1, 0, 2, 3, 4)
    y_off = jnp.einsum('bclhn,bchpn,bhcl->bclhp', cc, prev, jnp.exp(a_cs))
    y = (y_diag + y_off).reshape(bsz, n_chunk * SSM_CHUNK, n_heads, hp)
    return y[:, :seq]

def mamba2_branch(z, xs, bs, cs, dt_raw, conv_w, conv_b, dt_bias, a_log, d_skip, norm_w):
    bsz, seq, _ = z.shape
    xbc = jax.nn.silu(causal_dwconv(jnp.concatenate([xs, bs, cs], axis=-1), conv_w, conv_b))
    xs, bs, cs = jnp.split(xbc, [SSM_INNER, SSM_INNER + SSM_GROUPS * SSM_STATE], axis=-1)
    rep = SSM_HEADS // SSM_GROUPS
    xh = xs.reshape(bsz, seq, SSM_HEADS, SSM_HEAD_DIM).astype(jnp.float32)
    bh = jnp.repeat(bs.reshape(bsz, seq, SSM_GROUPS, SSM_STATE), rep, axis=2).astype(jnp.float32)
    ch = jnp.repeat(cs.reshape(bsz, seq, SSM_GROUPS, SSM_STATE), rep, axis=2).astype(jnp.float32)
    dt = jax.nn.softplus(dt_raw.astype(jnp.float32) + dt_bias.astype(jnp.float32))
    a = -jnp.exp(a_log.astype(jnp.float32))
    y = ssd_chunked(xh, dt, a, bh, ch) + d_skip.astype(jnp.float32)[:, None] * xh
    y = y.reshape(bsz, seq, SSM_INNER) * jax.nn.silu(z.astype(jnp.float32))
    yg = y.reshape(bsz, seq, SSM_GROUPS, -1)
    yg = yg * lax.rsqrt(jnp.mean(yg * yg, axis=-1, keepdims=True) + EPS)
    return (yg.reshape(bsz, seq, SSM_INNER) * norm_w.astype(jnp.float32)).astype(z.dtype)

def fox_branch(q, k, v, f_logit, f_bias):
    bsz, seq, n_heads, hd = q.shape
    log_f = jax.nn.log_sigmoid(f_logit.astype(jnp.float32) + f_bias.astype(jnp.float32))
    cf = jnp.cumsum(log_f, axis=1).transpose(0, 2, 1)
    kpos = jnp.arange(seq)
    scale = hd ** -0.5

    def block(i):
        start = i * Q_BLOCK
        qb = lax.dynamic_slice_in_dim(q, start, Q_BLOCK, axis=1)
        cq = lax.dynamic_slice_in_dim(cf, start, Q_BLOCK, axis=2)
        qpos = start + jnp.arange(Q_BLOCK)
        logits = jnp.einsum('bqhd,bkhd->bhqk', qb, k).astype(jnp.float32) * scale
        logits = logits + cq[..., :, None] - cf[..., None, :]
        logits = jnp.where(kpos[None, :] <= qpos[:, None], logits, -jnp.inf)
        p = jax.nn.softmax(logits, axis=-1).astype(v.dtype)
        return jnp.einsum('bhqk,bkhd->bqhd', p, v)

    out = lax.map(block, jnp.arange(seq // Q_BLOCK))
    return out.transpose(1, 0, 2, 3, 4).reshape(bsz, seq, n_heads * hd)

def moba_branch(q, k, v):
    bsz, seq, n_heads, hd = q.shape
    n_blk = -(-seq // MOBA_BLOCK)
    pad = n_blk * MOBA_BLOCK - seq
    to_blocks = lambda t: jnp.pad(t, ((0, 0), (0, pad), (0, 0), (0, 0))).reshape(
        bsz, n_blk, MOBA_BLOCK, n_heads, hd).transpose(0, 3, 1, 2, 4)
    k_blk, v_blk = to_blocks(k), to_blocks(v)
    k_mean = jnp.mean(k_blk.astype(jnp.float32), axis=3)
    n_sel = min(MOBA_TOPK, n_blk)
    n_sel_keys = n_sel * MOBA_BLOCK
    scale = hd ** -0.5
    b_ix = jnp.arange(bsz)[:, None, None, None]
    h_ix = jnp.arange(n_heads)[None, None, :, None]
    blk_ids = jnp.arange(n_blk)

    def block(i):
        start = i * MOBA_Q_BLOCK
        qb = lax.dynamic_slice_in_dim(q, start, MOBA_Q_BLOCK, axis=1)
        qpos = start + jnp.arange(MOBA_Q_BLOCK)
        cur = start // MOBA_BLOCK
        gate = jnp.einsum('bqhd,bhnd->bqhn', qb.astype(jnp.float32), k_mean)
        gate = jnp.where(blk_ids < cur, gate, -jnp.inf)
        _, sel = lax.top_k(gate, n_sel)
        sel_ok = sel < cur
        k_sel = k_blk[b_ix, h_ix, sel]
        v_sel = v_blk[b_ix, h_ix, sel]
        s_sel = jnp.einsum('bqhd,bqhnkd->bqhnk', qb, k_sel).astype(jnp.float32) * scale
        s_sel = jnp.where(sel_ok[..., None], s_sel, -jnp.inf)
        k_own = lax.dynamic_index_in_dim(k_blk, cur, axis=2, keepdims=False)
        v_own = lax.dynamic_index_in_dim(v_blk, cur, axis=2, keepdims=False)
        own_pos = cur * MOBA_BLOCK + jnp.arange(MOBA_BLOCK)
        s_own = jnp.einsum('bqhd,bhkd->bqhk', qb, k_own).astype(jnp.float32) * scale
        s_own = jnp.where(own_pos[None, None, None, :] <= qpos[None, :, None, None], s_own, -jnp.inf)
        logits = jnp.concatenate([s_sel.reshape(bsz, MOBA_Q_BLOCK, n_heads, n_sel_keys), s_own], axis=-1)
        p = jax.nn.softmax(logits, axis=-1).astype(v.dtype)
        p_sel = p[..., :n_sel_keys].reshape(bsz, MOBA_Q_BLOCK, n_heads, n_sel, MOBA_BLOCK)
        p_own = p[..., n_sel_keys:]
        return (jnp.einsum('bqhnk,bqhnkd->bqhd', p_sel, v_sel)
                + jnp.einsum('bqhk,bhkd->bqhd', p_own, v_own))

    out = lax.map(block, jnp.arange(seq // MOBA_Q_BLOCK))
    return out.transpose(1, 0, 2, 3, 4).reshape(bsz, seq, n_heads * hd)

def dsa_branch(q, k, v, qi, ki, wi):
    bsz, seq, n_heads, hd = q.shape
    n_keep = min(DSA_TOPK, seq // 4)
    kpos = jnp.arange(seq)
    scale = hd ** -0.5
    idx_scale = IDX_DIM ** -0.5
    w_scale = IDX_HEADS ** -0.5
    b_ix = jnp.arange(bsz)[:, None, None]

    def block(i):
        start = i * Q_BLOCK
        qb = lax.dynamic_slice_in_dim(q, start, Q_BLOCK, axis=1)
        qib = lax.dynamic_slice_in_dim(qi, start, Q_BLOCK, axis=1)
        wib = lax.dynamic_slice_in_dim(wi, start, Q_BLOCK, axis=1)
        qpos = start + jnp.arange(Q_BLOCK)
        isc = jax.nn.relu(jnp.einsum('bqhd,bkd->bqhk', qib, ki).astype(jnp.float32) * idx_scale)
        isc = jnp.einsum('bqh,bqhk->bqk', wib.astype(jnp.float32) * w_scale, isc)
        isc = jnp.where(kpos[None, None, :] <= qpos[None, :, None], isc, -jnp.inf)
        _, sel = lax.top_k(isc, n_keep)
        ok = sel <= qpos[None, :, None]
        k_sel = k[b_ix, sel]
        v_sel = v[b_ix, sel]
        logits = jnp.einsum('bqhd,bqkhd->bqhk', qb, k_sel).astype(jnp.float32) * scale
        logits = jnp.where(ok[:, :, None, :], logits, -jnp.inf)
        p = jax.nn.softmax(logits, axis=-1).astype(v.dtype)
        return jnp.einsum('bqhk,bqkhd->bqhd', p, v_sel)

    out = lax.map(block, jnp.arange(seq // Q_BLOCK))
    return out.transpose(1, 0, 2, 3, 4).reshape(bsz, seq, n_heads * hd)

def hybrid_mixer(h, w_in, conv_w, conv_b, dt_bias, a_log, d_skip, ssm_norm, fox_fbias,
                 w_gate, b_gate, w_branch, w_out, cos, sin):
    bsz, seq, _ = h.shape
    u = h @ w_in
    (z, xs, bs, cs, dt_raw, fq, fk, fv, ff, mq, mk, mv, dq, dk, dv, iq, ik, iw) = jnp.split(
        u, np.cumsum(IN_SPLITS)[:-1].tolist(), axis=-1)
    y_ssm = mamba2_branch(z, xs, bs, cs, dt_raw, conv_w, conv_b, dt_bias, a_log, d_skip, ssm_norm)
    y_fox = fox_branch(split_heads(fq, FOX_HEADS), split_heads(fk, FOX_HEADS),
                       split_heads(fv, FOX_HEADS), ff, fox_fbias)
    y_moba = moba_branch(apply_rope(split_heads(mq, MOBA_HEADS), cos, sin),
                         apply_rope(split_heads(mk, MOBA_HEADS), cos, sin),
                         split_heads(mv, MOBA_HEADS))
    y_dsa = dsa_branch(apply_rope(split_heads(dq, DSA_HEADS), cos, sin),
                       apply_rope(split_heads(dk, DSA_HEADS), cos, sin),
                       split_heads(dv, DSA_HEADS),
                       apply_rope(split_heads(iq, IDX_HEADS), cos, sin),
                       apply_rope(ik[:, :, None, :], cos, sin)[:, :, 0, :],
                       iw)
    ys = jnp.stack([y_ssm, y_fox, y_moba, y_dsa], axis=2)
    proj = jnp.einsum('bsnc,ncd->bsnd', ys, w_branch)
    gates = jax.nn.sigmoid(h @ w_gate + b_gate).reshape(bsz, seq, N_BRANCH, D_MODEL)
    merged = jnp.sum(gates * proj, axis=2)
    return merged @ w_out

def swiglu(h, w_in, w_out):
    g, up = jnp.split(h @ w_in, 2, axis=-1)
    return (jax.nn.silu(g) * up) @ w_out

def first_inputs(seed: int = 0) -> dict:
    key = jax.random.key(seed)
    ks = jax.random.split(key, 19)
    f32 = jnp.float32
    nrm = lambda k, shape, scale: jax.random.normal(k, shape, f32) * scale
    gain = lambda k, shape: 1.0 + 0.05 * jax.random.normal(k, shape, f32)
    dt0 = jnp.exp(jax.random.uniform(ks[5], (DEPTH, SSM_HEADS), f32, math.log(1e-3), math.log(1e-1)))
    return {
        'x': nrm(ks[0], (BATCH, SEQ, D_MODEL), 1.0),
        'norm_mix_pre': gain(ks[1], (DEPTH, D_MODEL)),
        'w_in': nrm(ks[2], (DEPTH, D_MODEL, D_IN), D_MODEL ** -0.5),
        'conv_w': nrm(ks[3], (DEPTH, SSM_CONV, SSM_CONV_CH), SSM_CONV ** -0.5),
        'conv_b': nrm(ks[4], (DEPTH, SSM_CONV_CH), 0.02),
        'dt_bias': dt0 + jnp.log(-jnp.expm1(-dt0)),
        'a_log': jnp.log(jax.random.uniform(ks[6], (DEPTH, SSM_HEADS), f32, 1.0, 16.0)),
        'd_skip': 1.0 + 0.1 * jax.random.normal(ks[7], (DEPTH, SSM_HEADS), f32),
        'ssm_norm': gain(ks[8], (DEPTH, SSM_INNER)),
        'fox_fbias': 3.0 + 0.5 * jax.random.normal(ks[9], (DEPTH, FOX_HEADS), f32),
        'w_gate': nrm(ks[10], (DEPTH, D_MODEL, N_BRANCH * D_MODEL), D_MODEL ** -0.5),
        'b_gate': nrm(ks[11], (DEPTH, N_BRANCH * D_MODEL), 0.02),
        'w_branch': nrm(ks[12], (DEPTH, N_BRANCH, BRANCH_WIDTH, D_MODEL), BRANCH_WIDTH ** -0.5),
        'w_out': nrm(ks[13], (DEPTH, D_MODEL, D_MODEL), D_MODEL ** -0.5),
        'norm_mix_post': gain(ks[14], (DEPTH, D_MODEL)),
        'norm_ffn_pre': gain(ks[15], (DEPTH, D_MODEL)),
        'w_ffn_in': nrm(ks[16], (DEPTH, D_MODEL, 2 * FFN_HIDDEN), D_MODEL ** -0.5),
        'w_ffn_out': nrm(ks[17], (DEPTH, FFN_HIDDEN, D_MODEL), FFN_HIDDEN ** -0.5),
        'norm_ffn_post': gain(ks[18], (DEPTH, D_MODEL)),
    }

def first_block(x, norm_mix_pre, w_in, conv_w, conv_b, dt_bias, a_log, d_skip, ssm_norm, fox_fbias,
              w_gate, b_gate, w_branch, w_out, norm_mix_post, norm_ffn_pre, w_ffn_in, w_ffn_out,
              norm_ffn_post):
    cos, sin = rope_tables(x.shape[1])
    for l in range(DEPTH):
        h = rms_norm(x, norm_mix_pre[l])
        mix = hybrid_mixer(h, w_in[l], conv_w[l], conv_b[l], dt_bias[l], a_log[l], d_skip[l],
                           ssm_norm[l], fox_fbias[l], w_gate[l], b_gate[l], w_branch[l], w_out[l],
                           cos, sin)
        x = x + rms_norm(mix, norm_mix_post[l])
        h = rms_norm(x, norm_ffn_pre[l])
        x = x + rms_norm(swiglu(h, w_ffn_in[l], w_ffn_out[l]), norm_ffn_post[l])
    return x


MEM_LEN = 256
NORM_EPS = 1e-6
BRANCH_WIDTH_2 = 256

MLA_HEADS = 4
MLA_Q_RANK = 256
MLA_KV_RANK = 128
MLA_NOPE = 64
MLA_ROPE = 32
MLA_V = 64
ATTN_BLOCK = 128

SG_GROUPS = 4
SG_WIDTH = 256
SG_CHUNK = 128

GLA_HEADS = 4
GLA_DK = 32
GLA_DV = 64
GLA_GATE_RANK = 16
GLA_GATE_TEMP = 16.0
GLA_CHUNK = 64

DN_HEADS = 4
DN_DK = 64
DN_DV = 64
DN_CONV = 4
DN_CHUNK = 64

XATTN_HEADS = 4
XATTN_DIM = D_MODEL // XATTN_HEADS
MLP_HIDDEN = 4 * D_MODEL

IN_SIZES = (
    MLA_Q_RANK, MLA_KV_RANK, MLA_ROPE,
    2 * SG_WIDTH,
    GLA_HEADS * GLA_DK, GLA_HEADS * GLA_DK, GLA_HEADS * GLA_DV,
    GLA_GATE_RANK, GLA_HEADS * GLA_DV,
    DN_HEADS * DN_DK, DN_HEADS * DN_DK, DN_HEADS * DN_DV,
    DN_HEADS, DN_HEADS, DN_HEADS * DN_DV,
    N_BRANCH * D_MODEL,
)
IN_WIDTH = sum(IN_SIZES)


def rmsnorm(x, g, eps=NORM_EPS):
    xf = x.astype(jnp.float32)
    y = xf * lax.rsqrt(jnp.mean(xf * xf, axis=-1, keepdims=True) + eps)
    return (y * g).astype(x.dtype)

def layernorm(x, g, b, eps=NORM_EPS):
    xf = x.astype(jnp.float32)
    mu = jnp.mean(xf, axis=-1, keepdims=True)
    xc = xf - mu
    y = xc * lax.rsqrt(jnp.mean(xc * xc, axis=-1, keepdims=True) + eps)
    return (y * g + b).astype(x.dtype)

def l2norm(x, eps=NORM_EPS):
    return x * lax.rsqrt(jnp.sum(x * x, axis=-1, keepdims=True) + eps)

def rope_angles(positions, dim):
    inv_freq = ROPE_THETA ** (-jnp.arange(0, dim, 2, dtype=jnp.float32) / dim)
    ang = positions.astype(jnp.float32)[..., None] * inv_freq
    return jnp.cos(ang), jnp.sin(ang)

def apply_rope_2(x, cos, sin):
    half = x.shape[-1] // 2
    x1 = x[..., :half].astype(jnp.float32)
    x2 = x[..., half:].astype(jnp.float32)
    return jnp.concatenate([x1 * cos - x2 * sin, x2 * cos + x1 * sin], axis=-1).astype(x.dtype)

def to_chunks(t, chunk):
    b, s, h = t.shape[:3]
    t = t.reshape((b, s // chunk, chunk, h) + t.shape[3:])
    return t.transpose((1, 0, 3, 2) + tuple(range(4, t.ndim)))

def from_chunks(t):
    n, b, h, c = t.shape[:4]
    t = t.transpose((1, 0, 3, 2) + tuple(range(4, t.ndim)))
    return t.reshape((b, n * c, h) + t.shape[4:])

def causal_block_attention(q, k, v, scale):
    s_len = q.shape[2]
    outs = []
    for start in range(0, s_len, ATTN_BLOCK):
        end = start + ATTN_BLOCK
        s = jnp.einsum('bhqd,bhkd->bhqk', q[:, :, start:end], k[:, :, :end]).astype(jnp.float32) * scale
        qi = start + jnp.arange(ATTN_BLOCK)
        ki = jnp.arange(end)
        s = jnp.where(qi[:, None] >= ki[None, :], s, -jnp.inf)
        p = jax.nn.softmax(s, axis=-1).astype(v.dtype)
        outs.append(jnp.einsum('bhqk,bhkd->bhqd', p, v[:, :, :end]))
    return jnp.concatenate(outs, axis=2)

def mla_branch(cq, ckv, kpe, positions, norm_q, norm_kv, w_uq, w_ukv):
    b, s, _ = cq.shape
    h = MLA_HEADS
    q = (rmsnorm(cq, norm_q) @ w_uq).reshape(b, s, h, MLA_NOPE + MLA_ROPE)
    kv = (rmsnorm(ckv, norm_kv) @ w_ukv).reshape(b, s, h, MLA_NOPE + MLA_V)
    q_nope, q_pe = q[..., :MLA_NOPE], q[..., MLA_NOPE:]
    k_nope, v = kv[..., :MLA_NOPE], kv[..., MLA_NOPE:]
    cos, sin = rope_angles(positions, MLA_ROPE)
    q_pe = apply_rope_2(q_pe, cos[:, :, None, :], sin[:, :, None, :])
    k_pe = apply_rope_2(kpe, cos, sin)
    q = jnp.concatenate([q_nope, q_pe], axis=-1).transpose(0, 2, 1, 3)
    k = jnp.concatenate([k_nope, jnp.broadcast_to(k_pe[:, :, None, :], (b, s, h, MLA_ROPE))],
                        axis=-1).transpose(0, 2, 1, 3)
    v = v.transpose(0, 2, 1, 3)
    o = causal_block_attention(q, k, v, (MLA_NOPE + MLA_ROPE) ** -0.5)
    return o.transpose(0, 2, 1, 3).reshape(b, s, h * MLA_V)

def spatial_gating_branch(uv, ln_g, ln_b, w_s, b_s):
    b, s, _ = uv.shape
    uv = jax.nn.gelu(uv)
    u, v = uv[..., :SG_WIDTH], uv[..., SG_WIDTH:]
    v = layernorm(v, ln_g, ln_b)
    n = s // SG_CHUNK
    v = v.reshape(b, n, SG_CHUNK, SG_GROUPS, SG_WIDTH // SG_GROUPS)
    mask = jnp.tril(jnp.ones((SG_CHUNK, SG_CHUNK), dtype=w_s.dtype))
    mixed = jnp.einsum('gij,bnjgc->bnigc', w_s * mask, v) + b_s.T[:, :, None]
    return u * mixed.reshape(b, s, SG_WIDTH)

def gla_branch(q, k, v, gate_lr, out_gate, w_gate, b_gate, norm_o):
    b, s, _ = q.shape
    h, c = GLA_HEADS, GLA_CHUNK
    f32 = jnp.float32
    log_a = jax.nn.log_sigmoid((gate_lr @ w_gate + b_gate).astype(f32)) / GLA_GATE_TEMP
    q = q.astype(f32).reshape(b, s, h, GLA_DK) * (GLA_DK ** -0.5)
    k = k.astype(f32).reshape(b, s, h, GLA_DK)
    v = v.astype(f32).reshape(b, s, h, GLA_DV)
    log_a = log_a.reshape(b, s, h, GLA_DK)
    qc, kc, vc, ac = (to_chunks(t, c) for t in (q, k, v, log_a))
    idx = jnp.arange(c)
    incl = (idx[:, None] >= idx[None, :])[:, :, None]

    def step(state, inp):
        qi, ki, vi, ai = inp
        cum = jnp.cumsum(ai, axis=2)
        diff = cum[:, :, :, None, :] - cum[:, :, None, :, :]
        decay = jnp.where(incl, jnp.exp(jnp.where(incl, diff, 0.0)), 0.0)
        scores = jnp.einsum('bhik,bhjk,bhijk->bhij', qi, ki, decay)
        o = (jnp.einsum('bhik,bhkv->bhiv', qi * jnp.exp(cum), state)
             + jnp.einsum('bhij,bhjv->bhiv', scores, vi))
        last = cum[:, :, -1:, :]
        state = (jnp.exp(last[:, :, 0, :])[..., None] * state
                 + jnp.einsum('bhjk,bhjv->bhkv', ki * jnp.exp(last - cum), vi))
        return state, o

    state0 = jnp.zeros((b, h, GLA_DK, GLA_DV), f32)
    _, o = lax.scan(step, state0, (qc, kc, vc, ac))
    o = from_chunks(o)
    o = rmsnorm(o, norm_o) * jax.nn.silu(out_gate.astype(f32).reshape(b, s, h, GLA_DV))
    return o.reshape(b, s, h * GLA_DV)

def causal_depthwise_conv(x, w):
    return lax.conv_general_dilated(x, w[:, None, :], window_strides=(1,),
                                    padding=[(DN_CONV - 1, 0)],
                                    dimension_numbers=('NWC', 'WIO', 'NWC'),
                                    feature_group_count=x.shape[-1])

def deltanet_branch(q, k, v, a, bt, z, conv_w, a_log, dt_bias, norm_o):
    b, s, _ = q.shape
    h, c = DN_HEADS, DN_CHUNK
    f32 = jnp.float32
    qkv = jax.nn.silu(causal_depthwise_conv(jnp.concatenate([q, k, v], axis=-1), conv_w))
    q, k, v = jnp.split(qkv, [h * DN_DK, 2 * h * DN_DK], axis=-1)
    q = l2norm(q.astype(f32).reshape(b, s, h, DN_DK)) * (DN_DK ** -0.5)
    k = l2norm(k.astype(f32).reshape(b, s, h, DN_DK))
    v = v.astype(f32).reshape(b, s, h, DN_DV)
    beta = jax.nn.sigmoid(bt.astype(f32))
    g = -jnp.exp(a_log.astype(f32)) * jax.nn.softplus(a.astype(f32) + dt_bias.astype(f32))
    qc, kc, vc = (to_chunks(t, c) for t in (q, k, v))
    beta_c, g_c = to_chunks(beta, c), to_chunks(g, c)
    gam = jnp.cumsum(g_c, axis=-1)
    idx = jnp.arange(c)
    incl = idx[:, None] >= idx[None, :]
    strict = idx[:, None] > idx[None, :]
    diff = gam[..., :, None] - gam[..., None, :]
    dec_incl = jnp.where(incl, jnp.exp(jnp.where(incl, diff, 0.0)), 0.0)
    dec_strict = jnp.where(strict, dec_incl, 0.0)
    kk = jnp.einsum('nbhid,nbhjd->nbhij', kc, kc)
    lower = jnp.eye(c, dtype=f32) + beta_c[..., :, None] * kk * dec_strict
    rhs = jnp.concatenate([beta_c[..., None] * vc, (beta_c * jnp.exp(gam))[..., None] * kc], axis=-1)
    sol = lax.linalg.triangular_solve(lower, rhs, left_side=True, lower=True, unit_diagonal=True)
    w_c, x_c = sol[..., :DN_DV], sol[..., DN_DV:]
    attn = jnp.einsum('nbhid,nbhjd->nbhij', qc, kc) * dec_incl
    q_dec = qc * jnp.exp(gam)[..., None]
    k_dec = kc * jnp.exp(gam[..., -1:] - gam)[..., None]
    g_last = jnp.exp(gam[..., -1])

    def step(state, inp):
        w_i, x_i, attn_i, qd_i, kd_i, gl_i = inp
        u = w_i - jnp.einsum('bhck,bhkv->bhcv', x_i, state)
        o = jnp.einsum('bhck,bhkv->bhcv', qd_i, state) + jnp.einsum('bhij,bhjv->bhiv', attn_i, u)
        state = gl_i[..., None, None] * state + jnp.einsum('bhjk,bhjv->bhkv', kd_i, u)
        return state, o

    state0 = jnp.zeros((b, h, DN_DK, DN_DV), f32)
    _, o = lax.scan(step, state0, (w_c, x_c, attn, q_dec, k_dec, g_last))
    o = from_chunks(o)
    o = rmsnorm(o, norm_o) * jax.nn.silu(z.astype(f32).reshape(b, s, h, DN_DV))
    return o.reshape(b, s, h * DN_DV)

def mixer_block(h, positions, w_in, mla_norm_q, mla_norm_kv, mla_w_uq, mla_w_ukv,
                sg_ln_g, sg_ln_b, sg_w, sg_b, gla_w_gate, gla_b_gate, gla_norm,
                dn_conv, dn_a_log, dn_dt_bias, dn_norm, w_branch, w_out):
    b, s, _ = h.shape
    zin = h @ w_in
    splits = [int(i) for i in np.cumsum(IN_SIZES)[:-1]]
    (cq, ckv, kpe, sg_uv, gq, gk, gv, g_lr, g_og,
     dq, dk, dv, da, db, dz, gates) = jnp.split(zin, splits, axis=-1)
    o_a = mla_branch(cq, ckv, kpe, positions, mla_norm_q, mla_norm_kv, mla_w_uq, mla_w_ukv)
    o_b = spatial_gating_branch(sg_uv, sg_ln_g, sg_ln_b, sg_w, sg_b)
    o_c = gla_branch(gq, gk, gv, g_lr, g_og, gla_w_gate, gla_b_gate, gla_norm)
    o_d = deltanet_branch(dq, dk, dv, da, db, dz, dn_conv, dn_a_log, dn_dt_bias, dn_norm)
    branches = jnp.stack([o.astype(h.dtype) for o in (o_a, o_b, o_c, o_d)], axis=2)
    proj = jnp.einsum('bsnw,nwd->bsnd', branches, w_branch)
    gate = jax.nn.sigmoid(gates).reshape(b, s, N_BRANCH, D_MODEL)
    merged = jnp.sum(gate * proj, axis=2)
    return merged @ w_out

def cross_attention(h, mem_n, wq, wk, wv, wo):
    b, s, _ = h.shape
    m = mem_n.shape[1]
    q = (h @ wq).reshape(b, s, XATTN_HEADS, XATTN_DIM)
    k = (mem_n @ wk).reshape(b, m, XATTN_HEADS, XATTN_DIM)
    v = (mem_n @ wv).reshape(b, m, XATTN_HEADS, XATTN_DIM)
    sc = jnp.einsum('bshd,bmhd->bhsm', q, k).astype(jnp.float32) * (XATTN_DIM ** -0.5)
    p = jax.nn.softmax(sc, axis=-1).astype(v.dtype)
    o = jnp.einsum('bhsm,bmhd->bshd', p, v).reshape(b, s, XATTN_HEADS * XATTN_DIM)
    return o @ wo

def squared_relu_mlp(h, w_up, w_down):
    a = jax.nn.relu(h @ w_up)
    return (a * a) @ w_down

def second_inputs(seed: int = 0) -> dict:
    key = jax.random.key(seed)
    ks = iter(jax.random.split(key, 48))
    f32 = jnp.float32
    L = DEPTH

    def nrm(shape, scale):
        return jax.random.normal(next(ks), shape, f32) * scale

    def gain(shape):
        return 1.0 + 0.1 * jax.random.normal(next(ks), shape, f32)

    x = nrm((BATCH, SEQ, D_MODEL), 1.0)
    mem = nrm((BATCH, MEM_LEN, D_MODEL), 1.0)
    offsets = jax.random.randint(next(ks), (BATCH, 1), 0, 1024, dtype=jnp.int32)
    positions = (offsets + jnp.arange(SEQ, dtype=jnp.int32)[None, :]).astype(jnp.int32)
    dn_ch = 2 * DN_HEADS * DN_DK + DN_HEADS * DN_DV
    a_init = jax.random.uniform(next(ks), (L, DN_HEADS), f32, 1.0, 16.0)
    dt = jnp.exp(jax.random.uniform(next(ks), (L, DN_HEADS), f32, math.log(1e-3), math.log(1e-1)))
    return {
        'x': x,
        'mem': mem,
        'positions': positions,
        'norm_mix': gain((L, D_MODEL)),
        'w_in': nrm((L, D_MODEL, IN_WIDTH), D_MODEL ** -0.5),
        'mla_norm_q': gain((L, MLA_Q_RANK)),
        'mla_norm_kv': gain((L, MLA_KV_RANK)),
        'mla_w_uq': nrm((L, MLA_Q_RANK, MLA_HEADS * (MLA_NOPE + MLA_ROPE)), MLA_Q_RANK ** -0.5),
        'mla_w_ukv': nrm((L, MLA_KV_RANK, MLA_HEADS * (MLA_NOPE + MLA_V)), MLA_KV_RANK ** -0.5),
        'sg_ln_g': gain((L, SG_WIDTH)),
        'sg_ln_b': nrm((L, SG_WIDTH), 0.02),
        'sg_w': nrm((L, SG_GROUPS, SG_CHUNK, SG_CHUNK), SG_CHUNK ** -0.5),
        'sg_b': 1.0 + nrm((L, SG_GROUPS, SG_CHUNK), 0.1),
        'gla_w_gate': nrm((L, GLA_GATE_RANK, GLA_HEADS * GLA_DK), GLA_GATE_RANK ** -0.5),
        'gla_b_gate': nrm((L, GLA_HEADS * GLA_DK), 0.1),
        'gla_norm': gain((L, GLA_DV)),
        'dn_conv': nrm((L, DN_CONV, dn_ch), DN_CONV ** -0.5),
        'dn_a_log': jnp.log(a_init),
        'dn_dt_bias': dt + jnp.log(-jnp.expm1(-dt)),
        'dn_norm': gain((L, DN_DV)),
        'w_branch': nrm((L, N_BRANCH, BRANCH_WIDTH_2, D_MODEL), BRANCH_WIDTH_2 ** -0.5),
        'w_out': nrm((L, D_MODEL, D_MODEL), D_MODEL ** -0.5),
        'norm_xattn': gain((L, D_MODEL)),
        'norm_mem': gain((L, D_MODEL)),
        'xattn_wq': nrm((L, D_MODEL, XATTN_HEADS * XATTN_DIM), D_MODEL ** -0.5),
        'xattn_wk': nrm((L, D_MODEL, XATTN_HEADS * XATTN_DIM), D_MODEL ** -0.5),
        'xattn_wv': nrm((L, D_MODEL, XATTN_HEADS * XATTN_DIM), D_MODEL ** -0.5),
        'xattn_wo': nrm((L, XATTN_HEADS * XATTN_DIM, D_MODEL), D_MODEL ** -0.5),
        'norm_mlp': gain((L, D_MODEL)),
        'w_up': nrm((L, D_MODEL, MLP_HIDDEN), D_MODEL ** -0.5),
        'w_down': nrm((L, MLP_HIDDEN, D_MODEL), MLP_HIDDEN ** -0.5),
        'norm_final': gain((D_MODEL,)),
    }

def second_block(x, mem, positions, norm_mix, w_in, mla_norm_q, mla_norm_kv, mla_w_uq, mla_w_ukv,
              sg_ln_g, sg_ln_b, sg_w, sg_b, gla_w_gate, gla_b_gate, gla_norm,
              dn_conv, dn_a_log, dn_dt_bias, dn_norm, w_branch, w_out,
              norm_xattn, norm_mem, xattn_wq, xattn_wk, xattn_wv, xattn_wo,
              norm_mlp, w_up, w_down, norm_final):
    for l in range(DEPTH):
        h = rmsnorm(x, norm_mix[l])
        x = x + mixer_block(h, positions, w_in[l], mla_norm_q[l], mla_norm_kv[l], mla_w_uq[l], mla_w_ukv[l],
                            sg_ln_g[l], sg_ln_b[l], sg_w[l], sg_b[l], gla_w_gate[l], gla_b_gate[l], gla_norm[l],
                            dn_conv[l], dn_a_log[l], dn_dt_bias[l], dn_norm[l], w_branch[l], w_out[l])
        x = x + cross_attention(rmsnorm(x, norm_xattn[l]), rmsnorm(mem, norm_mem[l]),
                                xattn_wq[l], xattn_wk[l], xattn_wv[l], xattn_wo[l])
        x = x + squared_relu_mlp(rmsnorm(x, norm_mlp[l]), w_up[l], w_down[l])
    return rmsnorm(x, norm_final)


def setup_inputs(seed=0):
    out = dict(first_inputs(seed))
    for name, value in second_inputs(seed + 1).items():
        if name != "x":
            out[name + "_2"] = value
    return out


def reference(
    x, norm_mix_pre, w_in, conv_w, conv_b, dt_bias, a_log, d_skip, ssm_norm, fox_fbias, w_gate,
    b_gate, w_branch, w_out, norm_mix_post, norm_ffn_pre, w_ffn_in, w_ffn_out, norm_ffn_post,
    mem_2, positions_2, norm_mix_2, w_in_2, mla_norm_q_2, mla_norm_kv_2, mla_w_uq_2,
    mla_w_ukv_2, sg_ln_g_2, sg_ln_b_2, sg_w_2, sg_b_2, gla_w_gate_2, gla_b_gate_2, gla_norm_2,
    dn_conv_2, dn_a_log_2, dn_dt_bias_2, dn_norm_2, w_branch_2, w_out_2, norm_xattn_2,
    norm_mem_2, xattn_wq_2, xattn_wk_2, xattn_wv_2, xattn_wo_2, norm_mlp_2, w_up_2, w_down_2,
    norm_final_2,
):
    x = first_block(
        x, norm_mix_pre, w_in, conv_w, conv_b, dt_bias, a_log, d_skip, ssm_norm, fox_fbias,
        w_gate, b_gate, w_branch, w_out, norm_mix_post, norm_ffn_pre, w_ffn_in, w_ffn_out,
        norm_ffn_post,
    )
    return second_block(
        x, mem_2, positions_2, norm_mix_2, w_in_2, mla_norm_q_2, mla_norm_kv_2, mla_w_uq_2,
        mla_w_ukv_2, sg_ln_g_2, sg_ln_b_2, sg_w_2, sg_b_2, gla_w_gate_2, gla_b_gate_2,
        gla_norm_2, dn_conv_2, dn_a_log_2, dn_dt_bias_2, dn_norm_2, w_branch_2, w_out_2,
        norm_xattn_2, norm_mem_2, xattn_wq_2, xattn_wk_2, xattn_wv_2, xattn_wo_2, norm_mlp_2,
        w_up_2, w_down_2, norm_final_2,
    )


_drawn_inputs = setup_inputs


def setup_inputs(seed=0):
    import zlib

    import numpy as np

    out = dict(_drawn_inputs(seed))
    spreads = {}
    factors = {'b_gate': 4.061,
     'mla_norm_q_2': 8.0,
     'mla_norm_kv_2': 5.012,
     'sg_ln_g_2': 3.588,
     'sg_ln_b_2': 8.0,
     'gla_b_gate_2': 5.486,
     'gla_norm_2': 2.746,
     'dn_norm_2': 3.48,
     'norm_xattn_2': 8.0,
     'norm_mem_2': 5.727}
    for name, (base, spread) in spreads.items():
        noise = np.random.default_rng([zlib.crc32(name.encode()), seed]).standard_normal(out[name].shape)
        drawn = base * np.exp(spread * noise) if base else spread * noise
        out[name] = jnp.asarray(drawn.astype(out[name].dtype))
    for name, factor in factors.items():
        out[name] = (out[name] * factor).astype(out[name].dtype)
    return out
```

```python
from contextlib import ExitStack

import numpy as np

import concourse.bass as bass
from concourse import mybir

F32 = mybir.dt.float32
BF16 = mybir.dt.bfloat16
I32 = mybir.dt.int32
U32 = mybir.dt.uint32
ALU = mybir.AluOpType
ACT = mybir.ActivationFunctionType
AX_X = mybir.AxisListType.X

P = 128
SEQ = 256
NT = SEQ // P
D = 1024
KD = D // P
DEPTH = 2
EPS = 1e-6
NEG = -1e30
TAKEN = -3e38
RING = 2
SLOT = 8 * 528

C_ID, C_U, C_MT, C_MQ, N_CONST = 0, 128, 640, 768, 896
C1_COS, C1_SIN, C1_ROT, N_CONST1 = 0, 256, 512, 640
C2_LV, C2_B64, C2_R2, C2_INV, N_CONST2 = 0, 1024, 1152, 1184, 1186


def shape_constants():
    c = np.zeros((P, N_CONST), np.float32)
    r = np.arange(P)
    t = np.arange(SEQ)
    c[:, C_ID:C_ID + P] = np.eye(P)
    for tile in range(NT):
        c[:, C_U + tile * SEQ:C_U + (tile + 1) * SEQ] = (tile * P + r)[:, None] <= t[None, :]
    c[:, C_MT:C_MT + P] = np.where(r[:, None] > r[None, :], NEG, 0)
    c[:, C_MQ:C_MQ + P] = np.where(r[None, :] > r[:, None], NEG, 0)
    return c


def shape_constants_1():
    c = np.zeros((P, N_CONST1), np.float32)
    r = np.arange(P)
    t = np.arange(SEQ)
    inv = (np.float32(10000.0) ** (-np.arange(0, 64, 2, dtype=np.float32) / np.float32(64))).astype(np.float32)
    ang = (t.astype(np.float32)[None, :] * inv[r % 32][:, None]).astype(np.float32).astype(np.float64)
    c[:, C1_COS:C1_COS + SEQ] = np.cos(ang)
    c[:, C1_SIN:C1_SIN + SEQ] = np.sin(ang)
    for m in range(P):
        k = m + 32 if m % 64 < 32 else m - 32
        c[k, C1_ROT + m] = -1.0 if m % 64 < 32 else 1.0
    return c


def shape_constants_2():
    c = np.zeros((P, N_CONST2), np.float32)
    r = np.arange(P)
    for n, b in enumerate((64, 32, 16, 8, 4, 2, 1)):
        same = r[:, None] // (2 * b) == r[None, :] // (2 * b)
        c[:, C2_LV + n * P:C2_LV + (n + 1) * P] = same & (r[:, None] // b % 2 == 0) & (r[None, :] // b % 2 == 1)
    c[:, C2_LV + 7 * P:C2_LV + 8 * P] = np.eye(P)
    c[:, C2_B64:C2_B64 + P] = r[:, None] // 64 == r[None, :] // 64
    for m in range(32):
        k = m + 16 if m < 16 else m - 16
        c[64 + k, C2_R2 + m] = -1.0 if m < 16 else 1.0
    inv2 = (np.float32(10000.0) ** (-np.arange(0, 32, 2, dtype=np.float32) / np.float32(32))).astype(np.float32)
    c[64:96, C2_INV] = inv2[np.arange(32) % 16]
    return c


def column(ap, n):
    return ap.broadcast_to([ap.shape[0], n])


class Weights:

    def __init__(self, chunks):
        self.chunks = chunks
        self.total = [0] * RING
        self.ready = []
        for w, (_, _, sources) in enumerate(chunks):
            self.total[w % RING] += 16 * len(sources)
            self.ready.append(self.total[w % RING])


W1 = 512
HID1 = 2816
KH1 = HID1 // P
IN1 = [
    (512, 512, [("F", 0, 2, "xbc", 0), ("F", 256, 2, "xbc", 2)]),
    (1024, 520, [("F", 0, 2, "xbc", 4), ("F", 256, 2, "xbc", 6), ("T", 512, 8, "dt")]),
    (2568, 520, [("T", 0, 512, "fv"), ("T", 512, 8, "ff")]),
    (3088, 512, [("F", 0, 2, "mq", 0), ("F", 256, 2, "mq", 2)]),
    (3600, 512, [("F", 0, 2, "mk", 0), ("F", 256, 2, "mk", 2)]),
    (6160, 324, [("F", 0, 2, "iqk", 0), ("I", 256, 1, "iqk", 2), ("T", 320, 4, "iw")]),
    (4624, 512, [("F", 0, 2, "dq", 0), ("F", 256, 2, "dq", 2)]),
    (5136, 512, [("F", 0, 2, "dk", 0), ("F", 256, 2, "dk", 2)]),
    (1544, 512, [("F", 0, 2, "fq", 0), ("F", 256, 2, "fq", 2)]),
    (2056, 512, [("F", 0, 2, "fk", 0), ("F", 256, 2, "fk", 2)]),
    (4112, 512, [("T", 0, 512, "mv")]),
    (5648, 512, [("T", 0, 512, "dv")]),
    (0, 512, [("T", 0, 512, "z")]),
]
ROPES = ["mq", "mk", "iqk", "dq", "dk"]
QSCALE = {"fq": 0.125, "mq": 0.125, "dq": 0.125}
PGM, PCW, PCB, PSN, PBG, PGF, NPAR1 = 0, 8, 40, 48, 52, 84, 92


def units_of(pieces):
    out = []
    for p in pieces:
        if p[0] in "FI":
            out.append((p[0], p[1], p[2], p[3], p[4]))
        elif p[2] > 256:
            out += [("T", p[1], p[2], p[3], t) for t in range(NT)]
        else:
            out.append(("S", p[1], p[2], p[3], 0))
    return out


def first_block(nc, ps, x, con, bfc, a):
    with ExitStack() as ctx:
        def sb(name, shape, dt=F32):
            return ctx.enter_context(nc.sbuf_tensor("a_" + name, shape, dt))

        def sem(name):
            s = ctx.enter_context(nc.semaphore("a_" + name))
            sems.append(s)
            return s

        sems = []
        ident = con[:, C_ID:C_ID + P]
        ident_bf, maskT_bf, maskQ_bf = (bfc[:, i, :] for i in range(3))
        tri = con[:, C_U:C_U + NT * SEQ].rearrange("p (t l) -> p t l", t=NT)
        maskQ = con[:, C_MQ:C_MQ + P]
        con1 = sb("con1", [P, N_CONST1])
        cos, sin = con1[:, C1_COS:C1_COS + SEQ], con1[:, C1_SIN:C1_SIN + SEQ]
        rot = con1[:, C1_ROT:C1_ROT + P]

        ring = sb("ring", [P, RING, SLOT])
        hT = sb("hT", [P, KD, SEQ])
        xm = sb("xm", [P, NT, D])
        par = sb("par", [NPAR1, P])
        parT = sb("parT", [P, NPAR1])
        small = sb("small", [P, 4, 8])
        nident = sb("nident", [16, 16])
        xbcp = sb("xbcp", [P, 8, SEQ + 4])
        probs = xbcp[:, :, 0:SEQ]
        xbc = sb("xbc", [P, 8, SEQ])
        merged = xbc
        sc8 = sb("sc8", [P, 8, 384])
        rt = sc8[:, :, :].rearrange("p a b -> p (a b)")[:, 0:2 * D].rearrange("p (a b) -> p a b", a=8)
        gpost = sc8[:, :, :].rearrange("p a b -> p (a b)")[:, 0:2 * D].rearrange("p (a b) -> p a b", a=2)
        xd = sb("xd", [P, 2, NT, W1])
        pT = xd[:, :, :, :].rearrange("p a t c -> p (a t c)").rearrange("p (s w) -> p s w", s=8)
        rl = pT[:, 0:4, :]
        bufs = {n: sb(n, [P, 4, SEQ]) for n in ("fq", "fk", "mq", "mk", "dq", "dk")}
        bufs |= {n: sb(n, [P, NT, W1]) for n in ("fv", "mv", "dv", "z")}
        iqk = sb("iqk", [P, 3, SEQ])
        y = sb("y", [P, NT, W1])
        o = y
        dtff = sb("dtff", [P, NT, 16])
        iw = sb("iw", [P, NT, 4])[:, :, :]
        sp = sb("sp", [P, 6, NT * 16])
        lcat = sb("lcat", [P, NT, 16])
        asg = sb("asg", [P, 16])
        cumT = sb("cumT", [16, SEQ])
        ncum = sb("ncum", [P, NT, 16])
        cb = sb("cb", [P, 2, 384])
        ys = sb("ys", [P, 4, 4, SEQ])
        gates = sb("gates", [P, 32, SEQ])
        hid = gates
        ffg = bufs["fq"][:, :, :].rearrange("p a b -> p (a b)").rearrange("p (a b) -> p a b", a=2)
        isc = sb("isc", [P, SEQ])
        top8 = sb("top8", [P, 8])
        pen = sb("pen", [P, SEQ], BF16)
        nmx = sb("nmx", [P, 2, 8])
        rsum = sb("rsum", [P, 2, 8])
        rinv = sb("rinv", [P, 8])
        ssq = sb("ssq", [P, 5, 4])
        msq = sb("msq", [P, 5, 4])
        rstd = sb("rstd", [P, 5, 4])
        nhalf = sb("nhalf", [P, 4])
        bufs.update(xbc=xbcp[:, :, 3:SEQ + 3], iqk=iqk, dt=dtff[:, :, 0:8], ff=dtff[:, :, 8:16], iw=iw)

        con1_in = sem("con1_in")
        par_in, small_in, gpost_in = sem("par_in"), sem("small_in"), sem("gpost_in")
        landed = [sem(f"landed{i}") for i in range(RING)]
        down_used = sem("down_used")
        full, free = sem("full"), sem("free")
        par_ps, par_ok = sem("par_ps"), sem("par_ok")
        ssq_ok, msq_ok, rstd_ok = sem("ssq_ok"), sem("msq_ok"), sem("rstd_ok")
        xn_ok, x_ok = sem("xn_ok"), sem("x_ok")
        conv_ok, silu_ok, init_ok = sem("conv_ok"), sem("silu_ok"), sem("init_ok")
        spv, spe = sem("spv"), sem("spe")
        rope_ps, rope_ok = sem("rope_ps"), sem("rope_ok")
        lcat_ok, cum_ps, cum_ok = sem("lcat_ok"), sem("cum_ps"), sem("cum_ok")
        cb_ps, cb_ok, xs_ps, xs_ok = sem("cb_ps"), sem("cb_ok"), sem("xs_ps"), sem("xs_ok")
        dec_ps, dec_ok, sc_ok = sem("dec_ps"), sem("dec_ok"), sem("sc_ok")
        y_ps, y_free, yt_ok, yt_ps, yt_out = sem("y_ps"), sem("y_free"), sem("yt_ok"), sem("yt_ps"), sem("yt_out")
        zs_ok = sem("zs_ok")
        ix_ps, ix_rl, pen_ok = sem("ix_ps"), sem("ix_rl"), sem("pen_ok")
        qk_ps, mx_ok, ex_ok, pt_ps = sem("qk_ps"), sem("mx_ok"), sem("ex_ok"), sem("pt_ps")
        pt_a, pt_v, o_ps, o_ok, ot_ps, ot_ok = (sem(n) for n in ("pt_a", "pt_v", "o_ps", "o_ok", "ot_ps", "ot_ok"))
        sig_ok, pr_ps, pr_free, mg_ok = sem("sig_ok"), sem("pr_ps"), sem("pr_free"), sem("mg_ok")
        mix_ok = sem("mix_ok")
        fg_ps, fg_free, fu_ps, fu_free = sem("fg_ps"), sem("fg_free"), sem("fu_ps"), sem("fu_free")
        dn_ps, dn_ok = sem("dn_ps"), sem("dn_ok")
        dch = sem("dch")
        ach = sem("ach")

        def cols(src, l, c, n):
            return src[bass.ds(l, 1), :, c:c + n].rearrange("a (k p) c -> p (a k) c", p=P)

        def rows(src, l, r, k):
            return src[bass.ds(l, 1), r:r + k * P, :].rearrange("a (k p) c -> p (a k) c", p=P)

        chunks = [(8, n, [lambda l, c=c, n=n: (0, cols(a["w_in"], l, c, n))]) for c, n, _ in IN1]
        N_IN = len(IN1)
        chunks += [(8, 512, [lambda l, c=c: (0, cols(a["w_gate"], l, 512 * c, 512))]) for c in range(8)]
        chunks += [(4, D, [lambda l, n=n: (0, a["w_branch"][bass.ds(l, 1), n].rearrange(
            "a (k p) c -> p (a k) c", p=P))]) for n in range(4)]
        chunks += [(8, 512, [lambda l, c=c: (0, cols(a["w_out"], l, 512 * c, 512))]) for c in range(2)]
        chunks += [(8, 512, [lambda l, c=c: (0, cols(a["w_ffn_in"], l, 256 * c, 256)),
                             lambda l, c=c: (256, cols(a["w_ffn_in"], l, HID1 + 256 * c, 256))])
                   for c in range(HID1 // 256)]
        DOWN = [(4 * c, min(4, KH1 - 4 * c)) for c in range((KH1 + 3) // 4)]
        chunks += [(k, D, [lambda l, r=r, k=k: (0, rows(a["w_ffn_out"], l, r * P, k))]) for r, k in DOWN]
        W = Weights(chunks)
        C_GATE, C_BR, C_OUT, C_FIN = N_IN, N_IN + 8, N_IN + 12, N_IN + 14
        C_FOUT = C_FIN + HID1 // 256

        def chunk(w):
            k, c, _ = chunks[w]
            return ring[:, w % RING, 0:k * c].rearrange("p (k c) -> p k c", c=c)

        in_units = [units_of(p) for _, _, p in IN1]
        U_X = 4
        U_IN = [U_X + sum(len(u) for u in in_units[:i]) for i in range(N_IN + 1)]
        U_GATE = U_IN[-1]
        U_OUT = U_GATE + 16
        U_X2 = U_OUT + 4
        ATT = [("fq", "fk", "fv", 1), ("mq", "mk", "mv", 2), ("dq", "dk", "dv", 3)]
        L = ps[:, 4:8, :].rearrange("p b (s w) -> p (b s) w", s=2)

        def head(s):
            return (s % 4) * 2 + s // 4

        read = [(full, U_IN[i + 1]) for i in range(N_IN)]
        read += [(full, U_GATE + 2 * c + 2) for c in range(8)]
        read += [(pr_ps, 4 * n + 4) for n in range(4)]
        read += [(full, U_OUT + 2 * c + 2) for c in range(2)]
        read += [(fu_ps, c + 1) for c in range(HID1 // 256)]
        read += [(down_used, c + 1) for c in range(len(DOWN) - 1)]

        with nc.Block() as block:

            @block.sync
            def _(sp_):
                sp_.dma_start(con1[:, :], a["constants_1"]).then_inc(con1_in, 16)
                sp_.wait_ge(con1_in, 16)

        with nc.Fori(0, DEPTH) as l:
            with nc.Block() as block:

                @block.sync
                def _(sp_):
                    row = 0
                    for name, n in (("norm_mix_pre", 8), ("conv_w", 32), ("conv_b", 8), ("ssm_norm", 4),
                                    ("b_gate", 32), ("norm_ffn_pre", 8)):
                        src = a[name][bass.ds(l, 1)]
                        src = src.rearrange("a j (k p) -> (a j k) p", p=P) if name == "conv_w" else \
                            src.rearrange("a (k p) -> (a k) p", p=P)
                        sp_.dma_start(par[row:row + n, :], src).then_inc(par_in, 16)
                        row += n
                    for i, name in enumerate(("dt_bias", "a_log", "d_skip", "fox_fbias")):
                        sp_.dma_start(small[:, i, :], a[name][bass.ds(l, 1)].broadcast_to([P, 8])
                                      ).then_inc(small_in, 16)
                    for w, (k, c, sources) in enumerate(chunks):
                        if w >= RING:
                            sp_.wait_ge(*read[w - RING])
                        if w == C_BR:
                            sp_.wait_ge(y_ps, 1)
                            for i, name in enumerate(("norm_mix_post", "norm_ffn_post")):
                                sp_.dma_start(gpost[:, i, :], a[name][bass.ds(l, 1)].broadcast_to([P, D])
                                              ).then_inc(gpost_in, 16)
                        for source in sources:
                            at, src = source(l)
                            sp_.dma_start(chunk(w)[:, :, at:at + src.shape[2]], src).then_inc(landed[w % RING], 16)

                @block.tensor
                def _(pe):
                    def bank(u):
                        if u >= 2:
                            pe.wait_ge(free, u - 1)
                        return ps[:, u % 2, :]

                    def take(w):
                        pe.wait_ge(landed[w % RING], W.ready[w])

                    def transposed(u0, n):
                        pe.wait_ge(xn_ok, n)
                        for k in range(KD):
                            if k % 2 == 0:
                                b = bank(u0 + k // 2)
                            for t in range(NT):
                                mm = nc.tensor.transpose(b[:, (k % 2) * SEQ + t * P:(k % 2) * SEQ + (t + 1) * P],
                                                         xm[:, t, k * P:(k + 1) * P], ident)
                            if k % 2:
                                mm.then_inc(full, 1)

                    def feature_unit(out, w, c, nb, act):
                        wt = chunk(w)
                        K = chunks[w][0]
                        for b in range(nb):
                            for k in range(K):
                                mm = nc.tensor.matmul(out[:, b * SEQ:(b + 1) * SEQ], wt[:, k, c + b * P:c + (b + 1) * P],
                                                      act[:, k, :], start=k == 0, stop=k == K - 1)
                        return mm

                    def token_unit(out, w, c, n, t, act):
                        wt = chunk(w)
                        K = chunks[w][0]
                        for k in range(K):
                            mm = nc.tensor.matmul(out, act[:, k, t * P:(t + 1) * P], wt[:, k, c:c + n],
                                                  start=k == 0, stop=k == K - 1)
                        return mm

                    def in_chunk(i):
                        take(i)
                        for n, (kind, c, size, _, at) in enumerate(in_units[i]):
                            b = bank(U_IN[i] + n)
                            if kind == "F":
                                mm = feature_unit(b, i, c, size, hT)
                            elif kind == "I":
                                for half in range(2):
                                    for k in range(KD):
                                        mm = nc.tensor.matmul(b[64 * half:64 * half + 64, 0:SEQ],
                                                              chunk(i)[:, k, c:c + 64], hT[:, k, :],
                                                              start=k == 0, stop=k == KD - 1)
                            elif kind == "T":
                                mm = token_unit(b[:, 0:size], i, c, size, at, hT)
                            else:
                                for t in range(NT):
                                    mm = token_unit(b[:, t * size:(t + 1) * size], i, c, size, t, hT)
                            mm.then_inc(full, 1)

                    def gate_unit(g):
                        w = C_GATE + g // 2
                        if g % 2 == 0:
                            take(w)
                        feature_unit(bank(U_GATE + g), w, (g % 2) * SEQ, 2, hT).then_inc(full, 1)

                    def rope(r):
                        name = ROPES[r]
                        nb = 3 if name == "iqk" else 4
                        i = [j for j in range(N_IN) if any(p[3] == name for p in IN1[j][2])][0]
                        pe.wait_ge(free, U_IN[i + 1] - (1 if name == "iqk" else 0))
                        if r >= 2:
                            pe.wait_ge(rope_ok, r - 1)
                        for b in range(nb):
                            mm = nc.tensor.matmul(ps[:, 4 + 2 * (r % 2) + b // 2, (b % 2) * SEQ:(b % 2 + 1) * SEQ], rot,
                                                  bufs[name][:, b, :], start=True, stop=True)
                        mm.then_inc(rope_ps, 1)

                    def qk(n):
                        q, k, _, _ = ATT[n // 2]
                        qt = n % 2
                        w = P * (qt + 1)
                        if n == 0:
                            pe.wait_ge(dec_ok, 2)
                        else:
                            pe.wait_ge(pt_a, n)
                            pe.wait_ge(pt_v, n)
                        if n == 4:
                            pe.wait_ge(rope_ok, 5)
                        if n == 2:
                            pe.wait_ge(rope_ok, 2)
                        if n >= 4:
                            pe.wait_ge(ix_rl, n - 3)
                            pe.wait_ge(pen_ok, n - 3)
                        for s in range(8):
                            h = head(s)
                            base, blk = 64 * (h % 2), h // 2
                            nc.tensor.matmul(L[:, s, 0:w], bufs[q][base:base + 64, blk, qt * P:(qt + 1) * P],
                                             bufs[k][base:base + 64, blk, 0:w], start=True, stop=False)
                            if n < 2:
                                nc.tensor.matmul(L[:, s, 0:w], column(nident[:, 8 + h:9 + h], P), cumT[:, 0:w],
                                                 start=False, stop=False)
                                nc.tensor.matmul(L[:, s, 0:w], cumT[:, qt * P:(qt + 1) * P],
                                                 column(ident[0:16, 8 + h:9 + h], w), start=False, stop=False)
                            if n >= 4:
                                nc.tensor.matmul(L[:, s, 0:w], ident_bf, pen[:, 0:w], start=False, stop=False)
                            mm = nc.tensor.matmul(L[:, s, w - P:w], ident_bf, maskQ_bf, start=False, stop=True)
                        mm.then_inc(qk_ps, 1)

                    def p_turn(n):
                        pe.wait_ge(ex_ok, n + 1)
                        for s in range(8):
                            for kt in range(n % 2 + 1):
                                mm = nc.tensor.transpose(L[:, s, kt * P:(kt + 1) * P], probs[:, s, kt * P:(kt + 1) * P],
                                                         ident)
                        mm.then_inc(pt_ps, 1)

                    def pv(n):
                        pe.wait_ge(pt_a, n + 1)
                        pe.wait_ge(pt_v, n + 1)
                        if n == 0:
                            pe.wait_ge(y_free, 1)
                        else:
                            pe.wait_ge(o_ok, n)
                        v = bufs[ATT[n // 2][2]]
                        for s in range(8):
                            h = head(s)
                            for kt in range(n % 2 + 1):
                                mm = nc.tensor.matmul(ps[:, 2, h * 64:(h + 1) * 64], pT[:, s, kt * P:(kt + 1) * P],
                                                      v[:, kt, h * 64:(h + 1) * 64], start=kt == 0, stop=kt == n % 2)
                        mm.then_inc(o_ps, 1)

                    def o_turn(n):
                        pe.wait_ge(o_ok, n + 1)
                        if n == 0:
                            pe.wait_ge(yt_out, 2)
                        else:
                            pe.wait_ge(ot_ok, n)
                        for b in range(4):
                            mm = nc.tensor.transpose(ps[:, 3, b * P:(b + 1) * P], o[:, n % 2, b * P:(b + 1) * P], ident)
                        mm.then_inc(ot_ps, 1)

                    def index_scores(t):
                        pe.wait_ge(rope_ok, 5)
                        pe.wait_ge(pt_a, 4 + t)
                        pe.wait_ge(pt_v, 4 + t)
                        w = P * (t + 1)
                        for h in range(4):
                            base = 64 * (h % 2)
                            s = 4 * (h % 2) + h // 2
                            mm = nc.tensor.matmul(L[:, s, 0:w], iqk[base:base + 64, h // 2, t * P:(t + 1) * P],
                                                  iqk[base:base + 64, 2, 0:w], start=True, stop=True)
                        mm.then_inc(ix_ps, 1)

                    pe.wait_ge(par_in, 96)
                    nc.tensor.transpose(ps[:, 2, 0:NPAR1], par[:, :], ident[0:NPAR1, 0:NPAR1]).then_inc(par_ps, 1)
                    transposed(0, 1)
                    pe.wait_ge(free, U_X)
                    for i in range(N_IN):
                        in_chunk(i)
                        if 5 <= i < 10:
                            rope(i - 5)
                    pe.wait_ge(lcat_ok, 1)
                    for t in range(NT):
                        nc.tensor.matmul(ps[0:16, 2, 0:SEQ], lcat[:, t, :], tri[:, t, :], start=t == 0, stop=t == NT - 1)
                    for t in range(NT):
                        for u in range(t + 1):
                            mm = nc.tensor.matmul(ps[:, 3, t * 16:(t + 1) * 16], tri[:, u, t * P:(t + 1) * P],
                                                  lcat[:, u, :], start=u == 0, stop=u == t)
                    mm.then_inc(cum_ps, 1)
                    gate_unit(0)
                    pe.wait_ge(cum_ok, 1)
                    pe.wait_ge(silu_ok, 1)
                    for g in range(2):
                        nc.tensor.matmul(ps[:, 2 + g, 0:SEQ], xbc[:, 4 + g, 0:P], xbc[:, 6 + g, :], start=True, stop=True)
                        mm = nc.tensor.matmul(ps[:, 2 + g, SEQ:384], xbc[:, 4 + g, P:SEQ], xbc[:, 6 + g, P:SEQ],
                                              start=True, stop=True)
                    mm.then_inc(cb_ps, 1)
                    pe.wait_ge(rope_ok, 5)
                    for t in range(NT):
                        for b in range(4):
                            mm = nc.tensor.transpose(ps[:, 4 + t, b * P:(b + 1) * P], xbc[:, b, t * P:(t + 1) * P], ident)
                    mm.then_inc(xs_ps, 1)
                    gate_unit(1)
                    for r in range(2):
                        if r == 0:
                            pe.wait_ge(xs_ok, 1)
                        else:
                            pe.wait_ge(dec_ok, 1)
                        for j in range(4):
                            h = 4 * r + j
                            pick = column(ident[0:16, h:h + 1], P)
                            b = ps[:, 4 + j, :]
                            nc.tensor.matmul(b[:, 0:SEQ], pick, cumT[:, :], start=True, stop=False)
                            nc.tensor.matmul(b[:, 0:P], ident_bf, maskT_bf, start=False, stop=True)
                            nc.tensor.matmul(b[:, SEQ:384], pick, cumT[:, P:SEQ], start=True, stop=False)
                            mm = nc.tensor.matmul(b[:, SEQ:384], ident_bf, maskT_bf, start=False, stop=True)
                        mm.then_inc(dec_ps, 1)
                        if r == 0:
                            gate_unit(2)
                    gate_unit(3)
                    pe.wait_ge(cb_ok, 1)
                    pe.wait_ge(sc_ok, 2)
                    for t in range(NT):
                        for h in range(8):
                            for s in range(t + 1):
                                c = (t * P) if s == 0 else SEQ
                                mm = nc.tensor.matmul(ps[:, 2 + t, h * 64:(h + 1) * 64], sc8[:, h, c:c + P],
                                                      xd[:, 0, s, h * 64:(h + 1) * 64], start=s == 0, stop=s == t)
                    mm.then_inc(y_ps, 1)
                    qk(0)
                    gate_unit(4)
                    for t in range(NT):
                        pe.wait_ge(yt_ok, 1)
                        pe.wait_ge(y_free, 1)
                        if t:
                            pe.wait_ge(yt_out, t)
                        for b in range(4):
                            mm = nc.tensor.transpose(ps[:, 3, b * P:(b + 1) * P], y[:, t, b * P:(b + 1) * P], ident)
                        mm.then_inc(yt_ps, 1)
                    pe_g = [5]

                    def gate():
                        if pe_g[0] < 16:
                            gate_unit(pe_g[0])
                            pe_g[0] += 1
                    p_turn(0)
                    for n in range(6):
                        gate()
                        pv(n)
                        if n + 1 < 6:
                            if n + 1 >= 4:
                                index_scores(n - 3)
                                gate()
                            qk(n + 1)
                            gate()
                        o_turn(n)
                        if n + 1 < 6:
                            p_turn(n + 1)
                    while pe_g[0] < 16:
                        gate()
                    for n in range(4):
                        take(C_BR + n)
                        if n:
                            pe.wait_ge(ot_ok, 2 * n)
                        for m in range(4):
                            i = 4 * n + m
                            if i == 0:
                                pe.wait_ge(pt_a, 6)
                                pe.wait_ge(pt_v, 6)
                                pe.wait_ge(yt_out, 2)
                            if i >= 4:
                                pe.wait_ge(pr_free, i - 3)
                            mm = feature_unit(ps[:, 4 + i % 4, :], C_BR + n, m * SEQ, 2, ys[:, n, :, :])
                            mm.then_inc(pr_ps, 1)
                    pe.wait_ge(mg_ok, 12)
                    for c in range(2):
                        take(C_OUT + c)
                        for t in range(NT):
                            token_unit(bank(U_OUT + 2 * c + t), C_OUT + c, 0, 512, t, merged).then_inc(full, 1)
                    transposed(U_X2, 2)
                    pe.wait_ge(free, U_X2 + 4)
                    pe.wait_ge(pr_free, 16)
                    for c in range(HID1 // 256):
                        take(C_FIN + c)
                        if c >= 2:
                            pe.wait_ge(fg_free, c - 1)
                        feature_unit(ps[:, 2 + c % 2, :], C_FIN + c, 0, 2, hT).then_inc(fg_ps, 1)
                        if c >= 2:
                            pe.wait_ge(fu_free, c - 1)
                        feature_unit(ps[:, 4 + c % 2, :], C_FIN + c, 256, 2, hT).then_inc(fu_ps, 1)
                    pe.wait_ge(fu_free, HID1 // 256)
                    for c, (r, k) in enumerate(DOWN):
                        take(C_FOUT + c)
                        for kk in range(k):
                            for t in range(NT):
                                for half in range(2):
                                    b = (0, 1, 6, 7)[2 * t + half]
                                    mm = nc.tensor.matmul(ps[:, b, :], hid[:, r + kk, t * P:(t + 1) * P],
                                                          chunk(C_FOUT + c)[:, kk, half * 512:(half + 1) * 512],
                                                          start=r + kk == 0, stop=r + kk == KH1 - 1)
                                    if r + kk == KH1 - 1:
                                        mm.then_inc(dn_ps, 1)
                        if c < len(DOWN) - 1:
                            mm.then_inc(down_used, 1)

                @block.scalar
                def _(act):
                    marks = {}

                    def mark(s, ins):
                        marks[s.name] = marks.get(s.name, 0) + 1
                        ins.then_inc(s, 1)
                        act.wait_ge(s, marks[s.name])

                    def empty(u):
                        act.wait_ge(full, u + 1)
                        return ps[:, u % 2, :]

                    def squares(e):
                        for t in range(NT):
                            src = x if e in (0, 3) else xm
                            i = nc.scalar.activation(hT[:, 4 * t:4 * t + 4, :].rearrange("p a b -> p (a b)"),
                                                     src[:, t, :], ACT.Square, accum_out=ssq[:, e, t:t + 1])
                        mark(ssq_ok, i)

                    def turned(u0, gain):
                        for k in range(KD):
                            b = empty(u0 + k // 2)
                            i = nc.scalar.activation(hT[:, k, :], b[:, (k % 2) * SEQ:(k % 2 + 1) * SEQ], ACT.Copy,
                                                     scale=parT[:, gain + k:gain + k + 1])
                            if k % 2:
                                mark(free, i)

                    def in_chunk(i):
                        for n, (kind, c, size, name, at) in enumerate(in_units[i]):
                            b = empty(U_IN[i] + n)
                            dst = bufs[name]
                            if kind in "FI":
                                ins = nc.scalar.activation(dst[:, at:at + size, :], b[:, 0:size * SEQ].rearrange(
                                    "p (a b) -> p a b", a=size), ACT.Copy, scale=QSCALE.get(name, 1.0))
                            elif kind == "T":
                                ins = nc.scalar.copy(dst[:, at, :], b[:, 0:size])
                            else:
                                ins = nc.scalar.copy(dst, b[:, 0:NT * size].rearrange("p (t c) -> p t c", t=NT))
                            mark(free, ins)

                    def gate_unit(g):
                        b = empty(U_GATE + g)
                        for j in range(2):
                            k = 2 * g + j
                            i = nc.scalar.activation(gates[:, k, :], b[:, j * SEQ:(j + 1) * SEQ], ACT.Identity,
                                                     bias=parT[:, PBG + k:PBG + k + 1])
                        mark(free, i)

                    def exps(n):
                        w = P * (n % 2 + 1)
                        act.wait_ge(mx_ok, n + 1)
                        if n >= 1:
                            act.wait_ge(pt_ps, n)
                        if n >= 2:
                            act.wait_ge(o_ok, n - 1)
                        for s in range(8):
                            i = nc.scalar.activation(probs[:, s, 0:w], L[:, s, 0:w], ACT.Exp,
                                                     bias=nmx[:, n % 2, s:s + 1], accum_out=rsum[:, n % 2, s:s + 1])
                        mark(ex_ok, i)

                    def p_out(n):
                        w = P * (n % 2 + 1)
                        act.wait_ge(pt_ps, n + 1)
                        if n >= 1:
                            act.wait_ge(o_ps, n)
                        mark(pt_a, nc.scalar.copy(pT[:, 0:4, 0:w], L[:, 0:4, 0:w]))

                    def o_out(n):
                        act.wait_ge(ot_ps, n + 1)
                        t = n % 2
                        mark(ot_ok, nc.scalar.copy(ys[:, ATT[n // 2][3], :, t * P:(t + 1) * P],
                                       ps[:, 3, :].rearrange("p (b c) -> p b c", b=4)))

                    def relus(t):
                        act.wait_ge(ix_ps, t + 1)
                        act.wait_ge(o_ps, 4 + t)
                        w = P * (t + 1)
                        for h in range(4):
                            i = nc.scalar.activation(rl[:, h, 0:w], L[:, 4 * (h % 2) + h // 2, 0:w], ACT.Relu,
                                                     scale=64 ** -0.5)
                        mark(ix_rl, i)

                    squares(0)
                    act.wait_ge(par_ok, 1)
                    turned(0, PGM)
                    act.wait_ge(init_ok, 1)
                    for i in range(3):
                        in_chunk(i)
                    act.wait_ge(spv, 1)
                    mark(spe, nc.scalar.activation(sp[:, 2, :], sp[:, 1, :], ACT.Exp, scale=-1.0))
                    act.wait_ge(small_in, 64)
                    mark(spe, nc.scalar.activation(asg[:, 0:8], small[:, 1, :], ACT.Exp))
                    act.wait_ge(spv, 2)
                    mark(spe, nc.scalar.activation(sp[:, 4, :], sp[:, 3, :], ACT.Ln))
                    in_chunk(3)
                    act.wait_ge(conv_ok, 1)
                    mark(silu_ok, nc.scalar.activation(xbc[:, :, :], xbc[:, :, :], ACT.Silu))
                    for i in range(4, N_IN):
                        in_chunk(i)
                    mark(zs_ok, nc.scalar.activation(bufs["z"][:, :, :], bufs["z"][:, :, :], ACT.Silu))
                    gate_unit(0)
                    act.wait_ge(cb_ps, 1)
                    mark(cb_ok, nc.scalar.copy(cb[:, :, :], ps[:, 2:4, 0:384]))
                    gate_unit(1)
                    act.wait_ge(rope_ok, 5)
                    for r in range(2):
                        act.wait_ge(dec_ps, r + 1)
                        for j in range(4):
                            h = 4 * r + j
                            nc.scalar.activation(sc8[:, h, 0:SEQ], ps[:, 4 + j, 0:SEQ], ACT.Exp,
                                                 bias=ncum[:, 0, h:h + 1])
                            i = nc.scalar.activation(sc8[:, h, SEQ:384], ps[:, 4 + j, SEQ:384], ACT.Exp,
                                                     bias=ncum[:, 1, h:h + 1])
                        mark(dec_ok, i)
                        gate_unit(2 + r)
                    gate_unit(4)
                    for t in range(NT):
                        act.wait_ge(yt_ps, t + 1)
                        for b in range(4):
                            i = nc.scalar.activation(ys[:, 0, b, t * P:(t + 1) * P], ps[:, 3, b * P:(b + 1) * P],
                                                     ACT.Copy, scale=parT[:, PSN + b:PSN + b + 1])
                        mark(yt_out, i)
                    act_g = [5]

                    def gate():
                        if act_g[0] < 16:
                            gate_unit(act_g[0])
                            act_g[0] += 1
                    exps(0)
                    p_out(0)
                    for n in range(6):
                        gate()
                        if n + 1 < 6:
                            if n + 1 >= 4:
                                relus(n - 3)
                                gate()
                            gate()
                            exps(n + 1)
                        o_out(n)
                        if n + 1 < 6:
                            p_out(n + 1)
                    while act_g[0] < 16:
                        gate()
                    for g in range(4):
                        i = nc.scalar.activation(gates[:, 8 * g:8 * g + 8, :], gates[:, 8 * g:8 * g + 8, :],
                                                 ACT.Sigmoid)
                        mark(sig_ok, i)
                    for c in range(2):
                        for t in range(NT):
                            i = nc.scalar.copy(xm[:, t, c * 512:(c + 1) * 512], empty(U_OUT + 2 * c + t))
                            mark(free, i)
                    act.wait_ge(free, U_OUT + 4)
                    squares(2)
                    act.wait_ge(x_ok, 1)
                    squares(3)
                    turned(U_X2, PGF)
                    for c in range(HID1 // 256):
                        act.wait_ge(fg_ps, c + 1)
                        if c >= 2:
                            act.wait_ge(fu_free, c - 1)
                        mark(fg_free, nc.scalar.activation(ffg[:, c % 2, :], ps[:, 2 + c % 2, :], ACT.Silu))
                    for t in range(NT):
                        for half in range(2):
                            act.wait_ge(dn_ps, 2 * t + half + 1)
                            mark(dn_ok, nc.scalar.copy(xm[:, t, half * 512:(half + 1) * 512],
                                           ps[:, (0, 1, 6, 7)[2 * t + half], :]))
                    act.wait_ge(dn_ok, 4)
                    squares(4)

                @block.vector
                def _(dve):
                    n_chain = [0]

                    def link(ins):
                        n_chain[0] += 1
                        ins.then_inc(dch, 1)
                        dve.wait_ge(dch, n_chain[0])

                    V = nc.vector
                    marks = {}

                    def mark(s, ins):
                        marks[s.name] = marks.get(s.name, 0) + 1
                        ins.then_inc(s, 1)
                        dve.wait_ge(s, marks[s.name])

                    def mean_square(e, n, width):
                        mark(msq_ok, V.tensor_scalar(msq[:, e, 0:n], ssq[:, e, 0:n], 1.0 / width, EPS, ALU.mult, ALU.add
                                        ))

                    def norm_in(e):
                        dve.wait_ge(ssq_ok, max(e, 1))
                        mean_square(e, 2, D)
                        dve.wait_ge(rstd_ok, e + 1)
                        for t in range(NT):
                            i = V.tensor_scalar(xm[:, t, :], x[:, t, :], rstd[:, e, t:t + 1], None, ALU.mult)
                        mark(xn_ok, i)

                    def norm_out(e, gain):
                        dve.wait_ge(ssq_ok, max(e, 1))
                        mean_square(e, 2, D)
                        dve.wait_ge(rstd_ok, e + 1)
                        for t in range(NT):
                            link(V.scalar_tensor_tensor(xm[:, t, :], xm[:, t, :], rstd[:, e, t:t + 1], gain,
                                                        ALU.mult, ALU.mult))
                        for t in range(NT):
                            i = V.tensor_tensor(x[:, t, :], x[:, t, :], xm[:, t, :], ALU.add)
                        mark(x_ok, i)

                    def rope(r):
                        name = ROPES[r]
                        nb = 3 if name == "iqk" else 4
                        t = bufs[name]
                        dve.wait_ge(rope_ps, r + 1)
                        turn = ps[:, 4 + 2 * (r % 2):6 + 2 * (r % 2), :].rearrange("p b (c d) -> p (b c) d", c=2)
                        link(V.tensor_tensor(rt[:, 0:nb, :], turn[:, 0:nb, :],
                                             sin.unsqueeze(1).broadcast_to([P, nb, SEQ]), ALU.mult))
                        link(V.tensor_tensor(rt[:, 4:4 + nb, :], t[:, :, :],
                                             cos.unsqueeze(1).broadcast_to([P, nb, SEQ]), ALU.mult))
                        mark(rope_ok, V.tensor_tensor(t[:, :, :], rt[:, 0:nb, :], rt[:, 4:4 + nb, :], ALU.add))

                    link(V.memset(nhalf[:, :], -0.5))
                    link(V.memset(xbcp[:, :, 0:3], 0.0))
                    link(V.tensor_scalar(nident[:, :], ident[0:16, 0:16], -1.0, None, ALU.mult))
                    mark(init_ok, V.memset(asg[:, 8:16], -1.0))
                    dve.wait_ge(par_ps, 1)
                    mark(par_ok, V.tensor_copy(parT[:, :], ps[:, 2, 0:NPAR1]))
                    norm_in(0)
                    dve.wait_ge(init_ok, 1)
                    dve.wait_ge(par_ok, 1)
                    for i in range(2):
                        dve.wait_ge(free, U_IN[i] + 2)
                        for b in range(4 * i, 4 * i + 4):
                            link(V.tensor_scalar(xbc[:, b, :], xbcp[:, b, 0:SEQ], parT[:, PCW + b:PCW + b + 1],
                                                 parT[:, PCB + b:PCB + b + 1], ALU.mult, ALU.add))
                            for j in range(1, 4):
                                ins = V.scalar_tensor_tensor(xbc[:, b, :], xbcp[:, b, j:j + SEQ],
                                                             parT[:, PCW + 8 * j + b:PCW + 8 * j + b + 1],
                                                             xbc[:, b, :], ALU.mult, ALU.add)
                                if b == 7 and j == 3:
                                    mark(conv_ok, ins)
                                else:
                                    link(ins)
                    dve.wait_ge(free, U_IN[3])
                    dve.wait_ge(small_in, 64)
                    v3 = sp[:, 0, :].rearrange("p (t c) -> p t c", t=NT)
                    link(V.tensor_tensor(v3[:, :, 0:8], dtff[:, :, 0:8],
                                         small[:, 0:1, :].broadcast_to([P, NT, 8]), ALU.add))
                    link(V.tensor_tensor(v3[:, :, 8:16], dtff[:, :, 8:16],
                                         small[:, 3:4, :].broadcast_to([P, NT, 8]), ALU.add))
                    link(V.tensor_scalar(v3[:, :, 8:16], v3[:, :, 8:16], -1.0, None, ALU.mult))
                    mark(spv, V.scalar_tensor_tensor(sp[:, 1, :], sp[:, 0, :], -1.0, sp[:, 0, :], ALU.mult, ALU.max))
                    dve.wait_ge(spe, 1)
                    mark(spv, V.tensor_scalar(sp[:, 3, :], sp[:, 2, :], 1.0, None, ALU.add))
                    dve.wait_ge(spv, 2)
                    dve.wait_ge(spe, 3)
                    link(V.tensor_scalar(sp[:, 1, :], sp[:, 3, :], -1.0, None, ALU.add))
                    link(V.tensor_tensor(sp[:, 1, :], sp[:, 2, :], sp[:, 1, :], ALU.subtract))
                    link(V.reciprocal(sp[:, 5, :], sp[:, 3, :]))
                    link(V.tensor_tensor(sp[:, 1, :], sp[:, 1, :], sp[:, 5, :], ALU.mult))
                    link(V.tensor_tensor(sp[:, 4, :], sp[:, 4, :], sp[:, 1, :], ALU.add))
                    link(V.scalar_tensor_tensor(sp[:, 5, :], sp[:, 0, :], 0.0, sp[:, 4, :], ALU.max, ALU.add))
                    link(V.tensor_scalar(asg[:, 0:8], asg[:, 0:8], -1.0, None, ALU.mult))
                    spt = sp[:, 5, :].rearrange("p (t c) -> p t c", t=NT)
                    mark(lcat_ok, V.tensor_tensor(lcat[:, :, :], spt, asg[:, :].unsqueeze(1).broadcast_to([P, NT, 16]), ALU.mult
                                    ))
                    for r in range(5):
                        rope(r)
                    dve.wait_ge(cum_ps, 1)
                    link(V.tensor_copy(cumT[:, :], ps[0:16, 2, 0:SEQ]))
                    mark(cum_ok, V.tensor_scalar(ncum[:, :, :], ps[:, 3, 0:32].rearrange("p (t c) -> p t c", t=NT), -1.0, None,
                                    ALU.mult))
                    dve.wait_ge(xs_ps, 1)
                    xs = ps[:, 4:6, :].rearrange("p t (h c) -> p t h c", h=8)
                    xdt = xd[:, 0, :, :].rearrange("p t (h c) -> p t h c", h=8)
                    xsk = xd[:, 1, :, :].rearrange("p t (h c) -> p t h c", h=8)
                    for t in range(NT):
                        link(V.tensor_tensor(xdt[:, t], xs[:, t],
                                             spt[:, t, 0:8].unsqueeze(2).broadcast_to([P, 8, 64]), ALU.mult))
                        i = V.tensor_tensor(xsk[:, t], xs[:, t],
                                            small[:, 2, :].unsqueeze(2).broadcast_to([P, 8, 64]), ALU.mult)
                        if t == 0:
                            link(i)
                    mark(xs_ok, i)
                    dve.wait_ge(cb_ok, 1)
                    for r in range(2):
                        dve.wait_ge(dec_ok, r + 1)
                        mark(sc_ok, V.tensor_tensor(sc8[:, 4 * r:4 * r + 4, :], sc8[:, 4 * r:4 * r + 4, :],
                                        cb[:, r:r + 1, :].broadcast_to([P, 4, 384]), ALU.mult))
                    dve.wait_ge(y_ps, 1)
                    dve.wait_ge(xs_ok, 1)
                    mark(y_free, V.tensor_tensor(y[:, :, :], ps[:, 2:4, :], xd[:, 1, :, :], ALU.add))
                    dve.wait_ge(y_free, 1)
                    dve.wait_ge(zs_ok, 1)
                    link(V.tensor_tensor(y[:, :, :], y[:, :, :], bufs["z"][:, :, :], ALU.mult))
                    link(V.tensor_tensor(xd[:, 1, :, :], y[:, :, :], y[:, :, :], ALU.mult))
                    link(V.tensor_reduce(ssq[:, 1, :], xd[:, 1, :, :].rearrange("p t (g c) -> p (t g) c", g=2), AX_X,
                                         ALU.add))
                    mean_square(1, 4, 256)
                    dve.wait_ge(rstd_ok, 2)
                    mark(yt_ok, V.tensor_tensor(y[:, :, :].rearrange("p t (g c) -> p (t g) c", g=2),
                                    y[:, :, :].rearrange("p t (g c) -> p (t g) c", g=2),
                                    rstd[:, 1, :].unsqueeze(2).broadcast_to([P, 4, 256]), ALU.mult))

                    def maxima(n):
                        w = P * (n % 2 + 1)
                        dve.wait_ge(qk_ps, n + 1)
                        if n >= 2:
                            dve.wait_ge(ex_ok, n - 1)
                        mark(mx_ok, V.tensor_reduce(nmx[:, n % 2, :], L[:, :, 0:w], AX_X, ALU.max, negate=True))

                    def p_out(n):
                        w = P * (n % 2 + 1)
                        dve.wait_ge(pt_ps, n + 1)
                        if n >= 1:
                            dve.wait_ge(o_ps, n)
                        mark(pt_v, V.tensor_copy(pT[:, 4:8, 0:w], L[:, 4:8, 0:w]))

                    def o_norm(n):
                        dve.wait_ge(ex_ok, n + 1)
                        link(V.reciprocal(rinv[:, :], rsum[:, n % 2, :]))
                        dve.wait_ge(o_ps, n + 1)
                        if n >= 2:
                            dve.wait_ge(ot_ps, n - 1)
                        else:
                            dve.wait_ge(yt_ps, 2)
                        mark(o_ok, V.tensor_tensor(o[:, n % 2, :].rearrange("p (b a c) -> p b a c", a=2, c=64),
                                        ps[:, 2, :].rearrange("p (b a c) -> p b a c", a=2, c=64),
                                        rinv[:, :].rearrange("p (a b) -> p b a", a=2).unsqueeze(3)
                                        .broadcast_to([P, 4, 2, 64]), ALU.mult))

                    def pick(t):
                        w = P * (t + 1)
                        dve.wait_ge(ix_rl, t + 1)
                        if t == 0:
                            link(V.tensor_scalar(iw[:, :, :], iw[:, :, :], 0.5, None, ALU.mult))
                        link(V.tensor_scalar(isc[:, 0:w], rl[:, 0, 0:w], iw[:, t, 0:1], None, ALU.mult))
                        for h in range(1, 4):
                            link(V.scalar_tensor_tensor(isc[:, 0:w], rl[:, h, 0:w], iw[:, t, h:h + 1], isc[:, 0:w],
                                                        ALU.mult, ALU.add))
                        link(V.tensor_tensor(isc[:, w - P:w], isc[:, w - P:w], maskQ, ALU.add))
                        for r in range(8):
                            link(V.max(top8[:, :], isc[:, 0:w]))
                            link(V.match_replace(isc[:, 0:w], top8[:, :], isc[:, 0:w], TAKEN))
                        if t:
                            dve.wait_ge(qk_ps, 5)
                        mark(pen_ok, V.tensor_scalar(pen[:, 0:w], isc[:, 0:w], -2e38, NEG, ALU.is_gt, ALU.mult))

                    maxima(0)
                    p_out(0)
                    for n in range(6):
                        if n + 1 < 6:
                            if n + 1 >= 4:
                                pick(n - 3)
                            if n + 1 < 4:
                                maxima(n + 1)
                        o_norm(n)
                        if n + 1 >= 4 and n + 1 < 6:
                            maxima(n + 1)
                        if n + 1 < 6:
                            p_out(n + 1)
                    for n in range(4):
                        dve.wait_ge(sig_ok, n + 1)
                        for m in range(4):
                            i = 4 * n + m
                            dve.wait_ge(pr_ps, i + 1)
                            src = ps[:, 4 + i % 4, :].rearrange("p (b c) -> p b c", b=2)
                            gt = gates[:, 8 * n + 2 * m:8 * n + 2 * m + 2, :]
                            out, tmp = (z[:, 2 * m:2 * m + 2, :] for z in (merged, probs))
                            if n == 0:
                                mark(pr_free, V.tensor_tensor(out, src, gt, ALU.mult))
                                continue
                            if n > 1:
                                dve.wait_ge(mg_ok, i - 7)
                            mark(pr_free, V.tensor_tensor(tmp, src, gt, ALU.mult))
                            dve.wait_ge(pr_free, i + 1)
                            mark(mg_ok, V.tensor_tensor(out, out, tmp, ALU.add))
                    dve.wait_ge(gpost_in, 32)
                    norm_out(2, gpost[:, 0, :])
                    dve.wait_ge(x_ok, 1)
                    norm_in(3)
                    for c in range(HID1 // 256):
                        dve.wait_ge(fg_free, c + 1)
                        dve.wait_ge(fu_ps, c + 1)
                        mark(fu_free, V.tensor_tensor(hid[:, 2 * c:2 * c + 2, :],
                                        ffg[:, c % 2, :].rearrange("p (b c) -> p b c", b=2),
                                        ps[:, 4 + c % 2, :].rearrange("p (b c) -> p b c", b=2), ALU.mult
                                        ))
                    norm_out(4, gpost[:, 1, :])

                @block.gpsimd
                def _(pool):
                    pool.wait_ge(init_ok, 1)
                    for e in range(5):
                        n = 4 if e == 1 else 2
                        pool.wait_ge(msq_ok, e + 1)
                        nc.gpsimd.tensor_tensor(rstd[:, e, 0:n], msq[:, e, 0:n], nhalf[:, 0:n], ALU.pow
                                                ).then_inc(rstd_ok, 1)

            nc.all_engine_barrier()
            for s in sems:
                nc.gpsimd.sem_clear(s)
            nc.all_engine_barrier()


W2 = 256
HID2 = 4096
KH2 = HID2 // P
MLA_D, MLA_NOPE = 96, 64
IN2 = [
    (0, 416, [("T", 0, 256, "cq"), ("T", 256, 128, "ckv"), ("G", 384, 32, "kpe", 64)]),
    (1712, 512, [("F", 0, 2, "dn", 0), ("F", 256, 2, "dn", 2)]),
    (2224, 520, [("F", 0, 2, "dn", 4), ("T", 256, 8, "dab"), ("T", 264, 256, "dz")]),
    (928, 256, [("F", 0, 1, "gqk", 0), ("F", 128, 1, "gqk", 1)]),
    (1184, 528, [("T", 0, 256, "gv"), ("G", 256, 16, "glr", 0), ("T", 272, 256, "gog")]),
    (416, 512, [("T", 0, 512, "uv")]),
]
GATE2 = 2744
QM, QX, QE, QL, QQ, QK, QS, QC, NPAR2 = 0, 8, 16, 24, 32, 34, 35, 39, 63
TWO_PI = 2 * np.pi
PI_A = 6.28125
PI_B = float(np.float32(np.float16(TWO_PI - PI_A)))
PI_C = float(np.float32(TWO_PI - PI_A - PI_B))
ROUND = 1.5 * 2.0 ** 23
SUBL = (64, 32, 16, 8, 4, 2, 1)


def second_block(nc, ps, x, con, bfc, a):
    with ExitStack() as ctx:
        def sb(name, shape, dt=F32):
            return ctx.enter_context(nc.sbuf_tensor("b_" + name, shape, dt))

        def sem(name):
            s = ctx.enter_context(nc.semaphore("b_" + name))
            sems.append(s)
            return s

        def flat(t):
            return t.rearrange("p a b -> p (a b)")

        sems = []
        ident = con[:, C_ID:C_ID + P]
        ident_bf, maskT_bf, maskQ_bf = (bfc[:, i, :] for i in range(3))
        tri = con[:, C_U:C_U + NT * SEQ].rearrange("p (t l) -> p t l", t=NT)
        upper = con[:, C_U:C_U + P]
        ones = column(con[:, C_U + P - 1:C_U + P], P)

        con2 = sb("con2", [P, N_CONST2])
        lmask = con2[:, C2_LV:C2_LV + 8 * P].rearrange("p (n i) -> p n i", n=8)
        half_turn = con2[64:96, C2_R2:C2_R2 + 32]
        same_head = con2[:, C2_B64:C2_B64 + P]
        ring = sb("ring", [P, RING, SLOT])
        hT = sb("hT", [P, KD, SEQ])
        xm = sb("xm", [P, NT, D])
        par = sb("par", [NPAR2, P])
        parT = sb("parT", [P, NPAR2])
        small = sb("small", [P, 2, 4])
        hgain = sb("hgain", [P, 2, 64])
        lnp = sb("lnp", [P, 2, W2])
        nhalf = sb("nhalf", [P, 8])
        probs = sb("probs", [P, 8, SEQ])
        memT = probs
        oT = probs
        l2s = probs[:, 0:4, :]
        l2r = probs[:, 4:8, :]
        pT = sb("pT", [P, 8, SEQ])
        merged = pT
        spb = flat(pT[:, :, :])[:, 0:5 * 264].rearrange("p (a b) -> p a b", a=5)
        big = sb("big", [P, 3, KD * SEQ])
        ed, qe, ke = (big[:, i, :].rearrange("p (a b) -> p a b", a=8) for i in range(3))
        xq, xk = (big[:, i, :].rearrange("p (a b) -> p a b", a=8) for i in range(2))
        xv = big[:, 2, :].rearrange("p (t c) -> p t c", t=NT)
        bigs = big[:, :, :].rearrange("p a (b c) -> p (a b) c", b=2)
        decT, LT, LTm, X, XT, Y = (bigs[:, i, :].rearrange("p (s i) -> p s i", s=8) for i in range(6))
        gates = sb("gates", [P, 32, SEQ])
        hid = gates
        ys = sb("ys", [P, 4, 2, SEQ])
        early = flat(big[:, :, :])
        cq, ckv = (early[:, c:c + n].rearrange("p (t c) -> p t c", t=NT) for c, n in ((0, 512), (512, 256)))
        cT = early[:, 768:1536].rearrange("p (a b) -> p a b", a=3)
        mv = early[:, 1536:2048].rearrange("p (t c) -> p t c", t=NT)
        qT = early[0:MLA_D, 2048:3328].rearrange("p (a b) -> p a b", a=5)
        kT = early[0:MLA_D, 3328:4352].rearrange("p (a b) -> p a b", a=4)
        wuq, wukv = sb("wuq", [P, 2, 384]), sb("wukv", [P, 4, P])
        pos = sb("pos", [MLA_D, SEQ], I32)
        trig = sb("trig", [MLA_D, 2, SEQ])
        tmp96 = lnp
        uv = sb("uv", [P, NT, 512])
        sgw = sb("sgw", [P, 4, P])
        wsT = sb("wsT", [P, 4, P])
        gqk = sb("gqk", [P, 2, SEQ])
        gv, gog, dz = (sb(n, [P, NT, W2]) for n in ("gv", "gog", "dz"))
        glr = sb("glr", [16, SEQ])
        wg, bg = sb("wg", [16, P]), sb("bg", [1, P])
        dab = sb("dab", [P, NT, 8])
        lcat = sb("lcat", [P, NT, 132])
        asc = sb("asc", [P, 4])
        gcum = sb("gcum", [P, SEQ])
        SaT = sb("SaT", [P, 4, NT, P])
        attnT = SaT[:, :, :, :].rearrange("p h t i -> p (h t) i")
        S01 = sb("S01", [P, 4, P])
        dnp = sb("dnp", [P, 6, SEQ + 4])
        dnc = sb("dnc", [P, 6, SEQ])
        gam = sb("gam", [P, 3, 4])
        ngam = sb("ngam", [P, NT, 4])
        egam = sb("egam", [P, 3, 4])
        beta = sb("beta", [P, NT, 4])
        dnb = flat(dnp[:, :, :])
        rv = dnb[:, 0:512].rearrange("p (t c) -> p t c", t=NT)
        kd = dnb[:, 512:768]
        u = dnb[:, 768:1280].rearrange("p (t c) -> p t c", t=NT)
        ssb = dnb[:, 1280:1408]
        ob = sb("ob", [P, NT, W2])
        tq = sb("tq", [P, NT, W2])
        nmx, rsum, rinv = sb("nmx", [P, 8]), sb("rsum", [P, 8]), sb("rinv", [P, 8])
        ssq, msq, rstd = (sb(n, [P, 8, 8]) for n in ("ssq", "msq", "rstd"))
        mean = sb("mean", [P, NT])
        bufs = dict(cq=cq[:, :, :], ckv=ckv[:, :, :], dn=dnp[:, :, 3:SEQ + 3], dab=dab[:, :, :], dz=dz[:, :, :],
                    gqk=gqk[:, :, :], gv=gv[:, :, :], gog=gog[:, :, :], uv=uv, kpe=qT[64:96, 4, :],
                    glr=glr[:, :])

        par_in, small_in, w_in_ = sem("par_in"), sem("small_in"), sem("w_small")
        mem_in = sem("mem_in")
        landed = [sem(f"landed{i}") for i in range(RING)]
        down_used = sem("down_used")
        full, free = sem("full"), sem("free")
        par_ps, par_ok, init_ok = sem("par_ps"), sem("par_ok"), sem("init_ok")
        ssq_ok, msq_ok, rstd_ok, xn_ok = sem("ssq_ok"), sem("msq_ok"), sem("rstd_ok"), sem("xn_ok")
        cn_ok, ct_ps, ct_ok = sem("cn_ok"), sem("ct_ps"), sem("ct_ok")
        mq_ps, mq_ok, rope_ps, rope_ok = sem("mq_ps"), sem("mq_ok"), sem("rope_ps"), sem("rope_ok")
        qk_ps, mx_ok, ex_ok, pn_ok = sem("qk_ps"), sem("mx_ok"), sem("ex_ok"), sem("pn_ok")
        pt_ps, pt_a, pt_v, o_ps, xo_ok = sem("pt_ps"), sem("pt_a"), sem("pt_v"), sem("o_ps"), sem("xo_ok")
        bt_in, bt_ps, bt_ok = sem("bt_in"), sem("bt_ps"), sem("bt_ok")
        conv_ok, silu_ok, l2_sq = sem("conv_ok"), sem("silu_ok"), sem("l2_sq")
        pre_ps, spv, spe, lc_ok = sem("pre_ps"), sem("spv"), sem("spe"), sem("lc_ok")
        ln_ok, mix_ps = sem("ln_ok"), sem("mix_ps")
        cum_ps, cum_ok, df_ok, le_ok, lev_ok = (sem(n) for n in ("cum_ps", "cum_ok", "df_ok", "le_ok", "lev_ok"))
        l2_ps, l2_in, l2_rt, l2_ok = sem("l2_ps"), sem("l2_in"), sem("l2_rt"), sem("l2_ok")
        sa_ps, sa_ok, go_ps, gn_ok, sil_ok = (sem(n) for n in ("sa_ps", "sa_ok", "go_ps", "gn_ok", "sil_ok"))
        tk_ps, tk_ok, row_ps, dec_ok, lt_ok = (sem(n) for n in ("tk_ps", "tk_ok", "row_ps", "dec_ok", "lt_ok"))
        kk_ps, at_ok, eg_in, eg_ok = sem("kk_ps"), sem("at_ok"), sem("eg_in"), sem("eg_ok")
        lm_ok, yy_ps, yy_ok, zz_ps, xx_ok = (sem(n) for n in ("lm_ok", "yy_ps", "yy_ok", "zz_ps", "xx_ok"))
        u_ps, u_ok, st_ps, st_ok, ks_ps, r1_ok, do_ps = (
            sem(n) for n in ("u_ps", "u_ok", "st_ps", "st_ok", "ks_ps", "r1_ok", "do_ps"))
        sig_ok, pr_ps, pr_free, mg_ok = sem("sig_ok"), sem("pr_ps"), sem("pr_free"), sem("mg_ok")
        res_ps, res_ok, rl_ok, hs_ok = sem("res_ps"), sem("res_ok"), sem("rl_ok"), sem("hs_ok")
        dch, con_in, fin_in, y_ok = sem("dch"), sem("con_in"), sem("fin_in"), sem("y_ok")

        def cols(src, l, c, n):
            return src[bass.ds(l, 1), :, c:c + n].rearrange("a (k p) c -> p (a k) c", p=P)

        def wide(name, n):
            return [(8, 512, [lambda l, c=c: (0, cols(a[name], l, 512 * c, 512))]) for c in range(n)]

        chunks = [(8, n, [lambda l, c=c, n=n: (0, cols(a["w_in_2"], l, c, n))]) for c, n, _ in IN2]
        N_IN = len(IN2)
        chunks += [(8, 512, [lambda l, c=c: (0, cols(a["w_in_2"], l, GATE2 + 512 * c, 512))]) for c in range(8)]
        chunks += wide("xattn_wk_2", 2) + wide("xattn_wv_2", 2)
        chunks += [(4, D, [lambda l, c=c: (0, a["w_branch_2"][bass.ds(l, 1), 2 * c:2 * c + 2].rearrange(
            "a n (k p) c -> p (a n k) c", p=P))]) for c in range(2)]
        chunks += wide("w_out_2", 2) + wide("xattn_wq_2", 2) + wide("xattn_wo_2", 2) + wide("w_up_2", 8)
        chunks += [(4, D, [lambda l, c=c: (0, a["w_down_2"][bass.ds(l, 1), c * 512:(c + 1) * 512, :].rearrange(
            "a (k p) c -> p (a k) c", p=P))]) for c in range(8)]
        W = Weights(chunks)
        C_GATE = N_IN
        C_WK, C_WV, C_BR, C_OUT = C_GATE + 8, C_GATE + 10, C_GATE + 12, C_GATE + 14
        C_WQ, C_WO, C_UP, C_DN = C_OUT + 2, C_OUT + 4, C_OUT + 6, C_OUT + 14

        def chunk(w):
            k, c, _ = chunks[w]
            return ring[:, w % RING, 0:k * c].rearrange("p (k c) -> p k c", c=c)

        in_units = []
        for _, _, pieces in IN2:
            out = []
            for p in pieces:
                out += [("G", p[1], p[2], p[3], p[4])] if p[0] == "G" else units_of([p])
            in_units.append(out)
        U_IN = [4 + sum(len(v) for v in in_units[:i]) for i in range(N_IN + 1)]
        U_GATE = U_IN[-1]
        U_MEM = U_GATE + 16
        U_WK = U_MEM + 4
        U_WV = U_WK + 4
        U_X6 = U_WV + 4
        U_WQ = U_X6 + 4
        U_X7 = U_WQ + 4
        U_UP = U_X7 + 4
        read = [(full, U_IN[i + 1]) for i in range(N_IN)]
        read += [(full, U_GATE + 2 * c + 2) for c in range(8)]
        read += [(full, U_WK + 2 * c + 2) for c in range(4)]
        read += [(pr_ps, 8 * c + 8) for c in range(2)]
        read += [(res_ps, 2 * c + 2) for c in range(2)]
        read += [(full, U_WQ + 2 * c + 2) for c in range(2)]
        read += [(res_ps, 4 + 2 * c + 2) for c in range(2)]
        read += [(full, U_UP + 2 * c + 2) for c in range(8)]
        read += [(down_used, c + 1) for c in range(7)]
        L = ps[:, 4:8, :].rearrange("p b (s w) -> p (b s) w", s=2)

        def system(t, h):
            return (h % 2) * 4 + t * 2 + h // 2

        with nc.Block() as block:

            @block.sync
            def _(sp_):
                sp_.dma_start(con2[:, :], a["constants_2"]).then_inc(con_in, 16)
                sp_.dma_start(pos[64:96, :], a["positions_2"].broadcast_to([32, SEQ])).then_inc(con_in, 16)

            @block.vector
            def _(dve):
                V = nc.vector
                n_chain = [0]

                def link(ins):
                    n_chain[0] += 1
                    ins.then_inc(dch, 1)
                    dve.wait_ge(dch, n_chain[0])

                ang, k = tmp96[64:96, 0, :], tmp96[64:96, 1, :]
                dve.wait_ge(con_in, 32)
                link(V.memset(nhalf[:, :], -0.5))
                link(V.tensor_copy(ang, pos[64:96, :]))
                link(V.tensor_scalar(ang, ang, con2[64:96, C2_INV:C2_INV + 1], None, ALU.mult))
                link(V.tensor_scalar(k, ang, 1.0 / TWO_PI, ROUND, ALU.mult, ALU.add))
                link(V.tensor_scalar(k, k, -ROUND, None, ALU.add))
                for part in (PI_A, PI_B, PI_C):
                    link(V.scalar_tensor_tensor(ang, k, -part, ang, ALU.mult, ALU.add))
                link(V.tensor_scalar(ang, ang, 3.141592, -3.141592, ALU.min, ALU.max))
                link(V.scalar_tensor_tensor(k, ang, -1.0, ang, ALU.mult, ALU.max))
                V.tensor_scalar(k, k, -1.0, float(np.pi / 2), ALU.mult, ALU.add).then_inc(con_in, 1)

            @block.scalar
            def _(act):
                act.wait_ge(con_in, 33)
                nc.scalar.activation(trig[64:96, 0, :], tmp96[64:96, 1, :], ACT.Sin).then_inc(y_ok, 1)
                nc.scalar.activation(trig[64:96, 1, :], tmp96[64:96, 0, :], ACT.Sin).then_inc(y_ok, 1)
                act.wait_ge(y_ok, 2)

        def clear():
            nc.all_engine_barrier()
            for s in sems:
                nc.gpsimd.sem_clear(s)
            nc.all_engine_barrier()

        clear()
        with nc.Fori(0, DEPTH) as l:
            with nc.Block() as block:

                @block.sync
                def _(sp_):
                    row = 0
                    for name, n in (("norm_mix_2", 8), ("norm_xattn_2", 8), ("norm_mem_2", 8), ("norm_mlp_2", 8),
                                    ("mla_norm_q_2", 2), ("mla_norm_kv_2", 1), ("sg_b_2", 4), ("dn_conv_2", 24)):
                        src = a[name][bass.ds(l, 1)]
                        if name == "dn_conv_2":
                            src = src.rearrange("a j (k p) -> (a j k) p", p=P)
                        elif name == "sg_b_2":
                            src = src.rearrange("a g p -> (a g) p")
                        else:
                            src = src.rearrange("a (k p) -> (a k) p", p=P)
                        sp_.dma_start(par[row:row + n, :], src).then_inc(par_in, 16)
                        row += n
                    sp_.dma_start(sgw[:, :, :], a["sg_w_2"][bass.ds(l, 1)].rearrange("a g i j -> i (a g) j")
                                  ).then_inc(par_in, 16)
                    mem_at = {}
                    for w, (k, c, sources) in enumerate(chunks):
                        if w >= RING:
                            sp_.wait_ge(*read[w - RING])
                        for source in sources:
                            at, src = source(l)
                            sp_.dma_start(chunk(w)[:, :, at:at + src.shape[2]], src).then_inc(landed[w % RING], 16)
                        if w == 0:
                            for i, name in enumerate(("dn_dt_bias_2", "dn_a_log_2")):
                                sp_.dma_start(small[:, i, :], a[name][bass.ds(l, 1)].broadcast_to([P, 4])
                                              ).then_inc(small_in, 16)
                            for i, name in enumerate(("gla_norm_2", "dn_norm_2")):
                                sp_.dma_start(hgain[:, i, :], a[name][bass.ds(l, 1)].broadcast_to([P, 64])
                                              ).then_inc(small_in, 16)
                            for i, name in enumerate(("sg_ln_g_2", "sg_ln_b_2")):
                                sp_.dma_start(lnp[:, i, :], a[name][bass.ds(l, 1)].broadcast_to([P, W2])
                                              ).then_inc(small_in, 16)
                            sp_.dma_start(wg[:, :], a["gla_w_gate_2"][bass.ds(l, 1)].rearrange("a r c -> (a r) c")
                                          ).then_inc(w_in_, 16)
                            sp_.dma_start(bg[:, :], a["gla_b_gate_2"][bass.ds(l, 1)]).then_inc(w_in_, 16)
                            sp_.dma_start(wuq[:, :, :], cols(a["mla_w_uq_2"], l, 0, 384)).then_inc(w_in_, 16)
                            sp_.dma_start(wukv[:, :, :].rearrange("p a b -> p (a b)"),
                                          a["mla_w_ukv_2"][bass.ds(l, 1)].rearrange("a p c -> (a p) c")
                                          ).then_inc(w_in_, 16)
                        if w == 2:
                            sp_.dma_start(xm[:, :, :], a["mem_2"].rearrange("a (t p) d -> p (a t) d", p=P)
                                          ).then_inc(mem_in, 16)

                @block.tensor
                def _(pe):
                    T = nc.tensor

                    def bank(v):
                        if v >= 2:
                            pe.wait_ge(free, v - 1)
                        return ps[:, v % 2, :]

                    def take(w):
                        pe.wait_ge(landed[w % RING], W.ready[w])

                    def transposed(u0, n):
                        pe.wait_ge(xn_ok, n)
                        for k in range(KD):
                            if k % 2 == 0:
                                b = bank(u0 + k // 2)
                            for t in range(NT):
                                mm = T.transpose(b[:, (k % 2) * SEQ + t * P:(k % 2) * SEQ + (t + 1) * P],
                                                 xm[:, t, k * P:(k + 1) * P], ident)
                            if k % 2:
                                mm.then_inc(full, 1)

                    def feature_unit(out, w, c, nb, act_, k0=0, K=None):
                        wt = chunk(w)
                        K = K or chunks[w][0]
                        for b in range(nb):
                            for k in range(K):
                                mm = T.matmul(out[:, b * SEQ:(b + 1) * SEQ], wt[:, k0 + k, c + b * P:c + (b + 1) * P],
                                              act_[:, k, :], start=k == 0, stop=k == K - 1)
                        return mm

                    def token_unit(out, w, c, n, t, act_):
                        for k in range(8):
                            mm = T.matmul(out, act_[:, k, t * P:(t + 1) * P], chunk(w)[:, k, c:c + n],
                                          start=k == 0, stop=k == 7)
                        return mm

                    def in_chunk(i):
                        take(i)
                        for n, (kind, c, size, _, at) in enumerate(in_units[i]):
                            b = bank(U_IN[i] + n)
                            if kind == "F":
                                mm = feature_unit(b, i, c, size, hT)
                            elif kind == "G":
                                for k in range(KD):
                                    mm = T.matmul(b[at:at + size, 0:SEQ], chunk(i)[:, k, c:c + size], hT[:, k, :],
                                                  start=k == 0, stop=k == KD - 1)
                            elif kind == "T":
                                mm = token_unit(b[:, 0:size], i, c, size, at, hT)
                            else:
                                for t in range(NT):
                                    mm = token_unit(b[:, t * size:(t + 1) * size], i, c, size, t, hT)
                            mm.then_inc(full, 1)

                    gate_n = [0]

                    def gate():
                        g = gate_n[0]
                        gate_n[0] += 1
                        w = C_GATE + g // 2
                        if g % 2 == 0:
                            take(w)
                        feature_unit(bank(U_GATE + g), w, (g % 2) * SEQ, 2, hT).then_inc(full, 1)

                    def b_turn(n):
                        pe.wait_ge(bt_in, n + 1)
                        for b in range(2):
                            for t in range(NT):
                                mm = T.transpose(ps[:, 3, b * SEQ + t * P:b * SEQ + (t + 1) * P],
                                                 ob[:, t, b * P:(b + 1) * P], ident)
                        mm.then_inc(bt_ps, 1)

                    pe.wait_ge(par_in, 144)
                    T.transpose(ps[:, 2, 0:NPAR2], par[:, :], ident[0:NPAR2, 0:NPAR2]).then_inc(par_ps, 1)
                    for g in range(4):
                        mm = T.transpose(ps[:, 3, g * P:(g + 1) * P], sgw[:, g, :], ident)
                    mm.then_inc(par_ps, 1)
                    transposed(0, 1)
                    pe.wait_ge(free, 4)
                    in_chunk(0)
                    in_chunk(1)
                    pe.wait_ge(cn_ok, 1)
                    pe.wait_ge(par_ok, 2)
                    for t in range(NT):
                        for b in range(2):
                            T.transpose(ps[:, 2, b * SEQ + t * P:b * SEQ + (t + 1) * P], cq[:, t, b * P:(b + 1) * P],
                                        ident)
                        mm = T.transpose(ps[:, 3, t * P:(t + 1) * P], ckv[:, t, :], ident)
                    mm.then_inc(ct_ps, 1)
                    in_chunk(2)
                    pe.wait_ge(ct_ok, 1)
                    pe.wait_ge(w_in_, 64)
                    for h in range(4):
                        c = (h % 2) * SEQ
                        for k in range(2):
                            T.matmul(ps[0:MLA_D, 4 + h // 2, c:c + SEQ], wuq[:, k, h * MLA_D:(h + 1) * MLA_D],
                                     cT[:, k, :], start=k == 0, stop=k == 1)
                        T.matmul(ps[0:64, 6 + h // 2, c:c + SEQ], wukv[:, h, 0:64], cT[:, 2, :], start=True, stop=True)
                    for t in range(NT):
                        mm = T.matmul(ps[:, 2, t * W2:(t + 1) * W2], cT[:, 2, t * P:(t + 1) * P], wukv[:, :, 64:P],
                                      start=True, stop=True)
                    mm.then_inc(mq_ps, 1)
                    in_chunk(3)
                    pe.wait_ge(mq_ok, 1)
                    for i in range(5):
                        mm = T.matmul(ps[64:96, 4 + i // 2, (i % 2) * SEQ:(i % 2 + 1) * SEQ], half_turn, qT[64:96, i, :],
                                      start=True, stop=True)
                    mm.then_inc(rope_ps, 1)
                    in_chunk(4)
                    pe.wait_ge(rope_ok, 1)
                    for s in range(8):
                        t, h = s // 4, s % 4
                        w = P * (t + 1)
                        T.matmul(L[:, s, 0:w], qT[:, h, t * P:(t + 1) * P], kT[:, h, 0:w], start=True, stop=False)
                        mm = T.matmul(L[:, s, w - P:w], ident_bf, maskQ_bf, start=False, stop=True)
                    mm.then_inc(qk_ps, 1)
                    in_chunk(5)
                    pe.wait_ge(ex_ok, 1)
                    for s in range(8):
                        for k in range(s // 4 + 1):
                            mm = T.transpose(L[:, s, k * P:(k + 1) * P], probs[:, s, k * P:(k + 1) * P], ident)
                    mm.then_inc(pt_ps, 1)
                    gate()
                    pe.wait_ge(pt_a, 1)
                    pe.wait_ge(pt_v, 1)
                    for s in range(8):
                        t, h = s // 4, s % 4
                        for k in range(t + 1):
                            mm = T.matmul(ps[:, 2, t * W2 + h * 64:t * W2 + (h + 1) * 64], pT[:, s, k * P:(k + 1) * P],
                                          mv[:, k, h * 64:(h + 1) * 64], start=k == 0, stop=k == t)
                    mm.then_inc(o_ps, 1)
                    gate()
                    b_turn(0)
                    for t in range(NT):
                        T.matmul(ps[:, 2, t * P:(t + 1) * P], glr[:, t * P:(t + 1) * P], wg[:, :], start=True, stop=False)
                        mm = T.matmul(ps[:, 2, t * P:(t + 1) * P], upper[0:1, :], bg[:, :], start=False, stop=True)
                    mm.then_inc(pre_ps, 1)
                    gate()
                    pe.wait_ge(ln_ok, 1)
                    pe.wait_ge(bt_ok, 1)
                    for t in range(NT):
                        for g in range(4):
                            mm = T.matmul(ps[:, 3, t * W2 + g * 64:t * W2 + (g + 1) * 64], wsT[:, g, :],
                                          uv[:, t, W2 + g * 64:W2 + (g + 1) * 64], start=True, stop=True)
                    mm.then_inc(mix_ps, 1)
                    gate()
                    b_turn(1)
                    pe.wait_ge(l2_sq, 1)
                    for b in range(4):
                        mm = T.matmul(ps[:, 4 + b // 2, (b % 2) * SEQ:(b % 2 + 1) * SEQ], same_head, l2s[:, b, :],
                                      start=True, stop=True)
                    mm.then_inc(l2_ps, 1)
                    gate()
                    pe.wait_ge(lc_ok, 1)
                    pe.wait_ge(bt_ok, 2)
                    for t in range(NT):
                        T.matmul(ps[:, 3, 0:SEQ], lcat[:, t, 0:P], tri[:, t, :], start=t == 0, stop=t == NT - 1)
                    for t in range(NT):
                        T.matmul(ps[:, 2, 4 * t:4 * t + 4], upper, lcat[:, t, P:P + 4], start=True, stop=True)
                    T.matmul(ps[:, 2, 8:12], ones, lcat[:, 0, P:P + 4], start=True, stop=True).then_inc(cum_ps, 1)
                    gate()
                    gate()
                    pe.wait_ge(lev_ok, 1)
                    pe.wait_ge(l2_in, 1)
                    for r in range(5):
                        if r:
                            pe.wait_ge(sa_ok, r)
                        for h in range(4):
                            rows = slice(32 * h, 32 * h + 32)
                            if r == 4:
                                mm = T.matmul(ps[:, 4 + h, 0:P], ke[rows, 0, 0:P], qe[rows, 0, P:SEQ],
                                              start=True, stop=True)
                                continue
                            for i in range(2):
                                n = 2 * r + i
                                kk_, qq_ = (ke[rows, n + 1, :], qe[rows, n + 1, :]) if n < 7 else \
                                    (gqk[rows, 1, :], gqk[rows, 0, :])
                                for t in range(NT):
                                    c = i * SEQ + t * P
                                    mm = T.matmul(ps[:, 4 + h, c:c + P], kk_[:, t * P:(t + 1) * P],
                                                  qq_[:, t * P:(t + 1) * P], start=True, stop=True)
                        mm.then_inc(sa_ps, 1)
                        if r in (1, 3):
                            gate()
                    pe.wait_ge(sa_ok, 5)
                    pe.wait_ge(cum_ok, 1)
                    for t in range(NT):
                        for h in range(4):
                            out = ps[:, 2, t * W2 + h * 64:t * W2 + (h + 1) * 64]
                            mm = T.matmul(out, SaT[:, h, t, :], gv[:, t, h * 64:(h + 1) * 64], start=True, stop=t == 0)
                            if t:
                                mm = T.matmul(out, S01[:, h, :], gv[:, 0, h * 64:(h + 1) * 64], start=False, stop=True)
                    mm.then_inc(go_ps, 1)
                    for t in range(NT):
                        for h in range(4):
                            s = system(t, h)
                            out = ps[:, 4 + s // 4, (s % 4) * P:(s % 4 + 1) * P]
                            T.matmul(out, column(lcat[:, t, P + h:P + h + 1], P), upper, start=True, stop=False)
                            T.matmul(out, ident_bf, maskT_bf, start=False, stop=True)
                            mm = T.matmul(ps[:, 6 + s // 4, (s % 4) * P:(s % 4 + 1) * P], column(beta[:, t, h:h + 1], P),
                                          ident, start=True, stop=True)
                    mm.then_inc(row_ps, 1)
                    gate()
                    b_turn(2)
                    pe.wait_ge(l2_ok, 1)
                    pe.wait_ge(gn_ok, 1)
                    for t in range(NT):
                        for b in range(2):
                            T.transpose(ps[:, 2, t * W2 + b * P:t * W2 + (b + 1) * P], dnc[:, 4 + b, t * P:(t + 1) * P],
                                        ident)
                    pe.wait_ge(bt_ok, 3)
                    for b in range(2):
                        mm = T.transpose(ps[:, 3, b * P:(b + 1) * P], dnc[:, 2 + b, 0:P], ident)
                    mm.then_inc(tk_ps, 1)
                    pe.wait_ge(dec_ok, 1)
                    pe.wait_ge(lt_ok, 1)
                    for t in range(NT):
                        for h in range(4):
                            s, base = system(t, h), 64 * (h % 2)
                            key = dnc[base:base + 64, 2 + h // 2, t * P:(t + 1) * P]
                            T.matmul(ps[:, 4 + s // 4, (s % 4) * P:(s % 4 + 1) * P], key, key, start=True, stop=True)
                            mm = T.matmul(ps[:, 6 + s // 4, (s % 4) * P:(s % 4 + 1) * P], key,
                                          dnc[base:base + 64, h // 2, t * P:(t + 1) * P], start=True, stop=True)
                    mm.then_inc(kk_ps, 1)
                    gate()
                    pe.wait_ge(tk_ok, 1)
                    for lv in range(7):
                        for p in range(2):
                            it = 2 * lv + p
                            pe.wait_ge(lm_ok, it + 1)
                            if lv:
                                pe.wait_ge(xx_ok, it - 1)
                            for s in range(4 * p, 4 * p + 4):
                                mm = T.matmul(ps[:, 2 + p, (s % 4) * P:(s % 4 + 1) * P], LTm[:, s, :], X[:, s, :],
                                              start=True, stop=True)
                            mm.then_inc(yy_ps, 1)
                        for p in range(2):
                            it = 2 * lv + p
                            pe.wait_ge(yy_ok, it + 1)
                            if lv == 0:
                                pe.wait_ge(at_ok, 1)
                            for s in range(4 * p, 4 * p + 4):
                                c = slice((s % 4) * P, (s % 4 + 1) * P)
                                T.matmul(ps[:, 4 + 2 * p, c], XT[:, s, :], Y[:, s, :], start=True, stop=True)
                                mm = T.matmul(ps[:, 5 + 2 * p, c], Y[:, s, :], XT[:, s, :], start=True, stop=True)
                            mm.then_inc(zz_ps, 1)
                    gate()
                    pe.wait_ge(xx_ok, 14)
                    for h in range(4):
                        mm = T.matmul(ps[:, 2, h * 64:(h + 1) * 64], XT[:, system(0, h), :], rv[:, 0, h * 64:(h + 1) * 64],
                                      start=True, stop=True)
                    mm.then_inc(u_ps, 1)
                    gate()
                    pe.wait_ge(u_ok, 1)
                    for h in range(4):
                        base = 64 * (h % 2)
                        mm = T.matmul(ps[base:base + 64, 3, (h // 2) * 64:(h // 2 + 1) * 64], kd[:, h * 64:(h + 1) * 64],
                                      u[:, 0, h * 64:(h + 1) * 64], start=True, stop=True)
                    mm.then_inc(st_ps, 1)
                    gate()
                    pe.wait_ge(st_ok, 1)
                    for h in range(4):
                        base, hb = 64 * (h % 2), h // 2
                        for i, blk in enumerate((2 + hb, hb)):
                            mm = T.matmul(ps[:, 4 + h % 2, i * P + hb * 64:i * P + (hb + 1) * 64],
                                          dnc[base:base + 64, blk, P:SEQ], ssb[base:base + 64, hb * 64:(hb + 1) * 64],
                                          start=True, stop=True)
                    mm.then_inc(ks_ps, 1)
                    gate()
                    pe.wait_ge(r1_ok, 1)
                    for h in range(4):
                        mm = T.matmul(ps[:, 2, W2 + h * 64:W2 + (h + 1) * 64], XT[:, system(1, h), :],
                                      rv[:, 1, h * 64:(h + 1) * 64], start=True, stop=True)
                    mm.then_inc(u_ps, 1)
                    pe.wait_ge(u_ok, 2)
                    for t in range(NT):
                        for h in range(4):
                            mm = T.matmul(ps[:, 3, t * W2 + h * 64:t * W2 + (h + 1) * 64], attnT[:, system(t, h), :],
                                          u[:, t, h * 64:(h + 1) * 64], start=True, stop=True)
                    mm.then_inc(do_ps, 1)
                    while gate_n[0] < 16:
                        gate()
                    transposed(U_MEM, 2)
                    pe.wait_ge(free, U_MEM + 4)
                    for c in range(2):
                        take(C_WK + c)
                        for i in range(2):
                            feature_unit(bank(U_WK + 2 * c + i), C_WK + c, i * SEQ, 2, memT).then_inc(full, 1)
                    for c in range(2):
                        take(C_WV + c)
                        for t in range(NT):
                            token_unit(bank(U_WV + 2 * c + t), C_WV + c, 0, 512, t, memT).then_inc(full, 1)
                    b_turn(3)
                    for n in range(4):
                        if n % 2 == 0:
                            take(C_BR + n // 2)
                        pe.wait_ge(bt_ok, n + 1)
                        for m in range(4):
                            i = 4 * n + m
                            if i >= 4:
                                pe.wait_ge(pr_free, i - 3)
                            feature_unit(ps[:, 4 + i % 4, :], C_BR + n // 2, m * SEQ, 2, ys[:, n, :, :], 2 * (n % 2), 2
                                         ).then_inc(pr_ps, 1)
                    pe.wait_ge(mg_ok, 12)
                    for c in range(2):
                        take(C_OUT + c)
                        for t in range(NT):
                            token_unit(ps[:, 4 + 2 * c + t, :], C_OUT + c, 0, 512, t, merged).then_inc(res_ps, 1)
                    transposed(U_X6, 3)
                    pe.wait_ge(free, U_X6 + 4)
                    for c in range(2):
                        take(C_WQ + c)
                        for i in range(2):
                            feature_unit(bank(U_WQ + 2 * c + i), C_WQ + c, i * SEQ, 2, hT).then_inc(full, 1)
                    pe.wait_ge(free, U_WQ + 4)
                    for s in range(8):
                        t, h = s // 4, s % 4
                        for k in range(2):
                            mm = T.matmul(L[:, s, :], xq[:, 2 * h + k, t * P:(t + 1) * P], xk[:, 2 * h + k, :],
                                          start=k == 0, stop=k == 1)
                    mm.then_inc(qk_ps, 1)
                    pe.wait_ge(pn_ok, 1)
                    for s in range(8):
                        for k in range(2):
                            mm = T.transpose(L[:, s, k * P:(k + 1) * P], probs[:, s, k * P:(k + 1) * P], ident)
                    mm.then_inc(pt_ps, 1)
                    pe.wait_ge(pt_a, 2)
                    pe.wait_ge(pt_v, 2)
                    for b in range(8):
                        for t in range(NT):
                            for k in range(2):
                                mm = T.matmul(L[:, b, t * P:(t + 1) * P], xv[:, k, b * P:(b + 1) * P],
                                              pT[:, 4 * t + b // 2, k * P:(k + 1) * P], start=k == 0, stop=k == 1)
                    mm.then_inc(o_ps, 1)
                    pe.wait_ge(xo_ok, 1)
                    for c in range(2):
                        take(C_WO + c)
                        for t in range(NT):
                            token_unit(ps[:, 4 + 2 * c + t, :], C_WO + c, 0, 512, t, oT).then_inc(res_ps, 1)
                    transposed(U_X7, 4)
                    pe.wait_ge(free, U_X7 + 4)
                    for c in range(8):
                        take(C_UP + c)
                        for i in range(2):
                            feature_unit(bank(U_UP + 2 * c + i), C_UP + c, i * SEQ, 2, hT).then_inc(full, 1)
                    for c in range(8):
                        take(C_DN + c)
                        pe.wait_ge(hs_ok, min(2 * c + 2, 16))
                        for kk in range(4):
                            for t in range(NT):
                                for half in range(2):
                                    k = 4 * c + kk
                                    mm = T.matmul(ps[:, 4 + 2 * half + t, :], hid[:, k, t * P:(t + 1) * P],
                                                  chunk(C_DN + c)[:, kk, half * 512:(half + 1) * 512],
                                                  start=k == 0, stop=k == KH2 - 1)
                                    if k == KH2 - 1:
                                        mm.then_inc(res_ps, 1)
                        if c < 7:
                            mm.then_inc(down_used, 1)

                @block.scalar
                def _(act):
                    marks = {}

                    def mark(s, ins):
                        marks[s.name] = marks.get(s.name, 0) + 1
                        ins.then_inc(s, 1)
                        act.wait_ge(s, marks[s.name])

                    A = nc.scalar

                    def empty(v):
                        act.wait_ge(full, v + 1)
                        return ps[:, v % 2, :]

                    def squares(e, src):
                        for t in range(NT):
                            i = A.activation(flat(pT[:, 4 * t:4 * t + 4, :]), src[:, t, :], ACT.Square,
                                             accum_out=ssq[:, e, t:t + 1])
                        mark(ssq_ok, i)

                    def turned(u0, gain, dst):
                        for k in range(KD):
                            b = empty(u0 + k // 2)
                            i = A.activation(dst[:, k, :], b[:, (k % 2) * SEQ:(k % 2 + 1) * SEQ], ACT.Copy,
                                             scale=parT[:, gain + k:gain + k + 1])
                            if k % 2:
                                mark(free, i)

                    def in_chunk(i):
                        for n, (kind, c, size, name, at) in enumerate(in_units[i]):
                            b = empty(U_IN[i] + n)
                            dst = bufs[name]
                            if kind == "F":
                                ins = A.activation(dst[:, at:at + size, :], b[:, 0:size * SEQ].rearrange(
                                    "p (a b) -> p a b", a=size), ACT.Copy,
                                    scale=32 ** -0.5 if name == "gqk" and at == 0 else 1.0)
                            elif kind == "G":
                                ins = A.copy(dst, b[at:at + size, 0:SEQ])
                            elif kind == "T":
                                ins = A.activation(dst[:, at, :], b[:, 0:size], ACT.Gelu_apprx_tanh)
                            else:
                                ins = A.copy(dst, b[:, 0:NT * size].rearrange("p (t c) -> p t c", t=NT))
                            mark(free, ins)

                    gate_n = [0]

                    def gate():
                        g = gate_n[0]
                        gate_n[0] += 1
                        mark(free, A.copy(gates[:, 2 * g:2 * g + 2, :],
                                          empty(U_GATE + g).rearrange("p (a b) -> p a b", a=2)))

                    def b_out(n):
                        act.wait_ge(bt_ps, n + 1)
                        mark(bt_ok, A.copy(ys[:, n, :, :], ps[:, 3, :].rearrange("p (a b) -> p a b", a=2)))

                    def p_out(n):
                        act.wait_ge(pt_ps, n + 1)
                        if n:
                            mark(pt_a, A.copy(pT[:, 0:4, :], L[:, 0:4, :]))
                        else:
                            mark(pt_a, A.copy(pT[:, 0:4, 0:P], L[:, 0:4, 0:P]))

                    squares(0, x)
                    act.wait_ge(par_ok, 2)
                    turned(0, QM, hT)
                    act.wait_ge(init_ok, 1)
                    in_chunk(0)
                    in_chunk(1)
                    act.wait_ge(ct_ps, 1)
                    for b in range(3):
                        i = A.activation(cT[:, b, :], ps[:, 2 + b // 2, (b % 2) * SEQ:(b % 2 + 1) * SEQ], ACT.Copy,
                                         scale=parT[:, QQ + b:QQ + b + 1])
                    mark(ct_ok, i)
                    in_chunk(2)
                    act.wait_ge(mq_ps, 1)
                    A.activation(qT[:, 0:4, :], L[0:MLA_D, 0:4, :], ACT.Copy, scale=MLA_D ** -0.5)
                    A.copy(kT[0:64, :, :], L[0:64, 4:8, :])
                    mark(mq_ok, A.copy(mv[:, :, :], ps[:, 2, :].rearrange("p (t c) -> p t c", t=NT)))
                    in_chunk(3)
                    act.wait_ge(conv_ok, 1)
                    mark(silu_ok, A.activation(dnc[:, :, :], dnc[:, :, :], ACT.Silu))
                    act.wait_ge(mem_in, 16)
                    squares(2, xm)
                    in_chunk(4)
                    act.wait_ge(mx_ok, 1)
                    for s in range(8):
                        w = P * (s // 4 + 1)
                        i = A.activation(probs[:, s, 0:w], L[:, s, 0:w], ACT.Exp, bias=nmx[:, s:s + 1],
                                         accum_out=rsum[:, s:s + 1])
                    mark(ex_ok, i)
                    in_chunk(5)
                    p_out(0)
                    mark(l2_sq, A.activation(l2s, dnc[:, 0:4, :], ACT.Square))
                    gate()
                    gate()
                    b_out(0)
                    act.wait_ge(spv, 1)
                    mark(spe, A.activation(spb[:, 2, :], spb[:, 1, :], ACT.Exp, scale=-1.0))
                    mark(spe, A.activation(beta[:, :, :], dab[:, :, 4:8], ACT.Exp, scale=-1.0))
                    mark(spe, A.activation(asc[:, :], small[:, 1, :], ACT.Exp))
                    act.wait_ge(spv, 2)
                    mark(spe, A.activation(spb[:, 4, :], spb[:, 3, :], ACT.Ln))
                    gate()
                    gate()
                    b_out(1)
                    gate()
                    act.wait_ge(l2_in, 1)
                    mark(l2_rt, A.activation(l2r, l2r, ACT.Sqrt))
                    act.wait_ge(df_ok, 1)
                    mark(le_ok, A.activation(ed[:, :, :], ed[:, :, :], ACT.Exp, scale=-1.0))
                    act.wait_ge(eg_in, 1)
                    mark(eg_ok, A.activation(egam[:, :, :], egam[:, :, :], ACT.Exp))
                    gate()
                    gate()
                    mark(sil_ok, A.activation(gog[:, :, :], gog[:, :, :], ACT.Silu))
                    mark(sil_ok, A.activation(dz[:, :, :], dz[:, :, :], ACT.Silu))
                    gate()
                    gate()
                    act.wait_ge(row_ps, 1)
                    for t in range(NT):
                        for h in range(4):
                            s = system(t, h)
                            i = A.activation(decT[:, s, :], ps[:, 4 + s // 4, (s % 4) * P:(s % 4 + 1) * P], ACT.Exp,
                                             bias=ngam[:, t, h:h + 1])
                    mark(dec_ok, i)
                    gate()
                    b_out(2)
                    gate()
                    for lv in range(7):
                        for p in range(2):
                            act.wait_ge(yy_ps, 2 * lv + p + 1)
                            if lv:
                                act.wait_ge(zz_ps, 2 * lv + p - 1)
                            mark(yy_ok, A.copy(flat(Y[:, 4 * p:4 * p + 4, :]), ps[:, 2 + p, :]))
                    while gate_n[0] < 16:
                        gate()
                    turned(U_MEM, QE, memT)
                    act.wait_ge(do_ps, 1)
                    for i in range(4):
                        mark(free, A.copy(xk[:, 2 * i:2 * i + 2, :],
                                          empty(U_WK + i).rearrange("p (a b) -> p a b", a=2)))
                    for i in range(4):
                        mark(free, A.copy(xv[:, i % 2, (i // 2) * 512:(i // 2 + 1) * 512], empty(U_WV + i)))
                    b_out(3)
                    for g in range(4):
                        mark(sig_ok, A.activation(gates[:, 8 * g:8 * g + 8, :], gates[:, 8 * g:8 * g + 8, :],
                                                  ACT.Sigmoid))
                    act.wait_ge(res_ok, 4)
                    squares(6, x)
                    turned(U_X6, QX, hT)
                    for i in range(4):
                        mark(free, A.activation(xq[:, 2 * i:2 * i + 2, :],
                                                empty(U_WQ + i).rearrange("p (a b) -> p a b", a=2), ACT.Copy,
                                                scale=256 ** -0.5))
                    act.wait_ge(mx_ok, 2)
                    for s in range(8):
                        i = A.activation(probs[:, s, :], L[:, s, :], ACT.Exp, bias=nmx[:, s:s + 1],
                                         accum_out=rsum[:, s:s + 1])
                    mark(ex_ok, i)
                    p_out(1)
                    act.wait_ge(o_ps, 2)
                    mark(xo_ok, A.copy(oT[:, :, :], L[:, :, :]))
                    act.wait_ge(res_ok, 8)
                    squares(7, x)
                    turned(U_X7, QL, hT)
                    for i in range(16):
                        mark(free, A.activation(hid[:, 2 * i:2 * i + 2, :],
                                                empty(U_UP + i).rearrange("p (a b) -> p a b", a=2), ACT.Relu))

                @block.vector
                def _(dve):
                    n_chain = [0]
                    marks = {}
                    V = nc.vector

                    def link(ins):
                        n_chain[0] += 1
                        ins.then_inc(dch, 1)
                        dve.wait_ge(dch, n_chain[0])

                    def mark(s, ins):
                        marks[s.name] = marks.get(s.name, 0) + 1
                        ins.then_inc(s, 1)
                        dve.wait_ge(s, marks[s.name])

                    def mean_square(e, n, width):
                        mark(msq_ok, V.tensor_scalar(msq[:, e, 0:n], ssq[:, e, 0:n], 1.0 / width, EPS, ALU.mult, ALU.add))
                        dve.wait_ge(rstd_ok, e + 1)

                    def norm_in(e, seen, src):
                        dve.wait_ge(ssq_ok, seen)
                        mean_square(e, 2, D)
                        for t in range(NT):
                            i = V.tensor_scalar(xm[:, t, :], src[:, t, :], rstd[:, e, t:t + 1], None, ALU.mult)
                            if t == 0:
                                link(i)
                        mark(xn_ok, i)

                    def maxima(n):
                        dve.wait_ge(qk_ps, n + 1)
                        if n:
                            mark(mx_ok, V.tensor_reduce(nmx[:, :], L[:, :, :], AX_X, ALU.max, negate=True))
                        else:
                            link(V.tensor_reduce(nmx[:, 0:4], L[:, 0:4, 0:P], AX_X, ALU.max, negate=True))
                            mark(mx_ok, V.tensor_reduce(nmx[:, 4:8], L[:, 4:8, :], AX_X, ALU.max, negate=True))

                    def p_out(n):
                        dve.wait_ge(pt_ps, n + 1)
                        mark(pt_v, V.tensor_copy(pT[:, 4:8, :], L[:, 4:8, :]))

                    def heads(t):
                        return t.rearrange("p t (h c) -> p (t h) c", c=64)

                    def head_norm(e, gate_, gain):
                        link(V.tensor_tensor(tq[:, :, :], ob[:, :, :], ob[:, :, :], ALU.mult))
                        link(V.tensor_reduce(ssq[:, e, :], heads(tq[:, :, :]), AX_X, ALU.add))
                        mean_square(e, 8, 64)
                        link(V.tensor_tensor(heads(ob[:, :, :]), heads(ob[:, :, :]),
                                             rstd[:, e, :].unsqueeze(2).broadcast_to([P, 8, 64]), ALU.mult))
                        link(V.tensor_tensor(heads(gate_), heads(gate_),
                                             hgain[:, gain:gain + 1, :].broadcast_to([P, 8, 64]), ALU.mult))
                        mark(bt_in, V.tensor_tensor(ob[:, :, :], ob[:, :, :], gate_, ALU.mult))

                    mark(init_ok, V.memset(dnp[:, :, 0:3], 0.0))
                    dve.wait_ge(par_ps, 2)
                    mark(par_ok, V.tensor_copy(parT[:, :], ps[:, 2, 0:NPAR2]))
                    mark(par_ok, V.tensor_tensor(wsT[:, :, :], ps[:, 3, :].rearrange("p (g i) -> p g i", g=4),
                                                 upper.unsqueeze(1).broadcast_to([P, 4, P]), ALU.mult))
                    norm_in(0, 1, x)
                    dve.wait_ge(free, U_IN[0] + 2)
                    for i, (c, n) in enumerate(((cq, 256), (ckv, 128))):
                        t = probs[:, 2 * i:2 * i + 2, 0:n]
                        link(V.tensor_tensor(t, c[:, :, :], c[:, :, :], ALU.mult))
                        link(V.tensor_reduce(ssq[:, 1, 2 * i:2 * i + 2], t, AX_X, ALU.add))
                    link(V.tensor_scalar(msq[:, 1, 0:2], ssq[:, 1, 0:2], 1.0 / 256, EPS, ALU.mult, ALU.add))
                    mark(msq_ok, V.tensor_scalar(msq[:, 1, 2:4], ssq[:, 1, 2:4], 1.0 / 128, EPS, ALU.mult, ALU.add))
                    dve.wait_ge(rstd_ok, 2)
                    for t in range(NT):
                        link(V.tensor_scalar(cq[:, t, :], cq[:, t, :], rstd[:, 1, t:t + 1], None, ALU.mult))
                        i = V.tensor_scalar(ckv[:, t, :], ckv[:, t, :], rstd[:, 1, 2 + t:3 + t], None, ALU.mult)
                        if t == 0:
                            link(i)
                    mark(cn_ok, i)
                    dve.wait_ge(free, U_IN[2] + 1)
                    for b in range(6):
                        link(V.tensor_scalar(dnc[:, b, :], dnp[:, b, 0:SEQ], parT[:, QC + b:QC + b + 1], None, ALU.mult))
                        for j in range(1, 4):
                            i = V.scalar_tensor_tensor(dnc[:, b, :], dnp[:, b, j:j + SEQ],
                                                       parT[:, QC + 6 * j + b:QC + 6 * j + b + 1], dnc[:, b, :],
                                                       ALU.mult, ALU.add)
                            if b == 5 and j == 3:
                                mark(conv_ok, i)
                            else:
                                link(i)
                    dve.wait_ge(rope_ps, 1)
                    turn = ps[64:96, 4:7, :].rearrange("p b (c d) -> p (b c) d", c=2)[:, 0:5, :]
                    t5 = probs[64:96, 0:5, :]
                    link(V.tensor_tensor(t5, turn, trig[64:96, 1:2, :].broadcast_to([32, 5, SEQ]), ALU.mult))
                    link(V.tensor_tensor(qT[64:96, :, :], qT[64:96, :, :],
                                         trig[64:96, 0:1, :].broadcast_to([32, 5, SEQ]), ALU.mult))
                    link(V.tensor_tensor(qT[64:96, :, :], qT[64:96, :, :], t5, ALU.add))
                    mark(rope_ok, V.tensor_copy(kT[64:96, :, :], qT[64:96, 4:5, :].broadcast_to([32, 4, SEQ])))
                    norm_in(2, 2, xm)
                    maxima(0)
                    p_out(0)
                    dve.wait_ge(ex_ok, 1)
                    link(V.reciprocal(rinv[:, :], rsum[:, :]))
                    dve.wait_ge(o_ps, 1)
                    mark(bt_in, V.tensor_tensor(heads(ob[:, :, :]), ps[:, 2, :].rearrange("p (s c) -> p s c", c=64),
                                                rinv[:, :].unsqueeze(2).broadcast_to([P, 8, 64]), ALU.mult))
                    dve.wait_ge(small_in, 96)
                    v3, r3 = (spb[:, i, :].rearrange("p (t c) -> p t c", t=NT) for i in (0, 1))
                    dve.wait_ge(pre_ps, 1)
                    link(V.tensor_scalar(v3[:, :, 0:P], ps[:, 2, 0:SEQ].rearrange("p (t c) -> p t c", t=NT), -1.0, None,
                                         ALU.mult))
                    link(V.tensor_tensor(v3[:, :, P:P + 4], dab[:, :, 0:4], small[:, 0:1, :].broadcast_to([P, NT, 4]),
                                         ALU.add))
                    mark(spv, V.scalar_tensor_tensor(spb[:, 1, :], spb[:, 0, :], -1.0, spb[:, 0, :], ALU.mult, ALU.max))
                    sv = uv[:, :, W2:2 * W2]
                    link(V.tensor_reduce(mean[:, :], sv, AX_X, ALU.add))
                    link(V.tensor_scalar(mean[:, :], mean[:, :], 1.0 / W2, None, ALU.mult))
                    link(V.tensor_tensor(sv, sv, mean[:, :].unsqueeze(2).broadcast_to([P, NT, W2]), ALU.subtract))
                    link(V.tensor_tensor(tq[:, :, :], sv, sv, ALU.mult))
                    link(V.tensor_reduce(ssq[:, 3, 0:2], tq[:, :, :], AX_X, ALU.add))
                    mean_square(3, 2, W2)
                    for t in range(NT):
                        link(V.scalar_tensor_tensor(sv[:, t, :], sv[:, t, :], rstd[:, 3, t:t + 1], lnp[:, 0, :],
                                                    ALU.mult, ALU.mult))
                    mark(ln_ok, V.tensor_tensor(sv, sv, lnp[:, 1:2, :].broadcast_to([P, NT, W2]), ALU.add))
                    dve.wait_ge(spe, 1)
                    mark(spv, V.tensor_scalar(spb[:, 3, :], spb[:, 2, :], 1.0, None, ALU.add))
                    dve.wait_ge(spe, 2)
                    link(V.tensor_scalar(beta[:, :, :], beta[:, :, :], 1.0, None, ALU.add))
                    link(V.reciprocal(beta[:, :, :], beta[:, :, :]))
                    dve.wait_ge(spe, 4)
                    link(V.tensor_scalar(spb[:, 1, :], spb[:, 3, :], -1.0, None, ALU.add))
                    link(V.tensor_tensor(spb[:, 1, :], spb[:, 2, :], spb[:, 1, :], ALU.subtract))
                    link(V.reciprocal(spb[:, 3, :], spb[:, 3, :]))
                    link(V.tensor_tensor(spb[:, 1, :], spb[:, 1, :], spb[:, 3, :], ALU.mult))
                    link(V.tensor_tensor(spb[:, 1, :], spb[:, 1, :], spb[:, 4, :], ALU.add))
                    link(V.scalar_tensor_tensor(spb[:, 1, :], spb[:, 0, :], 0.0, spb[:, 1, :], ALU.max, ALU.add))
                    link(V.tensor_scalar(asc[:, :], asc[:, :], -1.0, None, ALU.mult))
                    link(V.tensor_tensor(lcat[:, :, P:P + 4], r3[:, :, P:P + 4],
                                         asc[:, :].unsqueeze(1).broadcast_to([P, NT, 4]), ALU.mult))
                    mark(lc_ok, V.tensor_scalar(lcat[:, :, 0:P], r3[:, :, 0:P], -1.0 / 16.0, None, ALU.mult))
                    dve.wait_ge(mix_ps, 1)
                    dve.wait_ge(bt_ps, 1)
                    for t in range(NT):
                        link(V.tensor_tensor(tq[:, t, :].rearrange("p (g c) -> p g c", c=64),
                                             ps[:, 3, t * W2:(t + 1) * W2].rearrange("p (g c) -> p g c", c=64),
                                             parT[:, QS:QS + 4].unsqueeze(2).broadcast_to([P, 4, 64]), ALU.add))
                    mark(bt_in, V.tensor_tensor(ob[:, :, :], tq[:, :, :], uv[:, :, 0:W2], ALU.mult))
                    dve.wait_ge(l2_ps, 1)
                    mark(l2_in, V.tensor_scalar(l2r, L[:, 0:4, :], EPS, None, ALU.add))
                    dve.wait_ge(cum_ps, 1)
                    link(V.tensor_copy(gcum[:, :], ps[:, 3, 0:SEQ]))
                    mark(cum_ok, V.tensor_copy(gam[:, :, :], ps[:, 2, 0:12].rearrange("p (t h) -> p t h", h=4)))
                    for n, b in enumerate((P,) + SUBL):
                        v = gcum[:, :].rearrange("p (n w) -> p n w", w=2 * b)
                        link(V.tensor_tensor(ed[:, n, :].rearrange("p (n w) -> p n w", w=2 * b), v,
                                             v[:, :, b - 1:b].broadcast_to([P, P // b, 2 * b]), ALU.subtract))
                    mark(df_ok, V.scalar_tensor_tensor(ed[:, :, :], ed[:, :, :], -1.0, ed[:, :, :], ALU.mult, ALU.max))
                    link(V.tensor_scalar(ngam[:, :, :], gam[:, 0:2, :], -1.0, None, ALU.mult))
                    link(V.tensor_copy(egam[:, 0:2, :], gam[:, 0:2, :]))
                    mark(eg_in, V.tensor_tensor(egam[:, 2, :], gam[:, 2, :], gam[:, 0, :], ALU.subtract))
                    dve.wait_ge(l2_rt, 1)
                    link(V.reciprocal(l2r, l2r))
                    link(V.scalar_tensor_tensor(dnc[:, 0:2, :], dnc[:, 0:2, :], 0.125, l2r[:, 0:2, :], ALU.mult, ALU.mult))
                    mark(l2_ok, V.tensor_tensor(dnc[:, 2:4, :], dnc[:, 2:4, :], l2r[:, 2:4, :], ALU.mult))
                    dve.wait_ge(le_ok, 1)
                    link(V.tensor_tensor(qe, ed, gqk[:, 0:1, :].broadcast_to([P, 8, SEQ]), ALU.mult))
                    mark(lev_ok, V.tensor_tensor(ke, ed, gqk[:, 1:2, :].broadcast_to([P, 8, SEQ]), ALU.mult))
                    link(V.memset(SaT[:, :, :, :], 0.0))
                    for r in range(4):
                        dve.wait_ge(sa_ps, r + 1)
                        for i in range(2):
                            n = 2 * r + i
                            m = lmask[:, n, :].bitcast(U32).unsqueeze(1).unsqueeze(1).broadcast_to([P, 4, NT, P])
                            ins = V.copy_predicated(SaT[:, :, :, :], m, ps[:, 4:8, i * SEQ:(i + 1) * SEQ].rearrange(
                                "p h (t i) -> p h t i", t=NT))
                            if i == 0:
                                link(ins)
                        mark(sa_ok, ins)
                    dve.wait_ge(sa_ps, 5)
                    mark(sa_ok, V.tensor_copy(S01[:, :, :], ps[:, 4:8, 0:P]))
                    dve.wait_ge(go_ps, 1)
                    dve.wait_ge(bt_ps, 2)
                    mark(gn_ok, V.tensor_copy(ob[:, :, :], ps[:, 2, :].rearrange("p (t c) -> p t c", t=NT)))
                    dve.wait_ge(sil_ok, 2)
                    head_norm(4, gog[:, :, :], 0)
                    dve.wait_ge(dec_ok, 1)
                    two = ps[:, 6:8, :].rearrange("p b (s i) -> p (b s) i", s=4)
                    mark(lt_ok, V.tensor_tensor(LT, decT, two, ALU.mult))
                    dve.wait_ge(tk_ps, 1)
                    dve.wait_ge(eg_ok, 1)
                    link(V.tensor_tensor(heads(rv), ps[:, 2, :].rearrange("p (s c) -> p s c", c=64),
                                         beta[:, :, :].rearrange("p t h -> p (t h)").unsqueeze(2)
                                         .broadcast_to([P, 8, 64]), ALU.mult))
                    mark(tk_ok, V.tensor_tensor(kd.rearrange("p (h c) -> p h c", c=64),
                                                ps[:, 3, 0:W2].rearrange("p (h c) -> p h c", c=64),
                                                egam[:, 2, :].unsqueeze(2).broadcast_to([P, 4, 64]), ALU.mult))
                    dve.wait_ge(kk_ps, 1)
                    link(V.tensor_tensor(LT, LT, ps[:, 4:6, :].rearrange("p b (s i) -> p (b s) i", s=4), ALU.mult))
                    mark(at_ok, V.tensor_tensor(attnT, decT, two, ALU.mult))
                    eye = ident.unsqueeze(1).broadcast_to([P, 8, P])
                    link(V.tensor_copy(X, eye))
                    link(V.tensor_copy(XT, eye))
                    for lv in range(7):
                        for p in range(2):
                            s = slice(4 * p, 4 * p + 4)
                            if lv:
                                dve.wait_ge(yy_ps, 2 * lv + p - 1)
                            mark(lm_ok, V.tensor_tensor(LTm[:, s, :], LT[:, s, :],
                                                        lmask[:, 6 - lv:7 - lv, :].broadcast_to([P, 4, P]), ALU.mult))
                        for p in range(2):
                            dve.wait_ge(zz_ps, 2 * lv + p + 1)
                            for i, m in enumerate((X, XT)):
                                v = m[:, 4 * p:4 * p + 4, :]
                                ins = V.tensor_tensor(v, v, ps[:, 4 + 2 * p + i, :].rearrange("p (s i) -> p s i", s=4),
                                                      ALU.subtract)
                                if i == 0:
                                    link(ins)
                            mark(xx_ok, ins)
                    dve.wait_ge(u_ps, 1)
                    mark(u_ok, V.tensor_copy(u[:, 0, :], ps[:, 2, 0:W2]))
                    dve.wait_ge(st_ps, 1)
                    mark(st_ok, V.tensor_copy(ssb, ps[:, 3, 0:P]))
                    dve.wait_ge(ks_ps, 1)
                    kS, qS = (ps[:, 4:6, i * P:(i + 1) * P].rearrange("p a (b c) -> p b a c", b=2) for i in range(2))

                    def by_head(v):
                        return v.rearrange("p (b a c) -> p b a c", b=2, a=2)

                    def per_head(v):
                        return v.rearrange("p (b a) -> p b a", b=2).unsqueeze(3).broadcast_to([P, 2, 2, 64])

                    link(V.tensor_tensor(rinv[:, 0:4], beta[:, 1, :], egam[:, 1, :], ALU.mult))
                    link(V.tensor_tensor(by_head(tq[:, 0, :]), kS, per_head(rinv[:, 0:4]), ALU.mult))
                    mark(r1_ok, V.tensor_tensor(rv[:, 1, :], rv[:, 1, :], tq[:, 0, :], ALU.subtract))
                    link(V.tensor_tensor(by_head(tq[:, 1, :]), qS, per_head(egam[:, 1, :]), ALU.mult))
                    dve.wait_ge(u_ps, 2)
                    mark(u_ok, V.tensor_copy(u[:, 1, :], ps[:, 2, W2:2 * W2]))
                    dve.wait_ge(do_ps, 1)
                    dve.wait_ge(bt_ps, 3)
                    link(V.tensor_copy(ob[:, 0, :], ps[:, 3, 0:W2]))
                    link(V.tensor_tensor(ob[:, 1, :], ps[:, 3, W2:2 * W2], tq[:, 1, :], ALU.add))
                    head_norm(5, dz[:, :, :], 1)
                    for n in range(4):
                        dve.wait_ge(sig_ok, n + 1)
                        for m in range(4):
                            i = 4 * n + m
                            dve.wait_ge(pr_ps, i + 1)
                            src = ps[:, 4 + i % 4, :].rearrange("p (b c) -> p b c", b=2)
                            gt = gates[:, 8 * n + 2 * m:8 * n + 2 * m + 2, :]
                            out, tmp = (z[:, 2 * m:2 * m + 2, :] for z in (merged, hT))
                            if n == 0:
                                mark(pr_free, V.tensor_tensor(out, src, gt, ALU.mult))
                                continue
                            mark(pr_free, V.tensor_tensor(tmp, src, gt, ALU.mult))
                            mark(mg_ok, V.tensor_tensor(out, out, tmp, ALU.add))

                    def residual(n):
                        for i in range(4):
                            dve.wait_ge(res_ps, 4 * n + i + 1)
                            c, t = (i % 2, i // 2) if n == 2 else (i // 2, i % 2)
                            xs = x[:, t, c * 512:(c + 1) * 512]
                            mark(res_ok, V.tensor_tensor(xs, xs, ps[:, 4 + 2 * c + t, :], ALU.add))

                    residual(0)
                    norm_in(6, 3, x)
                    maxima(1)
                    dve.wait_ge(ex_ok, 2)
                    link(V.reciprocal(rinv[:, :], rsum[:, :]))
                    mark(pn_ok, V.tensor_tensor(probs[:, :, :], probs[:, :, :],
                                                rinv[:, :].unsqueeze(2).broadcast_to([P, 8, SEQ]), ALU.mult))
                    p_out(1)
                    residual(1)
                    norm_in(7, 4, x)
                    for i in range(16):
                        dve.wait_ge(free, U_UP + i + 1)
                        h2 = hid[:, 2 * i:2 * i + 2, :]
                        mark(hs_ok, V.tensor_tensor(h2, h2, h2, ALU.mult))
                    residual(2)

                @block.gpsimd
                def _(pool):
                    def rsqrt(e, n):
                        pool.wait_ge(msq_ok, e + 1)
                        nc.gpsimd.tensor_tensor(rstd[:, e, 0:n], msq[:, e, 0:n], nhalf[:, 0:n], ALU.pow
                                                ).then_inc(rstd_ok, 1)

                    rsqrt(0, 2)
                    rsqrt(1, 4)
                    rsqrt(2, 2)
                    rsqrt(3, 2)
                    rsqrt(4, 8)
                    rsqrt(5, 8)
                    rsqrt(6, 2)
                    rsqrt(7, 2)

            clear()

        with nc.Block() as block:

            @block.sync
            def _(sp_):
                sp_.dma_start(xm[:, 0, :], a["norm_final_2"].partition_broadcast(P)).then_inc(fin_in, 16)

            @block.scalar
            def _(act):
                for t in range(NT):
                    nc.scalar.activation(flat(pT[:, 4 * t:4 * t + 4, :]), x[:, t, :], ACT.Square,
                                         accum_out=ssq[:, 0, t:t + 1]).then_inc(ssq_ok, 1)

            @block.vector
            def _(dve):
                dve.wait_ge(ssq_ok, 2)
                nc.vector.tensor_scalar(msq[:, 0, 0:2], ssq[:, 0, 0:2], 1.0 / D, EPS, ALU.mult, ALU.add
                                        ).then_inc(msq_ok, 1)
                dve.wait_ge(rstd_ok, 1)
                dve.wait_ge(fin_in, 16)
                for t in range(NT):
                    nc.vector.scalar_tensor_tensor(x[:, t, :], x[:, t, :], rstd[:, 0, t:t + 1], xm[:, 0, :],
                                                   ALU.mult, ALU.mult).then_inc(y_ok, 1)
                dve.wait_ge(y_ok, 2)

            @block.gpsimd
            def _(pool):
                pool.wait_ge(msq_ok, 1)
                nc.gpsimd.tensor_tensor(rstd[:, 0, 0:2], msq[:, 0, 0:2], nhalf[:, 0:2], ALU.pow).then_inc(rstd_ok, 1)

def build(nc, a, y):
    with ExitStack() as ctx:
        ps = ctx.enter_context(nc.psum_tensor("ps", [P, 8, 512], F32))
        x = ctx.enter_context(nc.sbuf_tensor("x", [P, NT, D], F32))
        con = ctx.enter_context(nc.sbuf_tensor("con", [P, N_CONST], F32))
        bfc = ctx.enter_context(nc.sbuf_tensor("bfc", [P, 3, P], BF16))
        con_in, con_bf = (ctx.enter_context(nc.semaphore(n)) for n in ("con_in", "con_bf"))
        out_done = ctx.enter_context(nc.semaphore("out_done"))
        with nc.Block() as block:

            @block.sync
            def _(sp):
                sp.dma_start(con[:, :], a["constants"]).then_inc(con_in, 16)
                sp.dma_start(x[:, :, :], a["x"].rearrange("a (t p) d -> p (a t) d", p=P)).then_inc(con_in, 16)
                sp.wait_ge(con_in, 32)

            @block.vector
            def _(dve):
                dve.wait_ge(con_in, 32)
                for i, c in enumerate((C_ID, C_MT, C_MQ)):
                    nc.vector.tensor_copy(bfc[:, i, :], con[:, c:c + P]).then_inc(con_bf, 1)
                dve.wait_ge(con_bf, 3)

        first_block(nc, ps, x, con, bfc, a)
        second_block(nc, ps, x, con, bfc, a)

        with nc.Block() as block:

            @block.sync
            def _(sp):
                sp.dma_start(y.rearrange("a (t p) d -> p (a t) d", p=P), x[:, :, :]).then_inc(out_done, 16)
                sp.wait_ge(out_done, 16)


_INS = [
    "x", "norm_mix_pre", "w_in", "conv_w", "conv_b", "dt_bias", "a_log", "d_skip", "ssm_norm",
    "fox_fbias", "w_gate", "b_gate", "w_branch", "w_out", "norm_mix_post", "norm_ffn_pre", "w_ffn_in",
    "w_ffn_out", "norm_ffn_post", "mem_2", "positions_2", "norm_mix_2", "w_in_2", "mla_norm_q_2",
    "mla_norm_kv_2", "mla_w_uq_2", "mla_w_ukv_2", "sg_ln_g_2", "sg_ln_b_2", "sg_w_2", "sg_b_2",
    "gla_w_gate_2", "gla_b_gate_2", "gla_norm_2", "dn_conv_2", "dn_a_log_2", "dn_dt_bias_2",
    "dn_norm_2", "w_branch_2", "w_out_2", "norm_xattn_2", "norm_mem_2", "xattn_wq_2", "xattn_wk_2",
    "xattn_wv_2", "xattn_wo_2", "norm_mlp_2", "w_up_2", "w_down_2", "norm_final_2",
]


def kernel(**inputs):
    import concourse.bacc as bacc
    from concourse.bass_utils import run_bass_kernel_spmd

    nc = bacc.Bacc("TRN2", target_bir_lowering=False, num_devices=1)
    arrays, args = {}, {}
    for name, value in [(n, inputs[n]) for n in _INS] + [
            ("constants", shape_constants()), ("constants_1", shape_constants_1()),
            ("constants_2", shape_constants_2())]:
        value = np.ascontiguousarray(value)
        arrays["in_" + name] = value
        args[name] = nc.dram_tensor("in_" + name, value.shape, mybir.dt.from_np(value.dtype),
                                    kind="ExternalInput").ap()
    y = nc.dram_tensor("out_0", (1, SEQ, D), F32, kind="ExternalOutput").ap()
    build(nc, args, y)
    result = run_bass_kernel_spmd(nc, [arrays], core_ids=[0])
    return result.results[0]["out_0"]
```

```python
from contextlib import ExitStack

import numpy as np

import concourse.bass as bass
from concourse import mybir

F32 = mybir.dt.float32
F32R = mybir.dt.float32r
BF16 = mybir.dt.bfloat16
I32 = mybir.dt.int32
U32 = mybir.dt.uint32
ALU = mybir.AluOpType
ACT = mybir.ActivationFunctionType
AX_X = mybir.AxisListType.X

P = 128
SEQ = 256
NT = SEQ // P
D = 1024
KD = D // P
DEPTH = 2
EPS = 1e-6
NEG = -1e30
TAKEN = -3e38
RING = 2
SLOT = 8 * 528

HALVES = 3
HALF = 8 * 256

C_ID, C_U, C_MT, C_MQ, N_CONST = 0, 128, 640, 768, 896
C1_COS, C1_SIN, C1_ROT, N_CONST1 = 0, 256, 512, 640
C2_LV, C2_B64, C2_R2, C2_INV, N_CONST2 = 0, 1024, 1152, 1184, 1186


def shape_constants():
    c = np.zeros((P, N_CONST), np.float32)
    r = np.arange(P)
    t = np.arange(SEQ)
    c[:, C_ID:C_ID + P] = np.eye(P)
    for tile in range(NT):
        c[:, C_U + tile * SEQ:C_U + (tile + 1) * SEQ] = (tile * P + r)[:, None] <= t[None, :]
    c[:, C_MT:C_MT + P] = np.where(r[:, None] > r[None, :], NEG, 0)
    c[:, C_MQ:C_MQ + P] = np.where(r[None, :] > r[:, None], NEG, 0)
    return c


def shape_constants_1():
    c = np.zeros((P, N_CONST1), np.float32)
    r = np.arange(P)
    t = np.arange(SEQ)
    inv = (np.float32(10000.0) ** (-np.arange(0, 64, 2, dtype=np.float32) / np.float32(64))).astype(np.float32)
    ang = (t.astype(np.float32)[None, :] * inv[r % 32][:, None]).astype(np.float32).astype(np.float64)
    c[:, C1_COS:C1_COS + SEQ] = np.cos(ang)
    c[:, C1_SIN:C1_SIN + SEQ] = np.sin(ang)
    for m in range(P):
        k = m + 32 if m % 64 < 32 else m - 32
        c[k, C1_ROT + m] = -1.0 if m % 64 < 32 else 1.0
    return c


def shape_constants_2():
    c = np.zeros((P, N_CONST2), np.float32)
    r = np.arange(P)
    for n, b in enumerate((64, 32, 16, 8, 4, 2, 1)):
        same = r[:, None] // (2 * b) == r[None, :] // (2 * b)
        c[:, C2_LV + n * P:C2_LV + (n + 1) * P] = same & (r[:, None] // b % 2 == 0) & (r[None, :] // b % 2 == 1)
    c[:, C2_LV + 7 * P:C2_LV + 8 * P] = np.eye(P)
    c[:, C2_B64:C2_B64 + P] = r[:, None] // 64 == r[None, :] // 64
    for m in range(32):
        k = m + 16 if m < 16 else m - 16
        c[64 + k, C2_R2 + m] = -1.0 if m < 16 else 1.0
    inv2 = (np.float32(10000.0) ** (-np.arange(0, 32, 2, dtype=np.float32) / np.float32(32))).astype(np.float32)
    c[64:96, C2_INV] = inv2[np.arange(32) % 16]
    return c


def column(ap, n):
    return ap.broadcast_to([ap.shape[0], n])


class Weights:

    def __init__(self, chunks):
        self.chunks = chunks
        self.total = [0] * RING
        self.ready = []
        for w, (_, _, sources) in enumerate(chunks):
            self.total[w % RING] += 16 * len(sources)
            self.ready.append(self.total[w % RING])


W1 = 512
HID1 = 2816
KH1 = HID1 // P
IN1 = [
    (512, 512, [("F", 0, 2, "xbc", 0), ("F", 256, 2, "xbc", 2)]),
    (1024, 520, [("F", 0, 2, "xbc", 4), ("F", 256, 2, "xbc", 6), ("T", 512, 8, "dt")]),
    (2568, 520, [("T", 0, 512, "fv"), ("T", 512, 8, "ff")]),
    (3088, 512, [("F", 0, 2, "mq", 0), ("F", 256, 2, "mq", 2)]),
    (3600, 512, [("F", 0, 2, "mk", 0), ("F", 256, 2, "mk", 2)]),
    (6160, 324, [("F", 0, 2, "iqk", 0), ("I", 256, 1, "iqk", 2), ("T", 320, 4, "iw")]),
    (4624, 512, [("F", 0, 2, "dq", 0), ("F", 256, 2, "dq", 2)]),
    (5136, 512, [("F", 0, 2, "dk", 0), ("F", 256, 2, "dk", 2)]),
    (1544, 512, [("F", 0, 2, "fq", 0), ("F", 256, 2, "fq", 2)]),
    (2056, 512, [("F", 0, 2, "fk", 0), ("F", 256, 2, "fk", 2)]),
    (4112, 512, [("T", 0, 512, "mv")]),
    (5648, 512, [("T", 0, 512, "dv")]),
    (0, 512, [("T", 0, 512, "z")]),
]
ROPES = ["mq", "mk", "iqk", "dq", "dk"]
QSCALE = {"fq": 0.125, "mq": 0.125, "dq": 0.125}
PGM, PCW, PCB, PSN, PBG, PGF, NPAR1 = 0, 8, 40, 48, 52, 84, 92


def units_of(pieces):
    out = []
    for p in pieces:
        if p[0] in "FI":
            out.append((p[0], p[1], p[2], p[3], p[4]))
        elif p[2] > 256:
            out += [("T", p[1], p[2], p[3], t) for t in range(NT)]
        else:
            out.append(("S", p[1], p[2], p[3], 0))
    return out


def first_block(nc, ps, x, con, bfc, a):
    with ExitStack() as ctx:
        mixer = ExitStack()

        def sb(name, shape, dt=F32):
            return ctx.enter_context(nc.sbuf_tensor("a_" + name, shape, dt))

        def mix(name, shape, dt=F32):
            return mixer.enter_context(nc.sbuf_tensor("a_" + name, shape, dt))

        def sem(name):
            s = ctx.enter_context(nc.semaphore("a_" + name))
            sems.append(s)
            return s

        sems = []
        ident = con[:, C_ID:C_ID + P]
        ident_bf, maskT_bf, maskQ_bf = (bfc[:, i, :] for i in range(3))
        tri = con[:, C_U:C_U + NT * SEQ].rearrange("p (t l) -> p t l", t=NT)
        maskQ = con[:, C_MQ:C_MQ + P]
        con1 = sb("con1", [P, N_CONST1])
        cos, sin = con1[:, C1_COS:C1_COS + SEQ], con1[:, C1_SIN:C1_SIN + SEQ]
        rot = con1[:, C1_ROT:C1_ROT + P]

        ring = sb("ring", [P, RING, SLOT])
        hT = sb("hT", [P, KD, SEQ])
        with ExitStack() as under:
            nlo1 = under.enter_context(nc.sbuf_tensor("a_nlo1", [P, KD, SEQ], F32R))
        xm = sb("xm", [P, NT, D])
        par = sb("par", [NPAR1, P])
        parT = sb("parT", [P, NPAR1])
        small = sb("small", [P, 4, 8])
        nident = sb("nident", [16, 16])
        sc8 = sb("sc8", [P, 8, 384])
        dtff = sb("dtff", [P, NT, 16])
        iw = sb("iw", [P, NT, 4])[:, :, :]
        sp = sb("sp", [P, 6, NT * 16])
        lcat = sb("lcat", [P, NT, 16])
        asg = sb("asg", [P, 16])
        cumT = sb("cumT", [16, SEQ])
        ncum = sb("ncum", [P, NT, 16])
        cb = sb("cb", [P, 2, 384])
        top8 = sb("top8", [P, 8])
        nmx = sb("nmx", [P, 2, 8])
        rsum = sb("rsum", [P, 2, 8])
        rinv = sb("rinv", [P, 8])
        ssq = sb("ssq", [P, 5, 4])
        msq = sb("msq", [P, 5, 4])
        rstd = sb("rstd", [P, 5, 4])
        nhalf = sb("nhalf", [P, 4])
        with ExitStack() as under:
            whi1, wlo1 = (under.enter_context(nc.sbuf_tensor(f"a_{n}", [P, HALVES, 8 * 264], F32R))
                          for n in ("whi1", "wlo1"))
        gates = sb("gates", [P, 32, SEQ])
        ys = mix("ys", [P, 4, 4, SEQ])
        y = mix("y", [P, NT, W1])
        xbcp = mix("xbcp", [P, 8, SEQ + 4])
        probs = xbcp[:, :, 0:SEQ]
        xbc = mix("xbc", [P, 8, SEQ])
        merged = xbc
        rt = sc8[:, :, :].rearrange("p a b -> p (a b)")[:, 0:2 * D].rearrange("p (a b) -> p a b", a=8)
        gpost = sc8[:, :, :].rearrange("p a b -> p (a b)")[:, 0:2 * D].rearrange("p (a b) -> p a b", a=2)
        under = ExitStack()
        nhi1 = under.enter_context(nc.sbuf_tensor("a_nhi1", [P, KD, SEQ], F32R))
        under.close()
        xd = mix("xd", [P, 2, NT, W1])
        pT = xd[:, :, :, :].rearrange("p a t c -> p (a t c)").rearrange("p (s w) -> p s w", s=8)
        rl = pT[:, 0:4, :]
        bufs = {n: mix(n, [P, 4, SEQ]) for n in ("fq", "fk", "mq", "mk", "dq", "dk")}
        bufs |= {n: mix(n, [P, NT, W1]) for n in ("fv", "mv", "dv", "z")}
        iqk = mix("iqk", [P, 3, SEQ])
        o = y
        hid = gates
        isc = mix("isc", [P, SEQ])
        pen = mix("pen", [P, SEQ], BF16)
        mixer.close()
        whi, wlo = (sb(n, [P, HALVES, HALF], F32R) for n in ("whi", "wlo"))
        hhi, hlo = (sb(n, [P, HALVES, 2 * SEQ], F32R) for n in ("hhi", "hlo"))
        nhi, nlo = (sb(n, [P, KD, SEQ], F32R) for n in ("nhi", "nlo"))
        ffg = sb("ffg", [P, 2, 2 * SEQ])
        bufs.update(xbc=xbcp[:, :, 3:SEQ + 3], iqk=iqk, dt=dtff[:, :, 0:8], ff=dtff[:, :, 8:16], iw=iw)

        con1_in = sem("con1_in")
        par_in, small_in, gpost_in = sem("par_in"), sem("small_in"), sem("gpost_in")
        landed = [sem(f"landed{i}") for i in range(RING)]
        hi_ok, lo_ok = sem("hi_ok"), sem("lo_ok")
        half_used = sem("half_used")
        hi1_ok, lo1_ok, half1_used = sem("hi1_ok"), sem("lo1_ok"), sem("half1_used")
        nhi1_ok, nlo1_ok = sem("nhi1_ok"), sem("nlo1_ok")
        nlo_ok = sem("nlo_ok")
        full, free = sem("full"), sem("free")
        par_ps, par_ok = sem("par_ps"), sem("par_ok")
        ssq_ok, msq_ok, rstd_ok = sem("ssq_ok"), sem("msq_ok"), sem("rstd_ok")
        xn_ok, x_ok = sem("xn_ok"), sem("x_ok")
        conv_ok, silu_ok, init_ok = sem("conv_ok"), sem("silu_ok"), sem("init_ok")
        spv, spe = sem("spv"), sem("spe")
        rope_ps, rope_ok = sem("rope_ps"), sem("rope_ok")
        lcat_ok, cum_ps, cum_ok = sem("lcat_ok"), sem("cum_ps"), sem("cum_ok")
        cb_ps, cb_ok, xs_ps, xs_ok = sem("cb_ps"), sem("cb_ok"), sem("xs_ps"), sem("xs_ok")
        dec_ps, dec_ok, sc_ok = sem("dec_ps"), sem("dec_ok"), sem("sc_ok")
        y_ps, y_free, yt_ok, yt_ps, yt_out = sem("y_ps"), sem("y_free"), sem("yt_ok"), sem("yt_ps"), sem("yt_out")
        zs_ok = sem("zs_ok")
        ix_ps, ix_rl, pen_ok = sem("ix_ps"), sem("ix_rl"), sem("pen_ok")
        qk_ps, mx_ok, ex_ok, pt_ps = sem("qk_ps"), sem("mx_ok"), sem("ex_ok"), sem("pt_ps")
        pt_a, pt_v, o_ps, o_ok, ot_ps, ot_ok = (sem(n) for n in ("pt_a", "pt_v", "o_ps", "o_ok", "ot_ps", "ot_ok"))
        sig_ok, pr_ps, pr_free, mg_ok = sem("sig_ok"), sem("pr_ps"), sem("pr_free"), sem("mg_ok")
        mix_ok = sem("mix_ok")
        fg_free, fu_free = sem("fg_free"), sem("fu_free")
        dn_ps, dn_ok = sem("dn_ps"), sem("dn_ok")
        dch = sem("dch")

        def cols(src, l, c, n):
            return src[bass.ds(l, 1), :, c:c + n].rearrange("a (k p) c -> p (a k) c", p=P)

        def rows(src, l, r, k):
            return src[bass.ds(l, 1), r:r + k * P, :].rearrange("a (k p) c -> p (a k) c", p=P)

        chunks = [(8, n, [lambda l, c=c, n=n: (0, cols(a["w_in"], l, c, n))]) for c, n, _ in IN1]
        N_IN = len(IN1)
        chunks += [(8, 512, [lambda l, c=c: (0, cols(a["w_gate"], l, 512 * c, 512))]) for c in range(8)]
        chunks += [(4, D, [lambda l, n=n: (0, a["w_branch"][bass.ds(l, 1), n].rearrange(
            "a (k p) c -> p (a k) c", p=P))]) for n in range(4)]
        chunks += [(8, 512, [lambda l, c=c: (0, cols(a["w_out"], l, 512 * c, 512))]) for c in range(2)]
        chunks += [(8, 512, [lambda l, c=c: (0, cols(a["w_ffn_in"], l, 256 * c, 256)),
                             lambda l, c=c: (256, cols(a["w_ffn_in"], l, HID1 + 256 * c, 256))])
                   for c in range(HID1 // 256)]
        DOWN = [(4 * c, min(4, KH1 - 4 * c)) for c in range((KH1 + 3) // 4)]
        chunks += [(k, D, [lambda l, r=r, k=k: (0, rows(a["w_ffn_out"], l, r * P, k))]) for r, k in DOWN]
        W = Weights(chunks)
        C_GATE, C_BR, C_OUT, C_FIN = N_IN, N_IN + 8, N_IN + 12, N_IN + 14
        C_FOUT = C_FIN + HID1 // 256

        def chunk(w):
            k, c, _ = chunks[w]
            return ring[:, w % RING, 0:k * c].rearrange("p (k c) -> p k c", c=c)

        in_units = [units_of(p) for _, _, p in IN1]
        U_X = 4
        U_IN = [U_X + sum(len(u) for u in in_units[:i]) for i in range(N_IN + 1)]
        U_GATE = U_IN[-1]
        U_OUT = U_GATE + 16
        U_X2 = U_OUT + 4
        ATT = [("fq", "fk", "fv", 1), ("mq", "mk", "mv", 2), ("dq", "dk", "dv", 3)]
        L = ps[:, 4:8, :].rearrange("p b (s w) -> p (b s) w", s=2)

        def head(s):
            return (s % 4) * 2 + s // 4

        read = [(full, U_IN[i + 1]) if any(u[0] == "I" for u in in_units[i]) else (lo1_ok, 2 * i + 2)
                for i in range(N_IN)]
        read += [(full, U_GATE + 2 * c + 2) for c in range(8)]
        read += [(pr_ps, 4 * n + 4) for n in range(4)]
        read += [(full, U_OUT + 2 * c + 2) for c in range(2)]
        read += [(lo_ok, 2 * c + 2) for c in range(HID1 // 256 + len(DOWN) - 1)]
        N_FIN = 2 * (HID1 // 256)
        N_HALF = N_FIN + KH1 // 2

        def units_in(i, j):
            return [(U_IN[i] + n, kind, 0 if kind == "T" else c - 256 * j, size, name, at)
                    for n, (kind, c, size, name, at) in enumerate(in_units[i])
                    if kind == "T" or min(c // 256, 1) == j]

        used1, n_open = [], 0
        for i in range(N_IN):
            n_first = sum(kind != "T" for _, kind, *_ in units_in(i, 0))
            if n_first:
                used1.append((full, U_IN[i] + n_first))
            else:
                n_open += 1
                used1.append((half1_used, n_open))
            used1.append((full, U_IN[i + 1]))

        def half1_source(h):
            i, j = h // 2, h % 2
            return chunk(i)[:, :, 256 * j:min(chunks[i][1], 256 + 264 * j)]

        def half1_of(buf, h):
            n = half1_source(h).shape[2]
            return buf[:, h % HALVES, 0:8 * n].rearrange("p (k c) -> p k c", k=8)

        def half_source(h):
            wt = chunk(C_FIN + h // 2)
            return wt[:, :, 256 * (h % 2):256 * (h % 2) + 256] if h < N_FIN else wt[:, 2 * (h % 2):2 * (h % 2) + 2, :]

        def half_of(buf, h):
            return buf[:, h % HALVES, :].rearrange("p (k c) -> p k c", k=8 if h < N_FIN else 2)

        def hidden_of(buf, i):
            return buf[:, i % HALVES, :].rearrange("p (k c) -> p k c", k=2)

        with nc.Block() as block:

            @block.sync
            def _(sp_):
                sp_.dma_start(con1[:, :], a["constants_1"]).then_inc(con1_in, 16)
                sp_.wait_ge(con1_in, 16)

        with nc.Fori(0, DEPTH) as l:
            with nc.Block() as block:

                @block.sync
                def _(sp_):
                    row = 0
                    for name, n in (("norm_mix_pre", 8), ("conv_w", 32), ("conv_b", 8), ("ssm_norm", 4),
                                    ("b_gate", 32), ("norm_ffn_pre", 8)):
                        src = a[name][bass.ds(l, 1)]
                        src = src.rearrange("a j (k p) -> (a j k) p", p=P) if name == "conv_w" else \
                            src.rearrange("a (k p) -> (a k) p", p=P)
                        sp_.dma_start(par[row:row + n, :], src).then_inc(par_in, 16)
                        row += n
                    for i, name in enumerate(("dt_bias", "a_log", "d_skip", "fox_fbias")):
                        sp_.dma_start(small[:, i, :], a[name][bass.ds(l, 1)].broadcast_to([P, 8])
                                      ).then_inc(small_in, 16)
                    for w, (k, c, sources) in enumerate(chunks):
                        if w >= RING:
                            sp_.wait_ge(*read[w - RING])
                        if w == C_BR:
                            sp_.wait_ge(y_ps, 1)
                            for i, name in enumerate(("norm_mix_post", "norm_ffn_post")):
                                sp_.dma_start(gpost[:, i, :], a[name][bass.ds(l, 1)].broadcast_to([P, D])
                                              ).then_inc(gpost_in, 16)
                        for source in sources:
                            at, src = source(l)
                            sp_.dma_start(chunk(w)[:, :, at:at + src.shape[2]], src).then_inc(landed[w % RING], 16)

                @block.tensor
                def _(pe):
                    def bank(u):
                        if u >= 2:
                            pe.wait_ge(free, u - 1)
                        return ps[:, u % 2, :]

                    def take(w):
                        pe.wait_ge(landed[w % RING], W.ready[w])

                    def transposed(u0, n):
                        pe.wait_ge(xn_ok, n)
                        for k in range(KD):
                            if n == 2 and k in (4, 6):
                                pe.wait_ge(nlo_ok, k // 2 - 1)
                            if k % 2 == 0:
                                b = bank(u0 + k // 2)
                            for t in range(NT):
                                mm = nc.tensor.transpose(b[:, (k % 2) * SEQ + t * P:(k % 2) * SEQ + (t + 1) * P],
                                                         xm[:, t, k * P:(k + 1) * P], ident)
                            if k % 2:
                                mm.then_inc(full, 1)

                    def feature_unit(out, w, c, nb, act):
                        wt = chunk(w)
                        K = chunks[w][0]
                        for b in range(nb):
                            for k in range(K):
                                mm = nc.tensor.matmul(out[:, b * SEQ:(b + 1) * SEQ], wt[:, k, c + b * P:c + (b + 1) * P],
                                                      act[:, k, :], start=k == 0, stop=k == K - 1)
                        return mm

                    def token_unit(out, w, c, n, t, act):
                        wt = chunk(w)
                        K = chunks[w][0]
                        for k in range(K):
                            mm = nc.tensor.matmul(out, act[:, k, t * P:(t + 1) * P], wt[:, k, c:c + n],
                                                  start=k == 0, stop=k == K - 1)
                        return mm

                    def in_chunk(i):
                        for j in range(2):
                            pe.wait_ge(lo1_ok, 2 * i + j + 1)
                            hi, lo = half1_of(whi1, 2 * i + j), half1_of(wlo1, 2 * i + j)
                            passes = [(lo, nhi1), (hi, nlo1), (hi, nhi1)]
                            for u, kind, c, size, _, at in units_in(i, j):
                                b = ps[:, u % 2, :] if kind == "T" and j else bank(u)
                                products = []
                                if kind == "F":
                                    for m in range(size):
                                        products.append((b[:, m * SEQ:(m + 1) * SEQ], lambda w, x_, k, m=m: (
                                            w[:, k, c + m * P:c + (m + 1) * P], x_[:, k, :])))
                                elif kind == "I":
                                    take(i)
                                    for half in range(2):
                                        for k in range(KD):
                                            mm = nc.tensor.matmul(b[64 * half:64 * half + 64, 0:SEQ],
                                                                  chunk(i)[:, k, 256 + c:256 + c + 64], hT[:, k, :],
                                                                  start=k == 0, stop=k == KD - 1)
                                elif kind == "T":
                                    products.append((b[:, 256 * j:256 * j + 256], lambda w, x_, k: (
                                        x_[:, k, at * P:(at + 1) * P], w[:, k, 0:256])))
                                else:
                                    for t in range(NT):
                                        products.append((b[:, t * size:(t + 1) * size], lambda w, x_, k, t=t: (
                                            x_[:, k, t * P:(t + 1) * P], w[:, k, c:c + size])))
                                for out, operands in products:
                                    for k in range(KD):
                                        for n, (w, x_) in enumerate(passes):
                                            mm = nc.tensor.matmul(out, *operands(w, x_, k), start=k == 0 and n == 0,
                                                                  stop=k == KD - 1 and n == 2)
                                if kind != "T" or j:
                                    mm.then_inc(full, 1)
                            if j == 0 and used1[2 * i][0] is half1_used:
                                mm.then_inc(half1_used, 1)

                    def gate_unit(g):
                        w = C_GATE + g // 2
                        if g % 2 == 0:
                            take(w)
                        feature_unit(bank(U_GATE + g), w, (g % 2) * SEQ, 2, hT).then_inc(full, 1)

                    def rope(r):
                        name = ROPES[r]
                        nb = 3 if name == "iqk" else 4
                        i = [j for j in range(N_IN) if any(p[3] == name for p in IN1[j][2])][0]
                        pe.wait_ge(free, U_IN[i + 1] - (1 if name == "iqk" else 0))
                        if r >= 2:
                            pe.wait_ge(rope_ok, r - 1)
                        for b in range(nb):
                            mm = nc.tensor.matmul(ps[:, 4 + 2 * (r % 2) + b // 2, (b % 2) * SEQ:(b % 2 + 1) * SEQ], rot,
                                                  bufs[name][:, b, :], start=True, stop=True)
                        mm.then_inc(rope_ps, 1)

                    def qk(n):
                        q, k, _, _ = ATT[n // 2]
                        qt = n % 2
                        w = P * (qt + 1)
                        if n == 0:
                            pe.wait_ge(dec_ok, 2)
                        else:
                            pe.wait_ge(pt_a, n)
                            pe.wait_ge(pt_v, n)
                        if n == 4:
                            pe.wait_ge(rope_ok, 5)
                        if n == 2:
                            pe.wait_ge(rope_ok, 2)
                        if n >= 4:
                            pe.wait_ge(ix_rl, n - 3)
                            pe.wait_ge(pen_ok, n - 3)
                        for s in range(8):
                            h = head(s)
                            base, blk = 64 * (h % 2), h // 2
                            nc.tensor.matmul(L[:, s, 0:w], bufs[q][base:base + 64, blk, qt * P:(qt + 1) * P],
                                             bufs[k][base:base + 64, blk, 0:w], start=True, stop=False)
                            if n < 2:
                                nc.tensor.matmul(L[:, s, 0:w], column(nident[:, 8 + h:9 + h], P), cumT[:, 0:w],
                                                 start=False, stop=False)
                                nc.tensor.matmul(L[:, s, 0:w], cumT[:, qt * P:(qt + 1) * P],
                                                 column(ident[0:16, 8 + h:9 + h], w), start=False, stop=False)
                            if n >= 4:
                                nc.tensor.matmul(L[:, s, 0:w], ident_bf, pen[:, 0:w], start=False, stop=False)
                            mm = nc.tensor.matmul(L[:, s, w - P:w], ident_bf, maskQ_bf, start=False, stop=True)
                        mm.then_inc(qk_ps, 1)

                    def p_turn(n):
                        pe.wait_ge(ex_ok, n + 1)
                        for s in range(8):
                            for kt in range(n % 2 + 1):
                                mm = nc.tensor.transpose(L[:, s, kt * P:(kt + 1) * P], probs[:, s, kt * P:(kt + 1) * P],
                                                         ident)
                        mm.then_inc(pt_ps, 1)

                    def pv(n):
                        pe.wait_ge(pt_a, n + 1)
                        pe.wait_ge(pt_v, n + 1)
                        if n == 0:
                            pe.wait_ge(y_free, 1)
                        else:
                            pe.wait_ge(o_ok, n)
                        v = bufs[ATT[n // 2][2]]
                        for s in range(8):
                            h = head(s)
                            for kt in range(n % 2 + 1):
                                mm = nc.tensor.matmul(ps[:, 2, h * 64:(h + 1) * 64], pT[:, s, kt * P:(kt + 1) * P],
                                                      v[:, kt, h * 64:(h + 1) * 64], start=kt == 0, stop=kt == n % 2)
                        mm.then_inc(o_ps, 1)

                    def o_turn(n):
                        pe.wait_ge(o_ok, n + 1)
                        if n == 0:
                            pe.wait_ge(yt_out, 2)
                        else:
                            pe.wait_ge(ot_ok, n)
                        for b in range(4):
                            mm = nc.tensor.transpose(ps[:, 3, b * P:(b + 1) * P], o[:, n % 2, b * P:(b + 1) * P], ident)
                        mm.then_inc(ot_ps, 1)

                    def index_scores(t):
                        pe.wait_ge(rope_ok, 5)
                        pe.wait_ge(pt_a, 4 + t)
                        pe.wait_ge(pt_v, 4 + t)
                        w = P * (t + 1)
                        for h in range(4):
                            base = 64 * (h % 2)
                            s = 4 * (h % 2) + h // 2
                            mm = nc.tensor.matmul(L[:, s, 0:w], iqk[base:base + 64, h // 2, t * P:(t + 1) * P],
                                                  iqk[base:base + 64, 2, 0:w], start=True, stop=True)
                        mm.then_inc(ix_ps, 1)

                    pe.wait_ge(par_in, 96)
                    nc.tensor.transpose(ps[:, 2, 0:NPAR1], par[:, :], ident[0:NPAR1, 0:NPAR1]).then_inc(par_ps, 1)
                    transposed(0, 1)
                    pe.wait_ge(free, U_X)
                    pe.wait_ge(nlo1_ok, 2)
                    for i in range(N_IN):
                        in_chunk(i)
                        if 5 <= i < 10:
                            rope(i - 5)
                    pe.wait_ge(lcat_ok, 1)
                    for t in range(NT):
                        nc.tensor.matmul(ps[0:16, 2, 0:SEQ], lcat[:, t, :], tri[:, t, :], start=t == 0, stop=t == NT - 1)
                    for t in range(NT):
                        for u in range(t + 1):
                            mm = nc.tensor.matmul(ps[:, 3, t * 16:(t + 1) * 16], tri[:, u, t * P:(t + 1) * P],
                                                  lcat[:, u, :], start=u == 0, stop=u == t)
                    mm.then_inc(cum_ps, 1)
                    gate_unit(0)
                    pe.wait_ge(cum_ok, 1)
                    pe.wait_ge(silu_ok, 1)
                    for g in range(2):
                        nc.tensor.matmul(ps[:, 2 + g, 0:SEQ], xbc[:, 4 + g, 0:P], xbc[:, 6 + g, :], start=True, stop=True)
                        mm = nc.tensor.matmul(ps[:, 2 + g, SEQ:384], xbc[:, 4 + g, P:SEQ], xbc[:, 6 + g, P:SEQ],
                                              start=True, stop=True)
                    mm.then_inc(cb_ps, 1)
                    pe.wait_ge(rope_ok, 5)
                    for t in range(NT):
                        for b in range(4):
                            mm = nc.tensor.transpose(ps[:, 4 + t, b * P:(b + 1) * P], xbc[:, b, t * P:(t + 1) * P], ident)
                    mm.then_inc(xs_ps, 1)
                    gate_unit(1)
                    for r in range(2):
                        if r == 0:
                            pe.wait_ge(xs_ok, 1)
                        else:
                            pe.wait_ge(dec_ok, 1)
                        for j in range(4):
                            h = 4 * r + j
                            pick = column(ident[0:16, h:h + 1], P)
                            b = ps[:, 4 + j, :]
                            nc.tensor.matmul(b[:, 0:SEQ], pick, cumT[:, :], start=True, stop=False)
                            nc.tensor.matmul(b[:, 0:P], ident_bf, maskT_bf, start=False, stop=True)
                            nc.tensor.matmul(b[:, SEQ:384], pick, cumT[:, P:SEQ], start=True, stop=False)
                            mm = nc.tensor.matmul(b[:, SEQ:384], ident_bf, maskT_bf, start=False, stop=True)
                        mm.then_inc(dec_ps, 1)
                        if r == 0:
                            gate_unit(2)
                    gate_unit(3)
                    pe.wait_ge(cb_ok, 1)
                    pe.wait_ge(sc_ok, 2)
                    for t in range(NT):
                        for h in range(8):
                            for s in range(t + 1):
                                c = (t * P) if s == 0 else SEQ
                                mm = nc.tensor.matmul(ps[:, 2 + t, h * 64:(h + 1) * 64], sc8[:, h, c:c + P],
                                                      xd[:, 0, s, h * 64:(h + 1) * 64], start=s == 0, stop=s == t)
                    mm.then_inc(y_ps, 1)
                    qk(0)
                    gate_unit(4)
                    for t in range(NT):
                        pe.wait_ge(yt_ok, 1)
                        pe.wait_ge(y_free, 1)
                        if t:
                            pe.wait_ge(yt_out, t)
                        for b in range(4):
                            mm = nc.tensor.transpose(ps[:, 3, b * P:(b + 1) * P], y[:, t, b * P:(b + 1) * P], ident)
                        mm.then_inc(yt_ps, 1)
                    pe_g = [5]

                    def gate():
                        if pe_g[0] < 16:
                            gate_unit(pe_g[0])
                            pe_g[0] += 1
                    p_turn(0)
                    for n in range(6):
                        gate()
                        pv(n)
                        if n + 1 < 6:
                            if n + 1 >= 4:
                                index_scores(n - 3)
                                gate()
                            qk(n + 1)
                            gate()
                        o_turn(n)
                        if n + 1 < 6:
                            p_turn(n + 1)
                    while pe_g[0] < 16:
                        gate()
                    for n in range(4):
                        take(C_BR + n)
                        if n:
                            pe.wait_ge(ot_ok, 2 * n)
                        for m in range(4):
                            i = 4 * n + m
                            if i == 0:
                                pe.wait_ge(pt_a, 6)
                                pe.wait_ge(pt_v, 6)
                                pe.wait_ge(yt_out, 2)
                            if i >= 4:
                                pe.wait_ge(pr_free, i - 3)
                            mm = feature_unit(ps[:, 4 + i % 4, :], C_BR + n, m * SEQ, 2, ys[:, n, :, :])
                            mm.then_inc(pr_ps, 1)
                    pe.wait_ge(mg_ok, 12)
                    for c in range(2):
                        take(C_OUT + c)
                        for t in range(NT):
                            token_unit(bank(U_OUT + 2 * c + t), C_OUT + c, 0, 512, t, merged).then_inc(full, 1)
                    transposed(U_X2, 2)
                    pe.wait_ge(nlo_ok, 4)
                    pe.wait_ge(pr_free, 16)
                    for h in range(N_FIN):
                        c = h // 2
                        if c >= 2:
                            pe.wait_ge(fu_free if h % 2 else fg_free, c - 1)
                        pe.wait_ge(lo_ok, h + 1)
                        hi, lo = half_of(whi, h), half_of(wlo, h)
                        for b in range(2):
                            out = ps[:, 2 + 2 * (h % 2) + c % 2, b * SEQ:(b + 1) * SEQ]
                            for k in range(KD):
                                for j, (wt, act) in enumerate(((lo, nhi), (hi, nlo), (hi, nhi))):
                                    mm = nc.tensor.matmul(out, wt[:, k, b * P:(b + 1) * P], act[:, k, :],
                                                          start=k == 0 and j == 0, stop=k == KD - 1 and j == 2)
                            if b == 1:
                                mm.then_inc(half_used, 1)
                    for i in range(N_HALF - N_FIN):
                        pe.wait_ge(lo_ok, N_FIN + i + 1)
                        hi, lo = half_of(whi, N_FIN + i), half_of(wlo, N_FIN + i)
                        for kk in range(2):
                            for t in range(NT):
                                for half in range(2):
                                    b = (0, 1, 6, 7)[2 * t + half]
                                    first, last = i + kk == 0, 2 * i + kk == KH1 - 1
                                    for j, (act, wt) in enumerate(((hlo, hi), (hhi, lo), (hhi, hi))):
                                        mm = nc.tensor.matmul(ps[:, b, :], hidden_of(act, i)[:, kk, t * P:(t + 1) * P],
                                                              wt[:, kk, half * 512:(half + 1) * 512],
                                                              start=first and j == 0, stop=last and j == 2)
                                    if last:
                                        mm.then_inc(dn_ps, 1)
                        if i < N_HALF - N_FIN - 1:
                            mm.then_inc(half_used, 1)

                @block.scalar
                def _(act):
                    marks = {}

                    def mark(s, ins):
                        marks[s.name] = marks.get(s.name, 0) + 1
                        ins.then_inc(s, 1)
                        act.wait_ge(s, marks[s.name])

                    def empty(u):
                        act.wait_ge(full, u + 1)
                        return ps[:, u % 2, :]

                    def squares(e):
                        for t in range(NT):
                            src = x if e in (0, 3) else xm
                            i = nc.scalar.activation(hT[:, 4 * t:4 * t + 4, :].rearrange("p a b -> p (a b)"),
                                                     src[:, t, :], ACT.Square, accum_out=ssq[:, e, t:t + 1])
                        mark(ssq_ok, i)

                    def turned(u0, gain):
                        for k in range(KD):
                            b = empty(u0 + k // 2)
                            i = nc.scalar.activation(hT[:, k, :], b[:, (k % 2) * SEQ:(k % 2 + 1) * SEQ], ACT.Copy,
                                                     scale=parT[:, gain + k:gain + k + 1])
                            if k % 2:
                                mark(free, i)

                    def in_half(h):
                        for u, kind, _, size, name, at in units_in(h // 2, h % 2):
                            if kind == "T" and h % 2 == 0:
                                continue
                            b = empty(u)
                            dst = bufs[name]
                            if kind in "FI":
                                ins = nc.scalar.activation(dst[:, at:at + size, :], b[:, 0:size * SEQ].rearrange(
                                    "p (a b) -> p a b", a=size), ACT.Copy, scale=QSCALE.get(name, 1.0))
                            elif kind == "T":
                                ins = nc.scalar.copy(dst[:, at, :], b[:, 0:size])
                            else:
                                ins = nc.scalar.copy(dst, b[:, 0:NT * size].rearrange("p (t c) -> p t c", t=NT))
                            mark(free, ins)

                    def split1(h):
                        if h >= HALVES:
                            act.wait_ge(*used1[h - HALVES])
                        act.wait_ge(landed[h // 2 % RING], W.ready[h // 2])
                        mark(hi1_ok, nc.scalar.copy(half1_of(whi1, h), half1_source(h)))

                    def gate_unit(g):
                        b = empty(U_GATE + g)
                        for j in range(2):
                            k = 2 * g + j
                            i = nc.scalar.activation(gates[:, k, :], b[:, j * SEQ:(j + 1) * SEQ], ACT.Identity,
                                                     bias=parT[:, PBG + k:PBG + k + 1])
                        mark(free, i)

                    def exps(n):
                        w = P * (n % 2 + 1)
                        act.wait_ge(mx_ok, n + 1)
                        if n >= 1:
                            act.wait_ge(pt_ps, n)
                        if n >= 2:
                            act.wait_ge(o_ok, n - 1)
                        for s in range(8):
                            i = nc.scalar.activation(probs[:, s, 0:w], L[:, s, 0:w], ACT.Exp,
                                                     bias=nmx[:, n % 2, s:s + 1], accum_out=rsum[:, n % 2, s:s + 1])
                        mark(ex_ok, i)

                    def p_out(n):
                        w = P * (n % 2 + 1)
                        act.wait_ge(pt_ps, n + 1)
                        if n >= 1:
                            act.wait_ge(o_ps, n)
                        mark(pt_a, nc.scalar.copy(pT[:, 0:4, 0:w], L[:, 0:4, 0:w]))

                    def o_out(n):
                        act.wait_ge(ot_ps, n + 1)
                        t = n % 2
                        mark(ot_ok, nc.scalar.copy(ys[:, ATT[n // 2][3], :, t * P:(t + 1) * P],
                                       ps[:, 3, :].rearrange("p (b c) -> p b c", b=4)))

                    def relus(t):
                        act.wait_ge(ix_ps, t + 1)
                        act.wait_ge(o_ps, 4 + t)
                        w = P * (t + 1)
                        for h in range(4):
                            i = nc.scalar.activation(rl[:, h, 0:w], L[:, 4 * (h % 2) + h // 2, 0:w], ACT.Relu,
                                                     scale=64 ** -0.5)
                        mark(ix_rl, i)

                    squares(0)
                    split1(0)
                    act.wait_ge(par_ok, 1)
                    turned(0, PGM)
                    for i in range(2):
                        mark(nhi1_ok, nc.scalar.copy(nhi1[:, 4 * i:4 * i + 4, :], hT[:, 4 * i:4 * i + 4, :]))
                    act.wait_ge(init_ok, 1)
                    for h in range(1, HALVES):
                        split1(h)
                    for h in range(2 * N_IN):
                        in_half(h)
                        if h + HALVES < 2 * N_IN:
                            split1(h + HALVES)
                        if h == 10:
                            act.wait_ge(conv_ok, 1)
                            mark(silu_ok, nc.scalar.activation(xbc[:, :, :], xbc[:, :, :], ACT.Silu))
                        if h == 11:
                            act.wait_ge(spv, 1)
                            mark(spe, nc.scalar.activation(sp[:, 2, :], sp[:, 1, :], ACT.Exp, scale=-1.0))
                            act.wait_ge(small_in, 64)
                            mark(spe, nc.scalar.activation(asg[:, 0:8], small[:, 1, :], ACT.Exp))
                        if h == 13:
                            act.wait_ge(spv, 2)
                            mark(spe, nc.scalar.activation(sp[:, 4, :], sp[:, 3, :], ACT.Ln))
                    mark(zs_ok, nc.scalar.activation(bufs["z"][:, :, :], bufs["z"][:, :, :], ACT.Silu))
                    gate_unit(0)
                    act.wait_ge(cb_ps, 1)
                    mark(cb_ok, nc.scalar.copy(cb[:, :, :], ps[:, 2:4, 0:384]))
                    gate_unit(1)
                    act.wait_ge(rope_ok, 5)
                    for r in range(2):
                        act.wait_ge(dec_ps, r + 1)
                        for j in range(4):
                            h = 4 * r + j
                            nc.scalar.activation(sc8[:, h, 0:SEQ], ps[:, 4 + j, 0:SEQ], ACT.Exp,
                                                 bias=ncum[:, 0, h:h + 1])
                            i = nc.scalar.activation(sc8[:, h, SEQ:384], ps[:, 4 + j, SEQ:384], ACT.Exp,
                                                     bias=ncum[:, 1, h:h + 1])
                        mark(dec_ok, i)
                        gate_unit(2 + r)
                    gate_unit(4)
                    for t in range(NT):
                        act.wait_ge(yt_ps, t + 1)
                        for b in range(4):
                            i = nc.scalar.activation(ys[:, 0, b, t * P:(t + 1) * P], ps[:, 3, b * P:(b + 1) * P],
                                                     ACT.Copy, scale=parT[:, PSN + b:PSN + b + 1])
                        mark(yt_out, i)
                    act_g = [5]

                    def gate():
                        if act_g[0] < 16:
                            gate_unit(act_g[0])
                            act_g[0] += 1
                    exps(0)
                    p_out(0)
                    for n in range(6):
                        gate()
                        if n + 1 < 6:
                            if n + 1 >= 4:
                                relus(n - 3)
                                gate()
                            gate()
                            exps(n + 1)
                        o_out(n)
                        if n + 1 < 6:
                            p_out(n + 1)
                    while act_g[0] < 16:
                        gate()
                    for g in range(4):
                        i = nc.scalar.activation(gates[:, 8 * g:8 * g + 8, :], gates[:, 8 * g:8 * g + 8, :],
                                                 ACT.Sigmoid)
                        mark(sig_ok, i)
                    for c in range(2):
                        for t in range(NT):
                            i = nc.scalar.copy(xm[:, t, c * 512:(c + 1) * 512], empty(U_OUT + 2 * c + t))
                            mark(free, i)
                    act.wait_ge(free, U_OUT + 4)
                    squares(2)

                    def split(h):
                        if h >= HALVES:
                            act.wait_ge(half_used, h - HALVES + 1)
                        act.wait_ge(landed[(C_FIN + h // 2) % RING], W.ready[C_FIN + h // 2])
                        if h >= N_FIN:
                            i = h - N_FIN
                            act.wait_ge(fu_free, i + 1)
                            nc.scalar.copy(hidden_of(hhi, i), hid[:, 2 * i:2 * i + 2, :])
                        mark(hi_ok, nc.scalar.copy(half_of(whi, h), half_source(h)))

                    for h in range(HALVES):
                        split(h)
                    act.wait_ge(x_ok, 1)
                    squares(3)
                    for k in range(KD):
                        b = empty(U_X2 + k // 2)
                        i = nc.scalar.activation(nhi[:, k, :], b[:, (k % 2) * SEQ:(k % 2 + 1) * SEQ], ACT.Copy,
                                                 scale=parT[:, PGF + k:PGF + k + 1])
                        if k % 2:
                            mark(free, i)
                    for h in range(N_FIN):
                        if h % 2 == 0:
                            c = h // 2
                            act.wait_ge(half_used, h + 1)
                            if c >= 2:
                                act.wait_ge(fu_free, c - 1)
                            mark(fg_free, nc.scalar.activation(ffg[:, c % 2, :], ps[:, 2 + c % 2, :], ACT.Silu))
                        split(h + HALVES)
                    for h in range(N_FIN + HALVES, N_HALF):
                        split(h)
                    for t in range(NT):
                        for half in range(2):
                            act.wait_ge(dn_ps, 2 * t + half + 1)
                            mark(dn_ok, nc.scalar.copy(xm[:, t, half * 512:(half + 1) * 512],
                                           ps[:, (0, 1, 6, 7)[2 * t + half], :]))
                    act.wait_ge(dn_ok, 4)
                    squares(4)

                @block.vector
                def _(dve):
                    n_chain = [0]

                    def link(ins):
                        n_chain[0] += 1
                        ins.then_inc(dch, 1)
                        dve.wait_ge(dch, n_chain[0])

                    V = nc.vector
                    marks = {}

                    def mark(s, ins):
                        marks[s.name] = marks.get(s.name, 0) + 1
                        ins.then_inc(s, 1)
                        dve.wait_ge(s, marks[s.name])

                    def mean_square(e, n, width):
                        mark(msq_ok, V.tensor_scalar(msq[:, e, 0:n], ssq[:, e, 0:n], 1.0 / width, EPS, ALU.mult, ALU.add
                                        ))

                    def norm_in(e):
                        dve.wait_ge(ssq_ok, max(e, 1))
                        mean_square(e, 2, D)
                        dve.wait_ge(rstd_ok, e + 1)
                        for t in range(NT):
                            i = V.tensor_scalar(xm[:, t, :], x[:, t, :], rstd[:, e, t:t + 1], None, ALU.mult)
                        mark(xn_ok, i)

                    def norm_out(e, gain):
                        dve.wait_ge(ssq_ok, max(e, 1))
                        mean_square(e, 2, D)
                        dve.wait_ge(rstd_ok, e + 1)
                        for t in range(NT):
                            link(V.scalar_tensor_tensor(xm[:, t, :], xm[:, t, :], rstd[:, e, t:t + 1], gain,
                                                        ALU.mult, ALU.mult))
                        for t in range(NT):
                            i = V.tensor_tensor(x[:, t, :], x[:, t, :], xm[:, t, :], ALU.add)
                        mark(x_ok, i)

                    def rope(r):
                        name = ROPES[r]
                        nb = 3 if name == "iqk" else 4
                        t = bufs[name]
                        dve.wait_ge(rope_ps, r + 1)
                        turn = ps[:, 4 + 2 * (r % 2):6 + 2 * (r % 2), :].rearrange("p b (c d) -> p (b c) d", c=2)
                        link(V.tensor_tensor(rt[:, 0:nb, :], turn[:, 0:nb, :],
                                             sin.unsqueeze(1).broadcast_to([P, nb, SEQ]), ALU.mult))
                        link(V.tensor_tensor(rt[:, 4:4 + nb, :], t[:, :, :],
                                             cos.unsqueeze(1).broadcast_to([P, nb, SEQ]), ALU.mult))
                        mark(rope_ok, V.tensor_tensor(t[:, :, :], rt[:, 0:nb, :], rt[:, 4:4 + nb, :], ALU.add))

                    link(V.memset(nhalf[:, :], -0.5))
                    link(V.memset(xbcp[:, :, 0:3], 0.0))
                    link(V.tensor_scalar(nident[:, :], ident[0:16, 0:16], -1.0, None, ALU.mult))
                    mark(init_ok, V.memset(asg[:, 8:16], -1.0))
                    dve.wait_ge(par_ps, 1)
                    mark(par_ok, V.tensor_copy(parT[:, :], ps[:, 2, 0:NPAR1]))
                    norm_in(0)
                    dve.wait_ge(init_ok, 1)
                    dve.wait_ge(par_ok, 1)

                    def split1(h):
                        dve.wait_ge(hi1_ok, h + 1)
                        mark(lo1_ok, V.tensor_tensor(half1_of(wlo1, h), half1_source(h),
                                                     half1_of(whi1, h).bitcast(F32), ALU.subtract))

                    split1(0)
                    dve.wait_ge(full, U_X)
                    for i in range(2):
                        dve.wait_ge(nhi1_ok, i + 1)
                        mark(nlo1_ok, V.tensor_tensor(nlo1[:, 4 * i:4 * i + 4, :], hT[:, 4 * i:4 * i + 4, :],
                                                      nhi1[:, 4 * i:4 * i + 4, :].bitcast(F32), ALU.subtract))
                    for h in range(1, HALVES):
                        split1(h)

                    def convolve(b):
                        if b % 4 == 0:
                            dve.wait_ge(free, U_IN[b // 4] + 2)
                        link(V.tensor_scalar(xbc[:, b, :], xbcp[:, b, 0:SEQ], parT[:, PCW + b:PCW + b + 1],
                                             parT[:, PCB + b:PCB + b + 1], ALU.mult, ALU.add))
                        for j in range(1, 4):
                            ins = V.scalar_tensor_tensor(xbc[:, b, :], xbcp[:, b, j:j + SEQ],
                                                         parT[:, PCW + 8 * j + b:PCW + 8 * j + b + 1],
                                                         xbc[:, b, :], ALU.mult, ALU.add)
                            if b == 7 and j == 3:
                                mark(conv_ok, ins)
                            else:
                                link(ins)

                    spt = sp[:, 5, :].rearrange("p (t c) -> p t c", t=NT)

                    def softplus_1():
                        dve.wait_ge(free, U_IN[3])
                        dve.wait_ge(small_in, 64)
                        v3 = sp[:, 0, :].rearrange("p (t c) -> p t c", t=NT)
                        link(V.tensor_tensor(v3[:, :, 0:8], dtff[:, :, 0:8],
                                             small[:, 0:1, :].broadcast_to([P, NT, 8]), ALU.add))
                        link(V.tensor_tensor(v3[:, :, 8:16], dtff[:, :, 8:16],
                                             small[:, 3:4, :].broadcast_to([P, NT, 8]), ALU.add))
                        link(V.tensor_scalar(v3[:, :, 8:16], v3[:, :, 8:16], -1.0, None, ALU.mult))
                        mark(spv, V.scalar_tensor_tensor(sp[:, 1, :], sp[:, 0, :], -1.0, sp[:, 0, :], ALU.mult, ALU.max))

                    def softplus_2():
                        dve.wait_ge(spe, 1)
                        mark(spv, V.tensor_scalar(sp[:, 3, :], sp[:, 2, :], 1.0, None, ALU.add))

                    def softplus_3():
                        dve.wait_ge(spv, 2)
                        dve.wait_ge(spe, 3)
                        link(V.tensor_scalar(sp[:, 1, :], sp[:, 3, :], -1.0, None, ALU.add))
                        link(V.tensor_tensor(sp[:, 1, :], sp[:, 2, :], sp[:, 1, :], ALU.subtract))
                        link(V.reciprocal(sp[:, 5, :], sp[:, 3, :]))
                        link(V.tensor_tensor(sp[:, 1, :], sp[:, 1, :], sp[:, 5, :], ALU.mult))
                        link(V.tensor_tensor(sp[:, 4, :], sp[:, 4, :], sp[:, 1, :], ALU.add))
                        link(V.scalar_tensor_tensor(sp[:, 5, :], sp[:, 0, :], 0.0, sp[:, 4, :], ALU.max, ALU.add))
                        link(V.tensor_scalar(asg[:, 0:8], asg[:, 0:8], -1.0, None, ALU.mult))
                        mark(lcat_ok, V.tensor_tensor(lcat[:, :, :], spt, asg[:, :].unsqueeze(1).broadcast_to([P, NT, 16]), ALU.mult
                                        ))

                    for h in range(2 * N_IN):
                        if h + HALVES < 2 * N_IN:
                            split1(h + HALVES)
                        if 2 <= h < 10:
                            convolve(h - 2)
                        if h == 10:
                            softplus_1()
                        if h == 12:
                            softplus_2()
                        if h == 14:
                            softplus_3()
                        if h >= 13 and h % 2 and h <= 21:
                            rope((h - 13) // 2)
                    dve.wait_ge(cum_ps, 1)
                    link(V.tensor_copy(cumT[:, :], ps[0:16, 2, 0:SEQ]))
                    mark(cum_ok, V.tensor_scalar(ncum[:, :, :], ps[:, 3, 0:32].rearrange("p (t c) -> p t c", t=NT), -1.0, None,
                                    ALU.mult))
                    dve.wait_ge(xs_ps, 1)
                    xs = ps[:, 4:6, :].rearrange("p t (h c) -> p t h c", h=8)
                    xdt = xd[:, 0, :, :].rearrange("p t (h c) -> p t h c", h=8)
                    xsk = xd[:, 1, :, :].rearrange("p t (h c) -> p t h c", h=8)
                    for t in range(NT):
                        link(V.tensor_tensor(xdt[:, t], xs[:, t],
                                             spt[:, t, 0:8].unsqueeze(2).broadcast_to([P, 8, 64]), ALU.mult))
                        i = V.tensor_tensor(xsk[:, t], xs[:, t],
                                            small[:, 2, :].unsqueeze(2).broadcast_to([P, 8, 64]), ALU.mult)
                        if t == 0:
                            link(i)
                    mark(xs_ok, i)
                    dve.wait_ge(cb_ok, 1)
                    for r in range(2):
                        dve.wait_ge(dec_ok, r + 1)
                        mark(sc_ok, V.tensor_tensor(sc8[:, 4 * r:4 * r + 4, :], sc8[:, 4 * r:4 * r + 4, :],
                                        cb[:, r:r + 1, :].broadcast_to([P, 4, 384]), ALU.mult))
                    dve.wait_ge(y_ps, 1)
                    dve.wait_ge(xs_ok, 1)
                    mark(y_free, V.tensor_tensor(y[:, :, :], ps[:, 2:4, :], xd[:, 1, :, :], ALU.add))
                    dve.wait_ge(y_free, 1)
                    dve.wait_ge(zs_ok, 1)
                    link(V.tensor_tensor(y[:, :, :], y[:, :, :], bufs["z"][:, :, :], ALU.mult))
                    link(V.tensor_tensor(xd[:, 1, :, :], y[:, :, :], y[:, :, :], ALU.mult))
                    link(V.tensor_reduce(ssq[:, 1, :], xd[:, 1, :, :].rearrange("p t (g c) -> p (t g) c", g=2), AX_X,
                                         ALU.add))
                    mean_square(1, 4, 256)
                    dve.wait_ge(rstd_ok, 2)
                    mark(yt_ok, V.tensor_tensor(y[:, :, :].rearrange("p t (g c) -> p (t g) c", g=2),
                                    y[:, :, :].rearrange("p t (g c) -> p (t g) c", g=2),
                                    rstd[:, 1, :].unsqueeze(2).broadcast_to([P, 4, 256]), ALU.mult))

                    def maxima(n):
                        w = P * (n % 2 + 1)
                        dve.wait_ge(qk_ps, n + 1)
                        if n >= 2:
                            dve.wait_ge(ex_ok, n - 1)
                        mark(mx_ok, V.tensor_reduce(nmx[:, n % 2, :], L[:, :, 0:w], AX_X, ALU.max, negate=True))

                    def p_out(n):
                        w = P * (n % 2 + 1)
                        dve.wait_ge(pt_ps, n + 1)
                        if n >= 1:
                            dve.wait_ge(o_ps, n)
                        mark(pt_v, V.tensor_copy(pT[:, 4:8, 0:w], L[:, 4:8, 0:w]))

                    def o_norm(n):
                        dve.wait_ge(ex_ok, n + 1)
                        link(V.reciprocal(rinv[:, :], rsum[:, n % 2, :]))
                        dve.wait_ge(o_ps, n + 1)
                        if n >= 2:
                            dve.wait_ge(ot_ps, n - 1)
                        else:
                            dve.wait_ge(yt_ps, 2)
                        mark(o_ok, V.tensor_tensor(o[:, n % 2, :].rearrange("p (b a c) -> p b a c", a=2, c=64),
                                        ps[:, 2, :].rearrange("p (b a c) -> p b a c", a=2, c=64),
                                        rinv[:, :].rearrange("p (a b) -> p b a", a=2).unsqueeze(3)
                                        .broadcast_to([P, 4, 2, 64]), ALU.mult))

                    def pick(t):
                        w = P * (t + 1)
                        dve.wait_ge(ix_rl, t + 1)
                        if t == 0:
                            link(V.tensor_scalar(iw[:, :, :], iw[:, :, :], 0.5, None, ALU.mult))
                        link(V.tensor_scalar(isc[:, 0:w], rl[:, 0, 0:w], iw[:, t, 0:1], None, ALU.mult))
                        for h in range(1, 4):
                            link(V.scalar_tensor_tensor(isc[:, 0:w], rl[:, h, 0:w], iw[:, t, h:h + 1], isc[:, 0:w],
                                                        ALU.mult, ALU.add))
                        link(V.tensor_tensor(isc[:, w - P:w], isc[:, w - P:w], maskQ, ALU.add))
                        for r in range(8):
                            link(V.max(top8[:, :], isc[:, 0:w]))
                            link(V.match_replace(isc[:, 0:w], top8[:, :], isc[:, 0:w], TAKEN))
                        if t:
                            dve.wait_ge(qk_ps, 5)
                        mark(pen_ok, V.tensor_scalar(pen[:, 0:w], isc[:, 0:w], -2e38, NEG, ALU.is_gt, ALU.mult))

                    maxima(0)
                    p_out(0)
                    for n in range(6):
                        if n + 1 < 6:
                            if n + 1 >= 4:
                                pick(n - 3)
                            if n + 1 < 4:
                                maxima(n + 1)
                        o_norm(n)
                        if n + 1 >= 4 and n + 1 < 6:
                            maxima(n + 1)
                        if n + 1 < 6:
                            p_out(n + 1)
                    for n in range(4):
                        dve.wait_ge(sig_ok, n + 1)
                        for m in range(4):
                            i = 4 * n + m
                            dve.wait_ge(pr_ps, i + 1)
                            src = ps[:, 4 + i % 4, :].rearrange("p (b c) -> p b c", b=2)
                            gt = gates[:, 8 * n + 2 * m:8 * n + 2 * m + 2, :]
                            out, tmp = (z[:, 2 * m:2 * m + 2, :] for z in (merged, probs))
                            if n == 0:
                                mark(pr_free, V.tensor_tensor(out, src, gt, ALU.mult))
                                continue
                            if n > 1:
                                dve.wait_ge(mg_ok, i - 7)
                            mark(pr_free, V.tensor_tensor(tmp, src, gt, ALU.mult))
                            dve.wait_ge(pr_free, i + 1)
                            mark(mg_ok, V.tensor_tensor(out, out, tmp, ALU.add))
                    dve.wait_ge(gpost_in, 32)
                    norm_out(2, gpost[:, 0, :])
                    dve.wait_ge(x_ok, 1)
                    def split(h):
                        dve.wait_ge(hi_ok, h + 1)
                        if h >= N_FIN:
                            i = h - N_FIN
                            V.tensor_tensor(hidden_of(hlo, i), hid[:, 2 * i:2 * i + 2, :],
                                            hidden_of(hhi, i).bitcast(F32), ALU.subtract)
                        mark(lo_ok, V.tensor_tensor(half_of(wlo, h), half_source(h), half_of(whi, h).bitcast(F32),
                                                    ALU.subtract))

                    split(0)
                    norm_in(3)
                    split(1)
                    for k in range(KD):
                        dve.wait_ge(free, U_X2 + k // 2 + 1)
                        i = V.scalar_tensor_tensor(nlo[:, k, :], ps[:, (U_X2 + k // 2) % 2,
                                                                    (k % 2) * SEQ:(k % 2 + 1) * SEQ],
                                                   parT[:, PGF + k:PGF + k + 1], nhi[:, k, :].bitcast(F32),
                                                   ALU.mult, ALU.subtract)
                        if k % 2:
                            mark(nlo_ok, i)
                    for h in range(2, HALVES):
                        split(h)
                    for h in range(N_FIN):
                        if h % 2:
                            c = h // 2
                            dve.wait_ge(fg_free, c + 1)
                            dve.wait_ge(half_used, h + 1)
                            mark(fu_free, V.tensor_tensor(hid[:, 2 * c:2 * c + 2, :],
                                                          ffg[:, c % 2, :].rearrange("p (b c) -> p b c", b=2),
                                                          ps[:, 4 + c % 2, :].rearrange("p (b c) -> p b c", b=2),
                                                          ALU.mult))
                        split(h + HALVES)
                    for h in range(N_FIN + HALVES, N_HALF):
                        split(h)
                    norm_out(4, gpost[:, 1, :])

                @block.gpsimd
                def _(pool):
                    pool.wait_ge(init_ok, 1)
                    for e in range(5):
                        n = 4 if e == 1 else 2
                        pool.wait_ge(msq_ok, e + 1)
                        nc.gpsimd.tensor_tensor(rstd[:, e, 0:n], msq[:, e, 0:n], nhalf[:, 0:n], ALU.pow
                                                ).then_inc(rstd_ok, 1)

            nc.all_engine_barrier()
            for s in sems:
                nc.gpsimd.sem_clear(s)
            nc.all_engine_barrier()


W2 = 256
HID2 = 4096
KH2 = HID2 // P
MLA_D, MLA_NOPE = 96, 64
IN2 = [
    (0, 416, [("T", 0, 256, "cq"), ("T", 256, 128, "ckv"), ("G", 384, 32, "kpe", 64)]),
    (1712, 512, [("F", 0, 2, "dn", 0), ("F", 256, 2, "dn", 2)]),
    (2224, 520, [("F", 0, 2, "dn", 4), ("T", 256, 8, "dab"), ("T", 264, 256, "dz")]),
    (928, 256, [("F", 0, 1, "gqk", 0), ("F", 128, 1, "gqk", 1)]),
    (1184, 528, [("T", 0, 256, "gv"), ("G", 256, 16, "glr", 0), ("T", 272, 256, "gog")]),
    (416, 512, [("T", 0, 512, "uv")]),
]
GATE2 = 2744
QM, QX, QE, QL, QQ, QK, QS, QC, NPAR2 = 0, 8, 16, 24, 32, 34, 35, 39, 63
TWO_PI = 2 * np.pi
PI_A = 6.28125
PI_B = float(np.float32(np.float16(TWO_PI - PI_A)))
PI_C = float(np.float32(TWO_PI - PI_A - PI_B))
ROUND = 1.5 * 2.0 ** 23
SUBL = (64, 32, 16, 8, 4, 2, 1)


def second_block(nc, ps, x, con, bfc, a):
    with ExitStack() as ctx:
        mixer = ExitStack()

        def sb(name, shape, dt=F32):
            return ctx.enter_context(nc.sbuf_tensor("b_" + name, shape, dt))

        def mix(name, shape, dt=F32):
            return mixer.enter_context(nc.sbuf_tensor("b_" + name, shape, dt))

        def sem(name):
            s = ctx.enter_context(nc.semaphore("b_" + name))
            sems.append(s)
            return s

        def flat(t):
            return t.rearrange("p a b -> p (a b)")

        sems = []
        ident = con[:, C_ID:C_ID + P]
        ident_bf, maskT_bf, maskQ_bf = (bfc[:, i, :] for i in range(3))
        tri = con[:, C_U:C_U + NT * SEQ].rearrange("p (t l) -> p t l", t=NT)
        upper = con[:, C_U:C_U + P]
        ones = column(con[:, C_U + P - 1:C_U + P], P)

        con2 = sb("con2", [P, N_CONST2])
        lmask = con2[:, C2_LV:C2_LV + 8 * P].rearrange("p (n i) -> p n i", n=8)
        half_turn = con2[64:96, C2_R2:C2_R2 + 32]
        same_head = con2[:, C2_B64:C2_B64 + P]
        ring = sb("ring", [P, RING, SLOT])
        hT = sb("hT", [P, KD, SEQ])
        xm = sb("xm", [P, NT, D])
        par = sb("par", [NPAR2, P])
        parT = sb("parT", [P, NPAR2])
        small = sb("small", [P, 2, 4])
        hgain = sb("hgain", [P, 2, 64])
        lnp = sb("lnp", [P, 2, W2])
        nhalf = sb("nhalf", [P, 8])
        pT = sb("pT", [P, 8, SEQ])
        gates = sb("gates", [P, 32, SEQ])
        pos = sb("pos", [MLA_D, SEQ], I32)
        trig = sb("trig", [MLA_D, 2, SEQ])
        glr = sb("glr", [16, SEQ])
        wg, bg = sb("wg", [16, P]), sb("bg", [1, P])
        dab = sb("dab", [P, NT, 8])
        lcat = sb("lcat", [P, NT, 132])
        asc = sb("asc", [P, 4])
        gcum = sb("gcum", [P, SEQ])
        gam = sb("gam", [P, 3, 4])
        ngam = sb("ngam", [P, NT, 4])
        egam = sb("egam", [P, 3, 4])
        beta = sb("beta", [P, NT, 4])
        nmx, rsum, rinv = sb("nmx", [P, 8]), sb("rsum", [P, 8]), sb("rinv", [P, 8])
        ssq, msq, rstd = (sb(n, [P, 8, 8]) for n in ("ssq", "msq", "rstd"))
        mean = sb("mean", [P, NT])
        ys = mix("ys", [P, 4, 2, SEQ])
        wuq, wukv = mix("wuq", [P, 2, 384]), mix("wukv", [P, 4, P])
        uv = mix("uv", [P, NT, 512])
        sgw = mix("sgw", [P, 4, P])
        wsT = mix("wsT", [P, 4, P])
        gqk = mix("gqk", [P, 2, SEQ])
        gv, gog, dz = (mix(n, [P, NT, W2]) for n in ("gv", "gog", "dz"))
        SaT = mix("SaT", [P, 4, NT, P])
        S01 = mix("S01", [P, 4, P])
        dnp = mix("dnp", [P, 6, SEQ + 4])
        dnc = mix("dnc", [P, 6, SEQ])
        ob = mix("ob", [P, NT, W2])
        tq = mix("tq", [P, NT, W2])
        probs = mix("probs", [P, 8, SEQ])
        big = mix("big", [P, 3, KD * SEQ])
        memT = probs
        oT = probs
        l2s = probs[:, 0:4, :]
        l2r = probs[:, 4:8, :]
        merged = pT
        spb = flat(pT[:, :, :])[:, 0:5 * 264].rearrange("p (a b) -> p a b", a=5)
        ed, qe, ke = (big[:, i, :].rearrange("p (a b) -> p a b", a=8) for i in range(3))
        xq, xk = (big[:, i, :].rearrange("p (a b) -> p a b", a=8) for i in range(2))
        xv = big[:, 2, :].rearrange("p (t c) -> p t c", t=NT)
        bigs = big[:, :, :].rearrange("p a (b c) -> p (a b) c", b=2)
        decT, LT, LTm, X, XT, Y = (bigs[:, i, :].rearrange("p (s i) -> p s i", s=8) for i in range(6))
        hid = gates
        early = flat(big[:, :, :])
        cq, ckv = (early[:, c:c + n].rearrange("p (t c) -> p t c", t=NT) for c, n in ((0, 512), (512, 256)))
        cT = early[:, 768:1536].rearrange("p (a b) -> p a b", a=3)
        mv = early[:, 1536:2048].rearrange("p (t c) -> p t c", t=NT)
        qT = early[0:MLA_D, 2048:3328].rearrange("p (a b) -> p a b", a=5)
        kT = early[0:MLA_D, 3328:4352].rearrange("p (a b) -> p a b", a=4)
        tmp96 = lnp
        attnT = SaT[:, :, :, :].rearrange("p h t i -> p (h t) i")
        dnb = flat(dnp[:, :, :])
        rv = dnb[:, 0:512].rearrange("p (t c) -> p t c", t=NT)
        kd = dnb[:, 512:768]
        u = dnb[:, 768:1280].rearrange("p (t c) -> p t c", t=NT)
        ssb = dnb[:, 1280:1408]
        mixer.close()
        whi, wlo = (sb(n, [P, HALVES, HALF], F32R) for n in ("whi", "wlo"))
        hhi, hlo = (sb(n, [P, HALVES, 2 * SEQ], F32R) for n in ("hhi", "hlo"))
        nhi, nlo = (sb(n, [P, KD, SEQ], F32R) for n in ("nhi", "nlo"))
        bufs = dict(cq=cq[:, :, :], ckv=ckv[:, :, :], dn=dnp[:, :, 3:SEQ + 3], dab=dab[:, :, :], dz=dz[:, :, :],
                    gqk=gqk[:, :, :], gv=gv[:, :, :], gog=gog[:, :, :], uv=uv, kpe=qT[64:96, 4, :],
                    glr=glr[:, :])

        par_in, small_in, w_in_ = sem("par_in"), sem("small_in"), sem("w_small")
        mem_in = sem("mem_in")
        landed = [sem(f"landed{i}") for i in range(RING)]
        hi_ok, lo_ok = sem("hi_ok"), sem("lo_ok")
        half_used = sem("half_used")
        nlo_ok = sem("nlo_ok")
        full, free = sem("full"), sem("free")
        par_ps, par_ok, init_ok = sem("par_ps"), sem("par_ok"), sem("init_ok")
        ssq_ok, msq_ok, rstd_ok, xn_ok = sem("ssq_ok"), sem("msq_ok"), sem("rstd_ok"), sem("xn_ok")
        cn_ok, ct_ps, ct_ok = sem("cn_ok"), sem("ct_ps"), sem("ct_ok")
        mq_ps, mq_ok, rope_ps, rope_ok = sem("mq_ps"), sem("mq_ok"), sem("rope_ps"), sem("rope_ok")
        qk_ps, mx_ok, ex_ok, pn_ok = sem("qk_ps"), sem("mx_ok"), sem("ex_ok"), sem("pn_ok")
        pt_ps, pt_a, pt_v, o_ps, xo_ok = sem("pt_ps"), sem("pt_a"), sem("pt_v"), sem("o_ps"), sem("xo_ok")
        bt_in, bt_ps, bt_ok = sem("bt_in"), sem("bt_ps"), sem("bt_ok")
        conv_ok, silu_ok, l2_sq = sem("conv_ok"), sem("silu_ok"), sem("l2_sq")
        pre_ps, spv, spe, lc_ok = sem("pre_ps"), sem("spv"), sem("spe"), sem("lc_ok")
        ln_ok, mix_ps = sem("ln_ok"), sem("mix_ps")
        cum_ps, cum_ok, df_ok, le_ok, lev_ok = (sem(n) for n in ("cum_ps", "cum_ok", "df_ok", "le_ok", "lev_ok"))
        l2_ps, l2_in, l2_rt, l2_ok = sem("l2_ps"), sem("l2_in"), sem("l2_rt"), sem("l2_ok")
        sa_ps, sa_ok, go_ps, gn_ok, sil_ok = (sem(n) for n in ("sa_ps", "sa_ok", "go_ps", "gn_ok", "sil_ok"))
        tk_ps, tk_ok, row_ps, dec_ok, lt_ok = (sem(n) for n in ("tk_ps", "tk_ok", "row_ps", "dec_ok", "lt_ok"))
        kk_ps, at_ok, eg_in, eg_ok = sem("kk_ps"), sem("at_ok"), sem("eg_in"), sem("eg_ok")
        lm_ok, yy_ps, yy_ok, zz_ps, xx_ok = (sem(n) for n in ("lm_ok", "yy_ps", "yy_ok", "zz_ps", "xx_ok"))
        u_ps, u_ok, st_ps, st_ok, ks_ps, r1_ok, do_ps = (
            sem(n) for n in ("u_ps", "u_ok", "st_ps", "st_ok", "ks_ps", "r1_ok", "do_ps"))
        sig_ok, pr_ps, pr_free, mg_ok = sem("sig_ok"), sem("pr_ps"), sem("pr_free"), sem("mg_ok")
        res_ps, res_ok, hs_ok = sem("res_ps"), sem("res_ok"), sem("hs_ok")
        dch, con_in, fin_in, y_ok = sem("dch"), sem("con_in"), sem("fin_in"), sem("y_ok")

        def cols(src, l, c, n):
            return src[bass.ds(l, 1), :, c:c + n].rearrange("a (k p) c -> p (a k) c", p=P)

        def wide(name, n):
            return [(8, 512, [lambda l, c=c: (0, cols(a[name], l, 512 * c, 512))]) for c in range(n)]

        chunks = [(8, n, [lambda l, c=c, n=n: (0, cols(a["w_in_2"], l, c, n))]) for c, n, _ in IN2]
        N_IN = len(IN2)
        chunks += [(8, 512, [lambda l, c=c: (0, cols(a["w_in_2"], l, GATE2 + 512 * c, 512))]) for c in range(8)]
        chunks += wide("xattn_wk_2", 2) + wide("xattn_wv_2", 2)
        chunks += [(4, D, [lambda l, c=c: (0, a["w_branch_2"][bass.ds(l, 1), 2 * c:2 * c + 2].rearrange(
            "a n (k p) c -> p (a n k) c", p=P))]) for c in range(2)]
        chunks += wide("w_out_2", 2) + wide("xattn_wq_2", 2) + wide("xattn_wo_2", 2) + wide("w_up_2", 8)
        chunks += [(4, D, [lambda l, c=c: (0, a["w_down_2"][bass.ds(l, 1), c * 512:(c + 1) * 512, :].rearrange(
            "a (k p) c -> p (a k) c", p=P))]) for c in range(8)]
        W = Weights(chunks)
        C_GATE = N_IN
        C_WK, C_WV, C_BR, C_OUT = C_GATE + 8, C_GATE + 10, C_GATE + 12, C_GATE + 14
        C_WQ, C_WO, C_UP, C_DN = C_OUT + 2, C_OUT + 4, C_OUT + 6, C_OUT + 14

        def chunk(w):
            k, c, _ = chunks[w]
            return ring[:, w % RING, 0:k * c].rearrange("p (k c) -> p k c", c=c)

        in_units = []
        for _, _, pieces in IN2:
            out = []
            for p in pieces:
                out += [("G", p[1], p[2], p[3], p[4])] if p[0] == "G" else units_of([p])
            in_units.append(out)
        U_IN = [4 + sum(len(v) for v in in_units[:i]) for i in range(N_IN + 1)]
        U_GATE = U_IN[-1]
        U_MEM = U_GATE + 16
        U_WK = U_MEM + 4
        U_WV = U_WK + 4
        U_X6 = U_WV + 4
        U_WQ = U_X6 + 4
        U_X7 = U_WQ + 4
        U_UP = U_X7 + 4
        read = [(full, U_IN[i + 1]) for i in range(N_IN)]
        read += [(full, U_GATE + 2 * c + 2) for c in range(8)]
        read += [(full, U_WK + 2 * c + 2) for c in range(4)]
        read += [(pr_ps, 8 * c + 8) for c in range(2)]
        read += [(res_ps, 2 * c + 2) for c in range(2)]
        read += [(full, U_WQ + 2 * c + 2) for c in range(2)]
        read += [(res_ps, 4 + 2 * c + 2) for c in range(2)]
        read += [(lo_ok, 2 * c + 2) for c in range(15)]
        N_UP = 16
        N_HALF = N_UP + KH2 // 2

        def half_source(h):
            wt = chunk(C_UP + h // 2)
            return wt[:, :, 256 * (h % 2):256 * (h % 2) + 256] if h < N_UP else wt[:, 2 * (h % 2):2 * (h % 2) + 2, :]

        def half_of(buf, h):
            return buf[:, h % HALVES, :].rearrange("p (k c) -> p k c", k=8 if h < N_UP else 2)

        def hidden_of(buf, i):
            return buf[:, i % HALVES, :].rearrange("p (k c) -> p k c", k=2)

        L = ps[:, 4:8, :].rearrange("p b (s w) -> p (b s) w", s=2)

        def system(t, h):
            return (h % 2) * 4 + t * 2 + h // 2

        with nc.Block() as block:

            @block.sync
            def _(sp_):
                sp_.dma_start(con2[:, :], a["constants_2"]).then_inc(con_in, 16)
                sp_.dma_start(pos[64:96, :], a["positions_2"].broadcast_to([32, SEQ])).then_inc(con_in, 16)

            @block.vector
            def _(dve):
                V = nc.vector
                n_chain = [0]

                def link(ins):
                    n_chain[0] += 1
                    ins.then_inc(dch, 1)
                    dve.wait_ge(dch, n_chain[0])

                ang, k = tmp96[64:96, 0, :], tmp96[64:96, 1, :]
                dve.wait_ge(con_in, 32)
                link(V.memset(nhalf[:, :], -0.5))
                link(V.tensor_copy(ang, pos[64:96, :]))
                link(V.tensor_scalar(ang, ang, con2[64:96, C2_INV:C2_INV + 1], None, ALU.mult))
                link(V.tensor_scalar(k, ang, 1.0 / TWO_PI, ROUND, ALU.mult, ALU.add))
                link(V.tensor_scalar(k, k, -ROUND, None, ALU.add))
                for part in (PI_A, PI_B, PI_C):
                    link(V.scalar_tensor_tensor(ang, k, -part, ang, ALU.mult, ALU.add))
                link(V.tensor_scalar(ang, ang, 3.141592, -3.141592, ALU.min, ALU.max))
                link(V.scalar_tensor_tensor(k, ang, -1.0, ang, ALU.mult, ALU.max))
                V.tensor_scalar(k, k, -1.0, float(np.pi / 2), ALU.mult, ALU.add).then_inc(con_in, 1)

            @block.scalar
            def _(act):
                act.wait_ge(con_in, 33)
                nc.scalar.activation(trig[64:96, 0, :], tmp96[64:96, 1, :], ACT.Sin).then_inc(y_ok, 1)
                nc.scalar.activation(trig[64:96, 1, :], tmp96[64:96, 0, :], ACT.Sin).then_inc(y_ok, 1)
                act.wait_ge(y_ok, 2)

        def clear():
            nc.all_engine_barrier()
            for s in sems:
                nc.gpsimd.sem_clear(s)
            nc.all_engine_barrier()

        clear()
        with nc.Fori(0, DEPTH) as l:
            with nc.Block() as block:

                @block.sync
                def _(sp_):
                    row = 0
                    for name, n in (("norm_mix_2", 8), ("norm_xattn_2", 8), ("norm_mem_2", 8), ("norm_mlp_2", 8),
                                    ("mla_norm_q_2", 2), ("mla_norm_kv_2", 1), ("sg_b_2", 4), ("dn_conv_2", 24)):
                        src = a[name][bass.ds(l, 1)]
                        if name == "dn_conv_2":
                            src = src.rearrange("a j (k p) -> (a j k) p", p=P)
                        elif name == "sg_b_2":
                            src = src.rearrange("a g p -> (a g) p")
                        else:
                            src = src.rearrange("a (k p) -> (a k) p", p=P)
                        sp_.dma_start(par[row:row + n, :], src).then_inc(par_in, 16)
                        row += n
                    sp_.dma_start(sgw[:, :, :], a["sg_w_2"][bass.ds(l, 1)].rearrange("a g i j -> i (a g) j")
                                  ).then_inc(par_in, 16)
                    for w, (k, c, sources) in enumerate(chunks):
                        if w >= RING:
                            sp_.wait_ge(*read[w - RING])
                        for source in sources:
                            at, src = source(l)
                            sp_.dma_start(chunk(w)[:, :, at:at + src.shape[2]], src).then_inc(landed[w % RING], 16)
                        if w == 0:
                            for i, name in enumerate(("dn_dt_bias_2", "dn_a_log_2")):
                                sp_.dma_start(small[:, i, :], a[name][bass.ds(l, 1)].broadcast_to([P, 4])
                                              ).then_inc(small_in, 16)
                            for i, name in enumerate(("gla_norm_2", "dn_norm_2")):
                                sp_.dma_start(hgain[:, i, :], a[name][bass.ds(l, 1)].broadcast_to([P, 64])
                                              ).then_inc(small_in, 16)
                            for i, name in enumerate(("sg_ln_g_2", "sg_ln_b_2")):
                                sp_.dma_start(lnp[:, i, :], a[name][bass.ds(l, 1)].broadcast_to([P, W2])
                                              ).then_inc(small_in, 16)
                            sp_.dma_start(wg[:, :], a["gla_w_gate_2"][bass.ds(l, 1)].rearrange("a r c -> (a r) c")
                                          ).then_inc(w_in_, 16)
                            sp_.dma_start(bg[:, :], a["gla_b_gate_2"][bass.ds(l, 1)]).then_inc(w_in_, 16)
                            sp_.dma_start(wuq[:, :, :], cols(a["mla_w_uq_2"], l, 0, 384)).then_inc(w_in_, 16)
                            sp_.dma_start(wukv[:, :, :].rearrange("p a b -> p (a b)"),
                                          a["mla_w_ukv_2"][bass.ds(l, 1)].rearrange("a p c -> (a p) c")
                                          ).then_inc(w_in_, 16)
                        if w == 2:
                            sp_.dma_start(xm[:, :, :], a["mem_2"].rearrange("a (t p) d -> p (a t) d", p=P)
                                          ).then_inc(mem_in, 16)

                @block.tensor
                def _(pe):
                    T = nc.tensor

                    def bank(v):
                        if v >= 2:
                            pe.wait_ge(free, v - 1)
                        return ps[:, v % 2, :]

                    def take(w):
                        pe.wait_ge(landed[w % RING], W.ready[w])

                    def transposed(u0, n):
                        pe.wait_ge(xn_ok, n)
                        for k in range(KD):
                            if n == 4 and k in (4, 6):
                                pe.wait_ge(nlo_ok, k // 2 - 1)
                            if k % 2 == 0:
                                b = bank(u0 + k // 2)
                            for t in range(NT):
                                mm = T.transpose(b[:, (k % 2) * SEQ + t * P:(k % 2) * SEQ + (t + 1) * P],
                                                 xm[:, t, k * P:(k + 1) * P], ident)
                            if k % 2:
                                mm.then_inc(full, 1)

                    def feature_unit(out, w, c, nb, act_, k0=0, K=None):
                        wt = chunk(w)
                        K = K or chunks[w][0]
                        for b in range(nb):
                            for k in range(K):
                                mm = T.matmul(out[:, b * SEQ:(b + 1) * SEQ], wt[:, k0 + k, c + b * P:c + (b + 1) * P],
                                              act_[:, k, :], start=k == 0, stop=k == K - 1)
                        return mm

                    def token_unit(out, w, c, n, t, act_):
                        for k in range(8):
                            mm = T.matmul(out, act_[:, k, t * P:(t + 1) * P], chunk(w)[:, k, c:c + n],
                                          start=k == 0, stop=k == 7)
                        return mm

                    def in_chunk(i):
                        take(i)
                        for n, (kind, c, size, _, at) in enumerate(in_units[i]):
                            b = bank(U_IN[i] + n)
                            if kind == "F":
                                mm = feature_unit(b, i, c, size, hT)
                            elif kind == "G":
                                for k in range(KD):
                                    mm = T.matmul(b[at:at + size, 0:SEQ], chunk(i)[:, k, c:c + size], hT[:, k, :],
                                                  start=k == 0, stop=k == KD - 1)
                            elif kind == "T":
                                mm = token_unit(b[:, 0:size], i, c, size, at, hT)
                            else:
                                for t in range(NT):
                                    mm = token_unit(b[:, t * size:(t + 1) * size], i, c, size, t, hT)
                            mm.then_inc(full, 1)

                    gate_n = [0]

                    def gate():
                        g = gate_n[0]
                        gate_n[0] += 1
                        w = C_GATE + g // 2
                        if g % 2 == 0:
                            take(w)
                        feature_unit(bank(U_GATE + g), w, (g % 2) * SEQ, 2, hT).then_inc(full, 1)

                    def b_turn(n):
                        pe.wait_ge(bt_in, n + 1)
                        for b in range(2):
                            for t in range(NT):
                                mm = T.transpose(ps[:, 3, b * SEQ + t * P:b * SEQ + (t + 1) * P],
                                                 ob[:, t, b * P:(b + 1) * P], ident)
                        mm.then_inc(bt_ps, 1)

                    pe.wait_ge(par_in, 144)
                    T.transpose(ps[:, 2, 0:NPAR2], par[:, :], ident[0:NPAR2, 0:NPAR2]).then_inc(par_ps, 1)
                    for g in range(4):
                        mm = T.transpose(ps[:, 3, g * P:(g + 1) * P], sgw[:, g, :], ident)
                    mm.then_inc(par_ps, 1)
                    transposed(0, 1)
                    pe.wait_ge(free, 4)
                    in_chunk(0)
                    in_chunk(1)
                    pe.wait_ge(cn_ok, 1)
                    pe.wait_ge(par_ok, 2)
                    for t in range(NT):
                        for b in range(2):
                            T.transpose(ps[:, 2, b * SEQ + t * P:b * SEQ + (t + 1) * P], cq[:, t, b * P:(b + 1) * P],
                                        ident)
                        mm = T.transpose(ps[:, 3, t * P:(t + 1) * P], ckv[:, t, :], ident)
                    mm.then_inc(ct_ps, 1)
                    in_chunk(2)
                    pe.wait_ge(ct_ok, 1)
                    pe.wait_ge(w_in_, 64)
                    for h in range(4):
                        c = (h % 2) * SEQ
                        for k in range(2):
                            T.matmul(ps[0:MLA_D, 4 + h // 2, c:c + SEQ], wuq[:, k, h * MLA_D:(h + 1) * MLA_D],
                                     cT[:, k, :], start=k == 0, stop=k == 1)
                        T.matmul(ps[0:64, 6 + h // 2, c:c + SEQ], wukv[:, h, 0:64], cT[:, 2, :], start=True, stop=True)
                    for t in range(NT):
                        mm = T.matmul(ps[:, 2, t * W2:(t + 1) * W2], cT[:, 2, t * P:(t + 1) * P], wukv[:, :, 64:P],
                                      start=True, stop=True)
                    mm.then_inc(mq_ps, 1)
                    in_chunk(3)
                    pe.wait_ge(mq_ok, 1)
                    for i in range(5):
                        mm = T.matmul(ps[64:96, 4 + i // 2, (i % 2) * SEQ:(i % 2 + 1) * SEQ], half_turn, qT[64:96, i, :],
                                      start=True, stop=True)
                    mm.then_inc(rope_ps, 1)
                    in_chunk(4)
                    pe.wait_ge(rope_ok, 1)
                    for s in range(8):
                        t, h = s // 4, s % 4
                        w = P * (t + 1)
                        T.matmul(L[:, s, 0:w], qT[:, h, t * P:(t + 1) * P], kT[:, h, 0:w], start=True, stop=False)
                        mm = T.matmul(L[:, s, w - P:w], ident_bf, maskQ_bf, start=False, stop=True)
                    mm.then_inc(qk_ps, 1)
                    in_chunk(5)
                    pe.wait_ge(ex_ok, 1)
                    for s in range(8):
                        for k in range(s // 4 + 1):
                            mm = T.transpose(L[:, s, k * P:(k + 1) * P], probs[:, s, k * P:(k + 1) * P], ident)
                    mm.then_inc(pt_ps, 1)
                    gate()
                    pe.wait_ge(pt_a, 1)
                    pe.wait_ge(pt_v, 1)
                    for s in range(8):
                        t, h = s // 4, s % 4
                        for k in range(t + 1):
                            mm = T.matmul(ps[:, 2, t * W2 + h * 64:t * W2 + (h + 1) * 64], pT[:, s, k * P:(k + 1) * P],
                                          mv[:, k, h * 64:(h + 1) * 64], start=k == 0, stop=k == t)
                    mm.then_inc(o_ps, 1)
                    gate()
                    b_turn(0)
                    for t in range(NT):
                        T.matmul(ps[:, 2, t * P:(t + 1) * P], glr[:, t * P:(t + 1) * P], wg[:, :], start=True, stop=False)
                        mm = T.matmul(ps[:, 2, t * P:(t + 1) * P], upper[0:1, :], bg[:, :], start=False, stop=True)
                    mm.then_inc(pre_ps, 1)
                    gate()
                    pe.wait_ge(ln_ok, 1)
                    pe.wait_ge(bt_ok, 1)
                    for t in range(NT):
                        for g in range(4):
                            mm = T.matmul(ps[:, 3, t * W2 + g * 64:t * W2 + (g + 1) * 64], wsT[:, g, :],
                                          uv[:, t, W2 + g * 64:W2 + (g + 1) * 64], start=True, stop=True)
                    mm.then_inc(mix_ps, 1)
                    gate()
                    b_turn(1)
                    pe.wait_ge(l2_sq, 1)
                    for b in range(4):
                        mm = T.matmul(ps[:, 4 + b // 2, (b % 2) * SEQ:(b % 2 + 1) * SEQ], same_head, l2s[:, b, :],
                                      start=True, stop=True)
                    mm.then_inc(l2_ps, 1)
                    gate()
                    pe.wait_ge(lc_ok, 1)
                    pe.wait_ge(bt_ok, 2)
                    for t in range(NT):
                        T.matmul(ps[:, 3, 0:SEQ], lcat[:, t, 0:P], tri[:, t, :], start=t == 0, stop=t == NT - 1)
                    for t in range(NT):
                        T.matmul(ps[:, 2, 4 * t:4 * t + 4], upper, lcat[:, t, P:P + 4], start=True, stop=True)
                    T.matmul(ps[:, 2, 8:12], ones, lcat[:, 0, P:P + 4], start=True, stop=True).then_inc(cum_ps, 1)
                    gate()
                    gate()
                    pe.wait_ge(lev_ok, 1)
                    pe.wait_ge(l2_in, 1)
                    for r in range(5):
                        if r:
                            pe.wait_ge(sa_ok, r)
                        for h in range(4):
                            rows = slice(32 * h, 32 * h + 32)
                            if r == 4:
                                mm = T.matmul(ps[:, 4 + h, 0:P], ke[rows, 0, 0:P], qe[rows, 0, P:SEQ],
                                              start=True, stop=True)
                                continue
                            for i in range(2):
                                n = 2 * r + i
                                kk_, qq_ = (ke[rows, n + 1, :], qe[rows, n + 1, :]) if n < 7 else \
                                    (gqk[rows, 1, :], gqk[rows, 0, :])
                                for t in range(NT):
                                    c = i * SEQ + t * P
                                    mm = T.matmul(ps[:, 4 + h, c:c + P], kk_[:, t * P:(t + 1) * P],
                                                  qq_[:, t * P:(t + 1) * P], start=True, stop=True)
                        mm.then_inc(sa_ps, 1)
                        if r in (1, 3):
                            gate()
                    pe.wait_ge(sa_ok, 5)
                    pe.wait_ge(cum_ok, 1)
                    for t in range(NT):
                        for h in range(4):
                            out = ps[:, 2, t * W2 + h * 64:t * W2 + (h + 1) * 64]
                            mm = T.matmul(out, SaT[:, h, t, :], gv[:, t, h * 64:(h + 1) * 64], start=True, stop=t == 0)
                            if t:
                                mm = T.matmul(out, S01[:, h, :], gv[:, 0, h * 64:(h + 1) * 64], start=False, stop=True)
                    mm.then_inc(go_ps, 1)
                    for t in range(NT):
                        for h in range(4):
                            s = system(t, h)
                            out = ps[:, 4 + s // 4, (s % 4) * P:(s % 4 + 1) * P]
                            T.matmul(out, column(lcat[:, t, P + h:P + h + 1], P), upper, start=True, stop=False)
                            T.matmul(out, ident_bf, maskT_bf, start=False, stop=True)
                            mm = T.matmul(ps[:, 6 + s // 4, (s % 4) * P:(s % 4 + 1) * P], column(beta[:, t, h:h + 1], P),
                                          ident, start=True, stop=True)
                    mm.then_inc(row_ps, 1)
                    gate()
                    b_turn(2)
                    pe.wait_ge(l2_ok, 1)
                    pe.wait_ge(gn_ok, 1)
                    for t in range(NT):
                        for b in range(2):
                            T.transpose(ps[:, 2, t * W2 + b * P:t * W2 + (b + 1) * P], dnc[:, 4 + b, t * P:(t + 1) * P],
                                        ident)
                    pe.wait_ge(bt_ok, 3)
                    for b in range(2):
                        mm = T.transpose(ps[:, 3, b * P:(b + 1) * P], dnc[:, 2 + b, 0:P], ident)
                    mm.then_inc(tk_ps, 1)
                    pe.wait_ge(dec_ok, 1)
                    pe.wait_ge(lt_ok, 1)
                    for t in range(NT):
                        for h in range(4):
                            s, base = system(t, h), 64 * (h % 2)
                            key = dnc[base:base + 64, 2 + h // 2, t * P:(t + 1) * P]
                            T.matmul(ps[:, 4 + s // 4, (s % 4) * P:(s % 4 + 1) * P], key, key, start=True, stop=True)
                            mm = T.matmul(ps[:, 6 + s // 4, (s % 4) * P:(s % 4 + 1) * P], key,
                                          dnc[base:base + 64, h // 2, t * P:(t + 1) * P], start=True, stop=True)
                    mm.then_inc(kk_ps, 1)
                    gate()
                    pe.wait_ge(tk_ok, 1)
                    for lv in range(7):
                        for p in range(2):
                            it = 2 * lv + p
                            pe.wait_ge(lm_ok, it + 1)
                            if lv:
                                pe.wait_ge(xx_ok, it - 1)
                            for s in range(4 * p, 4 * p + 4):
                                mm = T.matmul(ps[:, 2 + p, (s % 4) * P:(s % 4 + 1) * P], LTm[:, s, :], X[:, s, :],
                                              start=True, stop=True)
                            mm.then_inc(yy_ps, 1)
                        for p in range(2):
                            it = 2 * lv + p
                            pe.wait_ge(yy_ok, it + 1)
                            if lv == 0:
                                pe.wait_ge(at_ok, 1)
                            for s in range(4 * p, 4 * p + 4):
                                c = slice((s % 4) * P, (s % 4 + 1) * P)
                                T.matmul(ps[:, 4 + 2 * p, c], XT[:, s, :], Y[:, s, :], start=True, stop=True)
                                mm = T.matmul(ps[:, 5 + 2 * p, c], Y[:, s, :], XT[:, s, :], start=True, stop=True)
                            mm.then_inc(zz_ps, 1)
                    gate()
                    pe.wait_ge(xx_ok, 14)
                    for h in range(4):
                        mm = T.matmul(ps[:, 2, h * 64:(h + 1) * 64], XT[:, system(0, h), :], rv[:, 0, h * 64:(h + 1) * 64],
                                      start=True, stop=True)
                    mm.then_inc(u_ps, 1)
                    gate()
                    pe.wait_ge(u_ok, 1)
                    for h in range(4):
                        base = 64 * (h % 2)
                        mm = T.matmul(ps[base:base + 64, 3, (h // 2) * 64:(h // 2 + 1) * 64], kd[:, h * 64:(h + 1) * 64],
                                      u[:, 0, h * 64:(h + 1) * 64], start=True, stop=True)
                    mm.then_inc(st_ps, 1)
                    gate()
                    pe.wait_ge(st_ok, 1)
                    for h in range(4):
                        base, hb = 64 * (h % 2), h // 2
                        for i, blk in enumerate((2 + hb, hb)):
                            mm = T.matmul(ps[:, 4 + h % 2, i * P + hb * 64:i * P + (hb + 1) * 64],
                                          dnc[base:base + 64, blk, P:SEQ], ssb[base:base + 64, hb * 64:(hb + 1) * 64],
                                          start=True, stop=True)
                    mm.then_inc(ks_ps, 1)
                    gate()
                    pe.wait_ge(r1_ok, 1)
                    for h in range(4):
                        mm = T.matmul(ps[:, 2, W2 + h * 64:W2 + (h + 1) * 64], XT[:, system(1, h), :],
                                      rv[:, 1, h * 64:(h + 1) * 64], start=True, stop=True)
                    mm.then_inc(u_ps, 1)
                    pe.wait_ge(u_ok, 2)
                    for t in range(NT):
                        for h in range(4):
                            mm = T.matmul(ps[:, 3, t * W2 + h * 64:t * W2 + (h + 1) * 64], attnT[:, system(t, h), :],
                                          u[:, t, h * 64:(h + 1) * 64], start=True, stop=True)
                    mm.then_inc(do_ps, 1)
                    while gate_n[0] < 16:
                        gate()
                    transposed(U_MEM, 2)
                    pe.wait_ge(free, U_MEM + 4)
                    for c in range(2):
                        take(C_WK + c)
                        for i in range(2):
                            feature_unit(bank(U_WK + 2 * c + i), C_WK + c, i * SEQ, 2, memT).then_inc(full, 1)
                    for c in range(2):
                        take(C_WV + c)
                        for t in range(NT):
                            token_unit(bank(U_WV + 2 * c + t), C_WV + c, 0, 512, t, memT).then_inc(full, 1)
                    b_turn(3)
                    for n in range(4):
                        if n % 2 == 0:
                            take(C_BR + n // 2)
                        pe.wait_ge(bt_ok, n + 1)
                        for m in range(4):
                            i = 4 * n + m
                            if i >= 4:
                                pe.wait_ge(pr_free, i - 3)
                            feature_unit(ps[:, 4 + i % 4, :], C_BR + n // 2, m * SEQ, 2, ys[:, n, :, :], 2 * (n % 2), 2
                                         ).then_inc(pr_ps, 1)
                    pe.wait_ge(mg_ok, 12)
                    for c in range(2):
                        take(C_OUT + c)
                        for t in range(NT):
                            token_unit(ps[:, 4 + 2 * c + t, :], C_OUT + c, 0, 512, t, merged).then_inc(res_ps, 1)
                    transposed(U_X6, 3)
                    pe.wait_ge(free, U_X6 + 4)
                    for c in range(2):
                        take(C_WQ + c)
                        for i in range(2):
                            feature_unit(bank(U_WQ + 2 * c + i), C_WQ + c, i * SEQ, 2, hT).then_inc(full, 1)
                    pe.wait_ge(free, U_WQ + 4)
                    for s in range(8):
                        t, h = s // 4, s % 4
                        for k in range(2):
                            mm = T.matmul(L[:, s, :], xq[:, 2 * h + k, t * P:(t + 1) * P], xk[:, 2 * h + k, :],
                                          start=k == 0, stop=k == 1)
                    mm.then_inc(qk_ps, 1)
                    pe.wait_ge(pn_ok, 1)
                    for s in range(8):
                        for k in range(2):
                            mm = T.transpose(L[:, s, k * P:(k + 1) * P], probs[:, s, k * P:(k + 1) * P], ident)
                    mm.then_inc(pt_ps, 1)
                    pe.wait_ge(pt_a, 2)
                    pe.wait_ge(pt_v, 2)
                    for b in range(8):
                        for t in range(NT):
                            for k in range(2):
                                mm = T.matmul(L[:, b, t * P:(t + 1) * P], xv[:, k, b * P:(b + 1) * P],
                                              pT[:, 4 * t + b // 2, k * P:(k + 1) * P], start=k == 0, stop=k == 1)
                    mm.then_inc(o_ps, 1)
                    pe.wait_ge(xo_ok, 1)
                    for c in range(2):
                        take(C_WO + c)
                        for t in range(NT):
                            token_unit(ps[:, 4 + 2 * c + t, :], C_WO + c, 0, 512, t, oT).then_inc(res_ps, 1)
                    transposed(U_X7, 4)
                    pe.wait_ge(free, U_X7 + 4)
                    pe.wait_ge(nlo_ok, 4)
                    for h in range(N_UP):
                        pe.wait_ge(lo_ok, h + 1)
                        hi, lo = half_of(whi, h), half_of(wlo, h)
                        out = bank(U_UP + h)
                        for b in range(2):
                            for k in range(KD):
                                for j, (wt, act_) in enumerate(((lo, nhi), (hi, nlo), (hi, nhi))):
                                    mm = T.matmul(out[:, b * SEQ:(b + 1) * SEQ], wt[:, k, b * P:(b + 1) * P],
                                                  act_[:, k, :], start=k == 0 and j == 0, stop=k == KD - 1 and j == 2)
                        mm.then_inc(full, 1)
                    for i in range(KH2 // 2):
                        pe.wait_ge(lo_ok, N_UP + i + 1)
                        hi, lo = half_of(whi, N_UP + i), half_of(wlo, N_UP + i)
                        for kk in range(2):
                            for t in range(NT):
                                for half in range(2):
                                    first, last = i + kk == 0, 2 * i + kk == KH2 - 1
                                    for j, (act_, wt) in enumerate(((hlo, hi), (hhi, lo), (hhi, hi))):
                                        mm = T.matmul(ps[:, 4 + 2 * half + t, :],
                                                      hidden_of(act_, i)[:, kk, t * P:(t + 1) * P],
                                                      wt[:, kk, half * 512:(half + 1) * 512],
                                                      start=first and j == 0, stop=last and j == 2)
                                    if last:
                                        mm.then_inc(res_ps, 1)
                        if i < KH2 // 2 - 1:
                            mm.then_inc(half_used, 1)

                @block.scalar
                def _(act):
                    marks = {}

                    def mark(s, ins):
                        marks[s.name] = marks.get(s.name, 0) + 1
                        ins.then_inc(s, 1)
                        act.wait_ge(s, marks[s.name])

                    A = nc.scalar

                    def empty(v):
                        act.wait_ge(full, v + 1)
                        return ps[:, v % 2, :]

                    def squares(e, src):
                        for t in range(NT):
                            i = A.activation(flat(pT[:, 4 * t:4 * t + 4, :]), src[:, t, :], ACT.Square,
                                             accum_out=ssq[:, e, t:t + 1])
                        mark(ssq_ok, i)

                    def turned(u0, gain, dst):
                        for k in range(KD):
                            b = empty(u0 + k // 2)
                            i = A.activation(dst[:, k, :], b[:, (k % 2) * SEQ:(k % 2 + 1) * SEQ], ACT.Copy,
                                             scale=parT[:, gain + k:gain + k + 1])
                            if k % 2:
                                mark(free, i)

                    def in_chunk(i):
                        for n, (kind, c, size, name, at) in enumerate(in_units[i]):
                            b = empty(U_IN[i] + n)
                            dst = bufs[name]
                            if kind == "F":
                                ins = A.activation(dst[:, at:at + size, :], b[:, 0:size * SEQ].rearrange(
                                    "p (a b) -> p a b", a=size), ACT.Copy,
                                    scale=32 ** -0.5 if name == "gqk" and at == 0 else 1.0)
                            elif kind == "G":
                                ins = A.copy(dst, b[at:at + size, 0:SEQ])
                            elif kind == "T":
                                ins = A.activation(dst[:, at, :], b[:, 0:size], ACT.Gelu_apprx_tanh)
                            else:
                                ins = A.copy(dst, b[:, 0:NT * size].rearrange("p (t c) -> p t c", t=NT))
                            mark(free, ins)

                    gate_n = [0]

                    def gate():
                        g = gate_n[0]
                        gate_n[0] += 1
                        mark(free, A.copy(gates[:, 2 * g:2 * g + 2, :],
                                          empty(U_GATE + g).rearrange("p (a b) -> p a b", a=2)))

                    def b_out(n):
                        act.wait_ge(bt_ps, n + 1)
                        mark(bt_ok, A.copy(ys[:, n, :, :], ps[:, 3, :].rearrange("p (a b) -> p a b", a=2)))

                    def p_out(n):
                        act.wait_ge(pt_ps, n + 1)
                        if n:
                            mark(pt_a, A.copy(pT[:, 0:4, :], L[:, 0:4, :]))
                        else:
                            mark(pt_a, A.copy(pT[:, 0:4, 0:P], L[:, 0:4, 0:P]))

                    squares(0, x)
                    act.wait_ge(par_ok, 2)
                    turned(0, QM, hT)
                    act.wait_ge(init_ok, 1)
                    in_chunk(0)
                    in_chunk(1)
                    act.wait_ge(ct_ps, 1)
                    for b in range(3):
                        i = A.activation(cT[:, b, :], ps[:, 2 + b // 2, (b % 2) * SEQ:(b % 2 + 1) * SEQ], ACT.Copy,
                                         scale=parT[:, QQ + b:QQ + b + 1])
                    mark(ct_ok, i)
                    in_chunk(2)
                    act.wait_ge(mq_ps, 1)
                    A.activation(qT[:, 0:4, :], L[0:MLA_D, 0:4, :], ACT.Copy, scale=MLA_D ** -0.5)
                    A.copy(kT[0:64, :, :], L[0:64, 4:8, :])
                    mark(mq_ok, A.copy(mv[:, :, :], ps[:, 2, :].rearrange("p (t c) -> p t c", t=NT)))
                    in_chunk(3)
                    act.wait_ge(conv_ok, 1)
                    mark(silu_ok, A.activation(dnc[:, :, :], dnc[:, :, :], ACT.Silu))
                    act.wait_ge(mem_in, 16)
                    squares(2, xm)
                    in_chunk(4)
                    act.wait_ge(mx_ok, 1)
                    for s in range(8):
                        w = P * (s // 4 + 1)
                        i = A.activation(probs[:, s, 0:w], L[:, s, 0:w], ACT.Exp, bias=nmx[:, s:s + 1],
                                         accum_out=rsum[:, s:s + 1])
                    mark(ex_ok, i)
                    in_chunk(5)
                    p_out(0)
                    mark(l2_sq, A.activation(l2s, dnc[:, 0:4, :], ACT.Square))
                    gate()
                    gate()
                    b_out(0)
                    act.wait_ge(spv, 1)
                    mark(spe, A.activation(spb[:, 2, :], spb[:, 1, :], ACT.Exp, scale=-1.0))
                    mark(spe, A.activation(beta[:, :, :], dab[:, :, 4:8], ACT.Exp, scale=-1.0))
                    mark(spe, A.activation(asc[:, :], small[:, 1, :], ACT.Exp))
                    act.wait_ge(spv, 2)
                    mark(spe, A.activation(spb[:, 4, :], spb[:, 3, :], ACT.Ln))
                    gate()
                    gate()
                    b_out(1)
                    gate()
                    act.wait_ge(l2_in, 1)
                    mark(l2_rt, A.activation(l2r, l2r, ACT.Sqrt))
                    act.wait_ge(df_ok, 1)
                    mark(le_ok, A.activation(ed[:, :, :], ed[:, :, :], ACT.Exp, scale=-1.0))
                    act.wait_ge(eg_in, 1)
                    mark(eg_ok, A.activation(egam[:, :, :], egam[:, :, :], ACT.Exp))
                    gate()
                    gate()
                    mark(sil_ok, A.activation(gog[:, :, :], gog[:, :, :], ACT.Silu))
                    mark(sil_ok, A.activation(dz[:, :, :], dz[:, :, :], ACT.Silu))
                    gate()
                    gate()
                    act.wait_ge(row_ps, 1)
                    for t in range(NT):
                        for h in range(4):
                            s = system(t, h)
                            i = A.activation(decT[:, s, :], ps[:, 4 + s // 4, (s % 4) * P:(s % 4 + 1) * P], ACT.Exp,
                                             bias=ngam[:, t, h:h + 1])
                    mark(dec_ok, i)
                    gate()
                    b_out(2)
                    gate()
                    for lv in range(7):
                        for p in range(2):
                            act.wait_ge(yy_ps, 2 * lv + p + 1)
                            if lv:
                                act.wait_ge(zz_ps, 2 * lv + p - 1)
                            mark(yy_ok, A.copy(flat(Y[:, 4 * p:4 * p + 4, :]), ps[:, 2 + p, :]))
                    while gate_n[0] < 16:
                        gate()
                    turned(U_MEM, QE, memT)
                    act.wait_ge(do_ps, 1)
                    for i in range(4):
                        mark(free, A.copy(xk[:, 2 * i:2 * i + 2, :],
                                          empty(U_WK + i).rearrange("p (a b) -> p a b", a=2)))
                    for i in range(4):
                        mark(free, A.copy(xv[:, i % 2, (i // 2) * 512:(i // 2 + 1) * 512], empty(U_WV + i)))
                    b_out(3)
                    for g in range(4):
                        mark(sig_ok, A.activation(gates[:, 8 * g:8 * g + 8, :], gates[:, 8 * g:8 * g + 8, :],
                                                  ACT.Sigmoid))
                    act.wait_ge(res_ok, 4)
                    squares(6, x)
                    turned(U_X6, QX, hT)
                    for i in range(4):
                        mark(free, A.activation(xq[:, 2 * i:2 * i + 2, :],
                                                empty(U_WQ + i).rearrange("p (a b) -> p a b", a=2), ACT.Copy,
                                                scale=256 ** -0.5))
                    act.wait_ge(mx_ok, 2)
                    for s in range(8):
                        i = A.activation(probs[:, s, :], L[:, s, :], ACT.Exp, bias=nmx[:, s:s + 1],
                                         accum_out=rsum[:, s:s + 1])
                    mark(ex_ok, i)
                    p_out(1)
                    act.wait_ge(o_ps, 2)
                    mark(xo_ok, A.copy(oT[:, :, :], L[:, :, :]))

                    def split(h):
                        if h >= HALVES:
                            if h - HALVES < N_UP:
                                act.wait_ge(full, U_UP + h - HALVES + 1)
                            else:
                                act.wait_ge(half_used, h - HALVES - N_UP + 1)
                        act.wait_ge(landed[(C_UP + h // 2) % RING], W.ready[C_UP + h // 2])
                        if h >= N_UP:
                            i = h - N_UP
                            act.wait_ge(hs_ok, i + 1)
                            A.copy(hidden_of(hhi, i), hid[:, 2 * i:2 * i + 2, :])
                        mark(hi_ok, A.copy(half_of(whi, h), half_source(h)))

                    split(0)
                    split(1)
                    act.wait_ge(res_ok, 8)
                    squares(7, x)
                    for k in range(KD):
                        b = empty(U_X7 + k // 2)
                        i = A.activation(nhi[:, k, :], b[:, (k % 2) * SEQ:(k % 2 + 1) * SEQ], ACT.Copy,
                                         scale=parT[:, QL + k:QL + k + 1])
                        if k % 2:
                            mark(free, i)
                    for h in range(2, HALVES):
                        split(h)
                    for i in range(N_UP):
                        mark(free, A.activation(hid[:, 2 * i:2 * i + 2, :],
                                                empty(U_UP + i).rearrange("p (a b) -> p a b", a=2), ACT.Relu))
                        split(i + HALVES)
                    for h in range(N_UP + HALVES, N_HALF):
                        split(h)

                @block.vector
                def _(dve):
                    n_chain = [0]
                    marks = {}
                    V = nc.vector

                    def link(ins):
                        n_chain[0] += 1
                        ins.then_inc(dch, 1)
                        dve.wait_ge(dch, n_chain[0])

                    def mark(s, ins):
                        marks[s.name] = marks.get(s.name, 0) + 1
                        ins.then_inc(s, 1)
                        dve.wait_ge(s, marks[s.name])

                    def mean_square(e, n, width):
                        mark(msq_ok, V.tensor_scalar(msq[:, e, 0:n], ssq[:, e, 0:n], 1.0 / width, EPS, ALU.mult, ALU.add))
                        dve.wait_ge(rstd_ok, e + 1)

                    def norm_in(e, seen, src):
                        dve.wait_ge(ssq_ok, seen)
                        mean_square(e, 2, D)
                        for t in range(NT):
                            i = V.tensor_scalar(xm[:, t, :], src[:, t, :], rstd[:, e, t:t + 1], None, ALU.mult)
                            if t == 0:
                                link(i)
                        mark(xn_ok, i)

                    def maxima(n):
                        dve.wait_ge(qk_ps, n + 1)
                        if n:
                            mark(mx_ok, V.tensor_reduce(nmx[:, :], L[:, :, :], AX_X, ALU.max, negate=True))
                        else:
                            link(V.tensor_reduce(nmx[:, 0:4], L[:, 0:4, 0:P], AX_X, ALU.max, negate=True))
                            mark(mx_ok, V.tensor_reduce(nmx[:, 4:8], L[:, 4:8, :], AX_X, ALU.max, negate=True))

                    def p_out(n):
                        dve.wait_ge(pt_ps, n + 1)
                        mark(pt_v, V.tensor_copy(pT[:, 4:8, :], L[:, 4:8, :]))

                    def heads(t):
                        return t.rearrange("p t (h c) -> p (t h) c", c=64)

                    def head_norm(e, gate_, gain):
                        link(V.tensor_tensor(tq[:, :, :], ob[:, :, :], ob[:, :, :], ALU.mult))
                        link(V.tensor_reduce(ssq[:, e, :], heads(tq[:, :, :]), AX_X, ALU.add))
                        mean_square(e, 8, 64)
                        link(V.tensor_tensor(heads(ob[:, :, :]), heads(ob[:, :, :]),
                                             rstd[:, e, :].unsqueeze(2).broadcast_to([P, 8, 64]), ALU.mult))
                        link(V.tensor_tensor(heads(gate_), heads(gate_),
                                             hgain[:, gain:gain + 1, :].broadcast_to([P, 8, 64]), ALU.mult))
                        mark(bt_in, V.tensor_tensor(ob[:, :, :], ob[:, :, :], gate_, ALU.mult))

                    mark(init_ok, V.memset(dnp[:, :, 0:3], 0.0))
                    dve.wait_ge(par_ps, 2)
                    mark(par_ok, V.tensor_copy(parT[:, :], ps[:, 2, 0:NPAR2]))
                    mark(par_ok, V.tensor_tensor(wsT[:, :, :], ps[:, 3, :].rearrange("p (g i) -> p g i", g=4),
                                                 upper.unsqueeze(1).broadcast_to([P, 4, P]), ALU.mult))
                    norm_in(0, 1, x)
                    dve.wait_ge(free, U_IN[0] + 2)
                    for i, (c, n) in enumerate(((cq, 256), (ckv, 128))):
                        t = probs[:, 2 * i:2 * i + 2, 0:n]
                        link(V.tensor_tensor(t, c[:, :, :], c[:, :, :], ALU.mult))
                        link(V.tensor_reduce(ssq[:, 1, 2 * i:2 * i + 2], t, AX_X, ALU.add))
                    link(V.tensor_scalar(msq[:, 1, 0:2], ssq[:, 1, 0:2], 1.0 / 256, EPS, ALU.mult, ALU.add))
                    mark(msq_ok, V.tensor_scalar(msq[:, 1, 2:4], ssq[:, 1, 2:4], 1.0 / 128, EPS, ALU.mult, ALU.add))
                    dve.wait_ge(rstd_ok, 2)
                    for t in range(NT):
                        link(V.tensor_scalar(cq[:, t, :], cq[:, t, :], rstd[:, 1, t:t + 1], None, ALU.mult))
                        i = V.tensor_scalar(ckv[:, t, :], ckv[:, t, :], rstd[:, 1, 2 + t:3 + t], None, ALU.mult)
                        if t == 0:
                            link(i)
                    mark(cn_ok, i)
                    dve.wait_ge(free, U_IN[2] + 1)
                    for b in range(6):
                        link(V.tensor_scalar(dnc[:, b, :], dnp[:, b, 0:SEQ], parT[:, QC + b:QC + b + 1], None, ALU.mult))
                        for j in range(1, 4):
                            i = V.scalar_tensor_tensor(dnc[:, b, :], dnp[:, b, j:j + SEQ],
                                                       parT[:, QC + 6 * j + b:QC + 6 * j + b + 1], dnc[:, b, :],
                                                       ALU.mult, ALU.add)
                            if b == 5 and j == 3:
                                mark(conv_ok, i)
                            else:
                                link(i)
                    dve.wait_ge(rope_ps, 1)
                    turn = ps[64:96, 4:7, :].rearrange("p b (c d) -> p (b c) d", c=2)[:, 0:5, :]
                    t5 = probs[64:96, 0:5, :]
                    link(V.tensor_tensor(t5, turn, trig[64:96, 1:2, :].broadcast_to([32, 5, SEQ]), ALU.mult))
                    link(V.tensor_tensor(qT[64:96, :, :], qT[64:96, :, :],
                                         trig[64:96, 0:1, :].broadcast_to([32, 5, SEQ]), ALU.mult))
                    link(V.tensor_tensor(qT[64:96, :, :], qT[64:96, :, :], t5, ALU.add))
                    mark(rope_ok, V.tensor_copy(kT[64:96, :, :], qT[64:96, 4:5, :].broadcast_to([32, 4, SEQ])))
                    norm_in(2, 2, xm)
                    maxima(0)
                    p_out(0)
                    dve.wait_ge(ex_ok, 1)
                    link(V.reciprocal(rinv[:, :], rsum[:, :]))
                    dve.wait_ge(o_ps, 1)
                    mark(bt_in, V.tensor_tensor(heads(ob[:, :, :]), ps[:, 2, :].rearrange("p (s c) -> p s c", c=64),
                                                rinv[:, :].unsqueeze(2).broadcast_to([P, 8, 64]), ALU.mult))
                    dve.wait_ge(small_in, 96)
                    v3, r3 = (spb[:, i, :].rearrange("p (t c) -> p t c", t=NT) for i in (0, 1))
                    dve.wait_ge(pre_ps, 1)
                    link(V.tensor_scalar(v3[:, :, 0:P], ps[:, 2, 0:SEQ].rearrange("p (t c) -> p t c", t=NT), -1.0, None,
                                         ALU.mult))
                    link(V.tensor_tensor(v3[:, :, P:P + 4], dab[:, :, 0:4], small[:, 0:1, :].broadcast_to([P, NT, 4]),
                                         ALU.add))
                    mark(spv, V.scalar_tensor_tensor(spb[:, 1, :], spb[:, 0, :], -1.0, spb[:, 0, :], ALU.mult, ALU.max))
                    sv = uv[:, :, W2:2 * W2]
                    link(V.tensor_reduce(mean[:, :], sv, AX_X, ALU.add))
                    link(V.tensor_scalar(mean[:, :], mean[:, :], 1.0 / W2, None, ALU.mult))
                    link(V.tensor_tensor(sv, sv, mean[:, :].unsqueeze(2).broadcast_to([P, NT, W2]), ALU.subtract))
                    link(V.tensor_tensor(tq[:, :, :], sv, sv, ALU.mult))
                    link(V.tensor_reduce(ssq[:, 3, 0:2], tq[:, :, :], AX_X, ALU.add))
                    mean_square(3, 2, W2)
                    for t in range(NT):
                        link(V.scalar_tensor_tensor(sv[:, t, :], sv[:, t, :], rstd[:, 3, t:t + 1], lnp[:, 0, :],
                                                    ALU.mult, ALU.mult))
                    mark(ln_ok, V.tensor_tensor(sv, sv, lnp[:, 1:2, :].broadcast_to([P, NT, W2]), ALU.add))
                    dve.wait_ge(spe, 1)
                    mark(spv, V.tensor_scalar(spb[:, 3, :], spb[:, 2, :], 1.0, None, ALU.add))
                    dve.wait_ge(spe, 2)
                    link(V.tensor_scalar(beta[:, :, :], beta[:, :, :], 1.0, None, ALU.add))
                    link(V.reciprocal(beta[:, :, :], beta[:, :, :]))
                    dve.wait_ge(spe, 4)
                    link(V.tensor_scalar(spb[:, 1, :], spb[:, 3, :], -1.0, None, ALU.add))
                    link(V.tensor_tensor(spb[:, 1, :], spb[:, 2, :], spb[:, 1, :], ALU.subtract))
                    link(V.reciprocal(spb[:, 3, :], spb[:, 3, :]))
                    link(V.tensor_tensor(spb[:, 1, :], spb[:, 1, :], spb[:, 3, :], ALU.mult))
                    link(V.tensor_tensor(spb[:, 1, :], spb[:, 1, :], spb[:, 4, :], ALU.add))
                    link(V.scalar_tensor_tensor(spb[:, 1, :], spb[:, 0, :], 0.0, spb[:, 1, :], ALU.max, ALU.add))
                    link(V.tensor_scalar(asc[:, :], asc[:, :], -1.0, None, ALU.mult))
                    link(V.tensor_tensor(lcat[:, :, P:P + 4], r3[:, :, P:P + 4],
                                         asc[:, :].unsqueeze(1).broadcast_to([P, NT, 4]), ALU.mult))
                    mark(lc_ok, V.tensor_scalar(lcat[:, :, 0:P], r3[:, :, 0:P], -1.0 / 16.0, None, ALU.mult))
                    dve.wait_ge(mix_ps, 1)
                    dve.wait_ge(bt_ps, 1)
                    for t in range(NT):
                        link(V.tensor_tensor(tq[:, t, :].rearrange("p (g c) -> p g c", c=64),
                                             ps[:, 3, t * W2:(t + 1) * W2].rearrange("p (g c) -> p g c", c=64),
                                             parT[:, QS:QS + 4].unsqueeze(2).broadcast_to([P, 4, 64]), ALU.add))
                    mark(bt_in, V.tensor_tensor(ob[:, :, :], tq[:, :, :], uv[:, :, 0:W2], ALU.mult))
                    dve.wait_ge(l2_ps, 1)
                    mark(l2_in, V.tensor_scalar(l2r, L[:, 0:4, :], EPS, None, ALU.add))
                    dve.wait_ge(cum_ps, 1)
                    link(V.tensor_copy(gcum[:, :], ps[:, 3, 0:SEQ]))
                    mark(cum_ok, V.tensor_copy(gam[:, :, :], ps[:, 2, 0:12].rearrange("p (t h) -> p t h", h=4)))
                    for n, b in enumerate((P,) + SUBL):
                        v = gcum[:, :].rearrange("p (n w) -> p n w", w=2 * b)
                        link(V.tensor_tensor(ed[:, n, :].rearrange("p (n w) -> p n w", w=2 * b), v,
                                             v[:, :, b - 1:b].broadcast_to([P, P // b, 2 * b]), ALU.subtract))
                    mark(df_ok, V.scalar_tensor_tensor(ed[:, :, :], ed[:, :, :], -1.0, ed[:, :, :], ALU.mult, ALU.max))
                    link(V.tensor_scalar(ngam[:, :, :], gam[:, 0:2, :], -1.0, None, ALU.mult))
                    link(V.tensor_copy(egam[:, 0:2, :], gam[:, 0:2, :]))
                    mark(eg_in, V.tensor_tensor(egam[:, 2, :], gam[:, 2, :], gam[:, 0, :], ALU.subtract))
                    dve.wait_ge(l2_rt, 1)
                    link(V.reciprocal(l2r, l2r))
                    link(V.scalar_tensor_tensor(dnc[:, 0:2, :], dnc[:, 0:2, :], 0.125, l2r[:, 0:2, :], ALU.mult, ALU.mult))
                    mark(l2_ok, V.tensor_tensor(dnc[:, 2:4, :], dnc[:, 2:4, :], l2r[:, 2:4, :], ALU.mult))
                    dve.wait_ge(le_ok, 1)
                    link(V.tensor_tensor(qe, ed, gqk[:, 0:1, :].broadcast_to([P, 8, SEQ]), ALU.mult))
                    mark(lev_ok, V.tensor_tensor(ke, ed, gqk[:, 1:2, :].broadcast_to([P, 8, SEQ]), ALU.mult))
                    link(V.memset(SaT[:, :, :, :], 0.0))
                    for r in range(4):
                        dve.wait_ge(sa_ps, r + 1)
                        for i in range(2):
                            n = 2 * r + i
                            m = lmask[:, n, :].bitcast(U32).unsqueeze(1).unsqueeze(1).broadcast_to([P, 4, NT, P])
                            ins = V.copy_predicated(SaT[:, :, :, :], m, ps[:, 4:8, i * SEQ:(i + 1) * SEQ].rearrange(
                                "p h (t i) -> p h t i", t=NT))
                            if i == 0:
                                link(ins)
                        mark(sa_ok, ins)
                    dve.wait_ge(sa_ps, 5)
                    mark(sa_ok, V.tensor_copy(S01[:, :, :], ps[:, 4:8, 0:P]))
                    dve.wait_ge(go_ps, 1)
                    dve.wait_ge(bt_ps, 2)
                    mark(gn_ok, V.tensor_copy(ob[:, :, :], ps[:, 2, :].rearrange("p (t c) -> p t c", t=NT)))
                    dve.wait_ge(sil_ok, 2)
                    head_norm(4, gog[:, :, :], 0)
                    dve.wait_ge(dec_ok, 1)
                    two = ps[:, 6:8, :].rearrange("p b (s i) -> p (b s) i", s=4)
                    mark(lt_ok, V.tensor_tensor(LT, decT, two, ALU.mult))
                    dve.wait_ge(tk_ps, 1)
                    dve.wait_ge(eg_ok, 1)
                    link(V.tensor_tensor(heads(rv), ps[:, 2, :].rearrange("p (s c) -> p s c", c=64),
                                         beta[:, :, :].rearrange("p t h -> p (t h)").unsqueeze(2)
                                         .broadcast_to([P, 8, 64]), ALU.mult))
                    mark(tk_ok, V.tensor_tensor(kd.rearrange("p (h c) -> p h c", c=64),
                                                ps[:, 3, 0:W2].rearrange("p (h c) -> p h c", c=64),
                                                egam[:, 2, :].unsqueeze(2).broadcast_to([P, 4, 64]), ALU.mult))
                    dve.wait_ge(kk_ps, 1)
                    link(V.tensor_tensor(LT, LT, ps[:, 4:6, :].rearrange("p b (s i) -> p (b s) i", s=4), ALU.mult))
                    mark(at_ok, V.tensor_tensor(attnT, decT, two, ALU.mult))
                    eye = ident.unsqueeze(1).broadcast_to([P, 8, P])
                    link(V.tensor_copy(X, eye))
                    link(V.tensor_copy(XT, eye))
                    for lv in range(7):
                        for p in range(2):
                            s = slice(4 * p, 4 * p + 4)
                            if lv:
                                dve.wait_ge(yy_ps, 2 * lv + p - 1)
                            mark(lm_ok, V.tensor_tensor(LTm[:, s, :], LT[:, s, :],
                                                        lmask[:, 6 - lv:7 - lv, :].broadcast_to([P, 4, P]), ALU.mult))
                        for p in range(2):
                            dve.wait_ge(zz_ps, 2 * lv + p + 1)
                            for i, m in enumerate((X, XT)):
                                v = m[:, 4 * p:4 * p + 4, :]
                                ins = V.tensor_tensor(v, v, ps[:, 4 + 2 * p + i, :].rearrange("p (s i) -> p s i", s=4),
                                                      ALU.subtract)
                                if i == 0:
                                    link(ins)
                            mark(xx_ok, ins)
                    dve.wait_ge(u_ps, 1)
                    mark(u_ok, V.tensor_copy(u[:, 0, :], ps[:, 2, 0:W2]))
                    dve.wait_ge(st_ps, 1)
                    mark(st_ok, V.tensor_copy(ssb, ps[:, 3, 0:P]))
                    dve.wait_ge(ks_ps, 1)
                    kS, qS = (ps[:, 4:6, i * P:(i + 1) * P].rearrange("p a (b c) -> p b a c", b=2) for i in range(2))

                    def by_head(v):
                        return v.rearrange("p (b a c) -> p b a c", b=2, a=2)

                    def per_head(v):
                        return v.rearrange("p (b a) -> p b a", b=2).unsqueeze(3).broadcast_to([P, 2, 2, 64])

                    link(V.tensor_tensor(rinv[:, 0:4], beta[:, 1, :], egam[:, 1, :], ALU.mult))
                    link(V.tensor_tensor(by_head(tq[:, 0, :]), kS, per_head(rinv[:, 0:4]), ALU.mult))
                    mark(r1_ok, V.tensor_tensor(rv[:, 1, :], rv[:, 1, :], tq[:, 0, :], ALU.subtract))
                    link(V.tensor_tensor(by_head(tq[:, 1, :]), qS, per_head(egam[:, 1, :]), ALU.mult))
                    dve.wait_ge(u_ps, 2)
                    mark(u_ok, V.tensor_copy(u[:, 1, :], ps[:, 2, W2:2 * W2]))
                    dve.wait_ge(do_ps, 1)
                    dve.wait_ge(bt_ps, 3)
                    link(V.tensor_copy(ob[:, 0, :], ps[:, 3, 0:W2]))
                    link(V.tensor_tensor(ob[:, 1, :], ps[:, 3, W2:2 * W2], tq[:, 1, :], ALU.add))
                    head_norm(5, dz[:, :, :], 1)
                    for n in range(4):
                        dve.wait_ge(sig_ok, n + 1)
                        for m in range(4):
                            i = 4 * n + m
                            dve.wait_ge(pr_ps, i + 1)
                            src = ps[:, 4 + i % 4, :].rearrange("p (b c) -> p b c", b=2)
                            gt = gates[:, 8 * n + 2 * m:8 * n + 2 * m + 2, :]
                            out, tmp = (z[:, 2 * m:2 * m + 2, :] for z in (merged, hT))
                            if n == 0:
                                mark(pr_free, V.tensor_tensor(out, src, gt, ALU.mult))
                                continue
                            mark(pr_free, V.tensor_tensor(tmp, src, gt, ALU.mult))
                            mark(mg_ok, V.tensor_tensor(out, out, tmp, ALU.add))

                    def residual(n):
                        for i in range(4):
                            dve.wait_ge(res_ps, 4 * n + i + 1)
                            c, t = (i % 2, i // 2) if n == 2 else (i // 2, i % 2)
                            xs = x[:, t, c * 512:(c + 1) * 512]
                            mark(res_ok, V.tensor_tensor(xs, xs, ps[:, 4 + 2 * c + t, :], ALU.add))

                    residual(0)
                    norm_in(6, 3, x)
                    maxima(1)
                    dve.wait_ge(ex_ok, 2)
                    link(V.reciprocal(rinv[:, :], rsum[:, :]))
                    mark(pn_ok, V.tensor_tensor(probs[:, :, :], probs[:, :, :],
                                                rinv[:, :].unsqueeze(2).broadcast_to([P, 8, SEQ]), ALU.mult))
                    p_out(1)
                    residual(1)

                    def split(h):
                        dve.wait_ge(hi_ok, h + 1)
                        if h >= N_UP:
                            i = h - N_UP
                            V.tensor_tensor(hidden_of(hlo, i), hid[:, 2 * i:2 * i + 2, :],
                                            hidden_of(hhi, i).bitcast(F32), ALU.subtract)
                        mark(lo_ok, V.tensor_tensor(half_of(wlo, h), half_source(h), half_of(whi, h).bitcast(F32),
                                                    ALU.subtract))

                    split(0)
                    norm_in(7, 4, x)
                    split(1)
                    for k in range(KD):
                        dve.wait_ge(free, U_X7 + k // 2 + 1)
                        i = V.scalar_tensor_tensor(nlo[:, k, :], ps[:, (U_X7 + k // 2) % 2,
                                                                    (k % 2) * SEQ:(k % 2 + 1) * SEQ],
                                                   parT[:, QL + k:QL + k + 1], nhi[:, k, :].bitcast(F32),
                                                   ALU.mult, ALU.subtract)
                        if k % 2:
                            mark(nlo_ok, i)
                    for h in range(2, HALVES):
                        split(h)
                    for i in range(N_UP):
                        dve.wait_ge(free, U_UP + i + 1)
                        h2 = hid[:, 2 * i:2 * i + 2, :]
                        mark(hs_ok, V.tensor_tensor(h2, h2, h2, ALU.mult))
                        split(i + HALVES)
                    for h in range(N_UP + HALVES, N_HALF):
                        split(h)
                    residual(2)

                @block.gpsimd
                def _(pool):
                    def rsqrt(e, n):
                        pool.wait_ge(msq_ok, e + 1)
                        nc.gpsimd.tensor_tensor(rstd[:, e, 0:n], msq[:, e, 0:n], nhalf[:, 0:n], ALU.pow
                                                ).then_inc(rstd_ok, 1)

                    rsqrt(0, 2)
                    rsqrt(1, 4)
                    rsqrt(2, 2)
                    rsqrt(3, 2)
                    rsqrt(4, 8)
                    rsqrt(5, 8)
                    rsqrt(6, 2)
                    rsqrt(7, 2)

            clear()

        with nc.Block() as block:

            @block.sync
            def _(sp_):
                sp_.dma_start(xm[:, 0, :], a["norm_final_2"].partition_broadcast(P)).then_inc(fin_in, 16)

            @block.scalar
            def _(act):
                for t in range(NT):
                    nc.scalar.activation(flat(pT[:, 4 * t:4 * t + 4, :]), x[:, t, :], ACT.Square,
                                         accum_out=ssq[:, 0, t:t + 1]).then_inc(ssq_ok, 1)

            @block.vector
            def _(dve):
                dve.wait_ge(ssq_ok, 2)
                nc.vector.tensor_scalar(msq[:, 0, 0:2], ssq[:, 0, 0:2], 1.0 / D, EPS, ALU.mult, ALU.add
                                        ).then_inc(msq_ok, 1)
                dve.wait_ge(rstd_ok, 1)
                dve.wait_ge(fin_in, 16)
                for t in range(NT):
                    nc.vector.scalar_tensor_tensor(x[:, t, :], x[:, t, :], rstd[:, 0, t:t + 1], xm[:, 0, :],
                                                   ALU.mult, ALU.mult).then_inc(y_ok, 1)
                dve.wait_ge(y_ok, 2)

            @block.gpsimd
            def _(pool):
                pool.wait_ge(msq_ok, 1)
                nc.gpsimd.tensor_tensor(rstd[:, 0, 0:2], msq[:, 0, 0:2], nhalf[:, 0:2], ALU.pow).then_inc(rstd_ok, 1)

def build(nc, a, y):
    with ExitStack() as ctx:
        ps = ctx.enter_context(nc.psum_tensor("ps", [P, 8, 512], F32))
        x = ctx.enter_context(nc.sbuf_tensor("x", [P, NT, D], F32))
        con = ctx.enter_context(nc.sbuf_tensor("con", [P, N_CONST], F32))
        bfc = ctx.enter_context(nc.sbuf_tensor("bfc", [P, 3, P], BF16))
        con_in, con_bf = (ctx.enter_context(nc.semaphore(n)) for n in ("con_in", "con_bf"))
        out_done = ctx.enter_context(nc.semaphore("out_done"))
        with nc.Block() as block:

            @block.sync
            def _(sp):
                sp.dma_start(con[:, :], a["constants"]).then_inc(con_in, 16)
                sp.dma_start(x[:, :, :], a["x"].rearrange("a (t p) d -> p (a t) d", p=P)).then_inc(con_in, 16)
                sp.wait_ge(con_in, 32)

            @block.vector
            def _(dve):
                dve.wait_ge(con_in, 32)
                for i, c in enumerate((C_ID, C_MT, C_MQ)):
                    nc.vector.tensor_copy(bfc[:, i, :], con[:, c:c + P]).then_inc(con_bf, 1)
                dve.wait_ge(con_bf, 3)

        first_block(nc, ps, x, con, bfc, a)
        second_block(nc, ps, x, con, bfc, a)

        with nc.Block() as block:

            @block.sync
            def _(sp):
                sp.dma_start(y.rearrange("a (t p) d -> p (a t) d", p=P), x[:, :, :]).then_inc(out_done, 16)
                sp.wait_ge(out_done, 16)


_INS = [
    "x", "norm_mix_pre", "w_in", "conv_w", "conv_b", "dt_bias", "a_log", "d_skip", "ssm_norm",
    "fox_fbias", "w_gate", "b_gate", "w_branch", "w_out", "norm_mix_post", "norm_ffn_pre", "w_ffn_in",
    "w_ffn_out", "norm_ffn_post", "mem_2", "positions_2", "norm_mix_2", "w_in_2", "mla_norm_q_2",
    "mla_norm_kv_2", "mla_w_uq_2", "mla_w_ukv_2", "sg_ln_g_2", "sg_ln_b_2", "sg_w_2", "sg_b_2",
    "gla_w_gate_2", "gla_b_gate_2", "gla_norm_2", "dn_conv_2", "dn_a_log_2", "dn_dt_bias_2",
    "dn_norm_2", "w_branch_2", "w_out_2", "norm_xattn_2", "norm_mem_2", "xattn_wq_2", "xattn_wk_2",
    "xattn_wv_2", "xattn_wo_2", "norm_mlp_2", "w_up_2", "w_down_2", "norm_final_2",
]


def kernel(**inputs):
    import concourse.bacc as bacc
    from concourse.bass_utils import run_bass_kernel_spmd

    nc = bacc.Bacc("TRN2", target_bir_lowering=False, num_devices=1)
    arrays, args = {}, {}
    for name, value in [(n, inputs[n]) for n in _INS] + [
            ("constants", shape_constants()), ("constants_1", shape_constants_1()),
            ("constants_2", shape_constants_2())]:
        value = np.ascontiguousarray(value)
        arrays["in_" + name] = value
        args[name] = nc.dram_tensor("in_" + name, value.shape, mybir.dt.from_np(value.dtype),
                                    kind="ExternalInput").ap()
    y = nc.dram_tensor("out_0", (1, SEQ, D), F32, kind="ExternalOutput").ap()
    build(nc, args, y)
    result = run_bass_kernel_spmd(nc, [arrays], core_ids=[0])
    return result.results[0]["out_0"]
```
